# Optimizing a Trainium2 kernel written in Bass

```python
import jax, jax.numpy as jnp
from jax import lax
import numpy as np

D_MODEL = 1024
BATCH = 1
SEQ = 256
DEPTH = 2

GRID_W = 64
CTX_LEN = 256
D_MIX = D_MODEL
POOL_WIDTH = D_MIX // 2
POOL_WINDOWS = (2, 4, 8, 16)
POOL_GROUP = POOL_WIDTH // len(POOL_WINDOWS)
GLA_WIDTH = D_MIX - POOL_WIDTH
GLA_HEADS = 4
GLA_DV = GLA_WIDTH // GLA_HEADS
GLA_DK = GLA_DV // 2
GLA_KW = GLA_HEADS * GLA_DK
GATE_RANK = 16
GATE_TAU = 16.0
GLA_CHUNK = 64
D_FF = 2816
N_MOD = 9
DN_ALPHA = (2.0 * DEPTH) ** 0.25
DN_BETA = (8.0 * DEPTH) ** -0.25
LN_EPS = 1e-6
IN_SPLITS = (POOL_WIDTH, GLA_KW, GLA_KW, GLA_WIDTH, GLA_WIDTH, GATE_RANK, GATE_RANK)
IN_COLS = sum(IN_SPLITS)

kernel_name = "hybrid_pool_gla_dit_trunk"

def _layernorm(x):
    x32 = x.astype(jnp.float32)
    mu = jnp.mean(x32, axis=-1, keepdims=True)
    var = jnp.mean(jnp.square(x32 - mu), axis=-1, keepdims=True)
    return ((x32 - mu) * lax.rsqrt(var + LN_EPS)).astype(x.dtype)

def _post_norm(x, y, g, b):
    z = (DN_ALPHA * x + y).astype(jnp.float32)
    mu = jnp.mean(z, axis=-1, keepdims=True)
    var = jnp.mean(jnp.square(z - mu), axis=-1, keepdims=True)
    return ((z - mu) * lax.rsqrt(var + LN_EPS) * g + b).astype(x.dtype)

def _modulate(h, shift, scale):
    return h * (1.0 + scale) + shift

def _ada(cond, w, b):
    m = jax.nn.silu(cond) @ w + b
    m = m.reshape(m.shape[:-1] + (N_MOD, D_MODEL))
    m = jnp.moveaxis(m, -2, 0)
    return m[..., None, :]

def _swiglu(h, w_in, w_out):
    g, u = jnp.split(h @ w_in, 2, axis=-1)
    return (jax.nn.silu(g) * u) @ w_out

def _pos_embed_2d(L, dtype):
    rows = L // GRID_W
    f32 = jnp.float32
    r = jnp.repeat(jnp.arange(rows, dtype=f32), GRID_W)
    col = jnp.tile(jnp.arange(GRID_W, dtype=f32), rows)
    quarter = D_MODEL // 4
    omega = 1.0 / (10000.0 ** (jnp.arange(quarter, dtype=f32) / quarter))

    def enc(p):
        a = p[:, None] * omega
        return jnp.concatenate([jnp.sin(a), jnp.cos(a)], axis=-1)

    return jnp.concatenate([enc(r), enc(col)], axis=-1).astype(dtype)

def _pool_mixer(u, pool_w, pool_scale):
    B, L, _ = u.shape
    u32 = u.astype(jnp.float32)
    cs = jnp.concatenate([jnp.zeros((B, 1, POOL_WIDTH), jnp.float32),
                          jnp.cumsum(u32, axis=1)], axis=1)
    t = jnp.arange(L)
    pooled = []
    for g, w in enumerate(POOL_WINDOWS):
        lo = jnp.maximum(t - w // 2, 0)
        hi = jnp.minimum(t + (w - 1 - w // 2), L - 1)
        csg = cs[:, :, g * POOL_GROUP:(g + 1) * POOL_GROUP]
        s = jnp.take(csg, hi + 1, axis=1) - jnp.take(csg, lo, axis=1)
        pooled.append(s / (hi - lo + 1).astype(jnp.float32)[None, :, None])
    pooled = jnp.stack(pooled, axis=2) - u32.reshape(B, L, len(POOL_WINDOWS), POOL_GROUP)
    y = jnp.einsum('blgc,gcd->blgd', pooled, pool_w.astype(jnp.float32))
    return (y.reshape(B, L, POOL_WIDTH) * pool_scale).astype(u.dtype)

def _project(h, w_in, gate_up_f, gate_bias_f, gate_up_b, gate_bias_b):
    B, L, _ = h.shape
    offs = tuple(int(o) for o in np.cumsum(IN_SPLITS)[:-1])
    u, q, k, v, r, gdf, gdb = jnp.split(h @ w_in, offs, axis=-1)

    def heads(t, d):
        return t.reshape(B, L, GLA_HEADS, d).transpose(0, 2, 1, 3)

    la_f = jax.nn.log_sigmoid((gdf @ gate_up_f + gate_bias_f).astype(jnp.float32)) / GATE_TAU
    la_b = jax.nn.log_sigmoid((gdb @ gate_up_b + gate_bias_b).astype(jnp.float32)) / GATE_TAU
    q = heads(q, GLA_DK) * (GLA_DK ** -0.5)
    return (u, q, heads(k, GLA_DK), heads(v, GLA_DV), r,
            heads(la_f, GLA_DK), heads(la_b, GLA_DK))

def _chunks(t):
    B, H, L, d = t.shape
    return t.reshape(B, H, L // GLA_CHUNK, GLA_CHUNK, d)

def _chunk_state_scan(kc, vc, b, S0):
    b_last = b[..., -1:, :]
    k_end = kc * jnp.exp(b_last - b)
    U = jnp.einsum('bhncd,bhnce->nbhde', k_end, vc)
    decay = jnp.moveaxis(jnp.exp(b_last[..., 0, :]), 2, 0)

    def step(S, inp):
        U_n, d_n = inp
        return d_n[..., None] * S + U_n, S

    S_fin, S_starts = lax.scan(step, S0, (U, decay))
    return S_starts, S_fin

def _gla_direction(q, k, v, log_a, S0):
    B, H, L, _ = v.shape
    f32 = jnp.float32
    qc, kc, vc = (_chunks(t.astype(f32)) for t in (q, k, v))
    b = jnp.cumsum(_chunks(log_a), axis=-2)
    S_starts, S_fin = _chunk_state_scan(kc, vc, b, S0)
    q_in = qc * jnp.exp(b)
    k_in = kc * jnp.exp(-b)
    lower = jnp.tril(jnp.ones((GLA_CHUNK, GLA_CHUNK), dtype=bool))
    scores = jnp.where(lower, jnp.einsum('bhnid,bhnjd->bhnij', q_in, k_in), 0.0)
    o = (jnp.einsum('bhnij,bhnje->bhnie', scores, vc)
         + jnp.einsum('bhnid,nbhde->bhnie', q_in, S_starts))
    return o.reshape(B, H, L, GLA_DV), S_fin

def _gla_final_state(k, v, log_a, S0):
    kc, vc = (_chunks(t.astype(jnp.float32)) for t in (k, v))
    b = jnp.cumsum(_chunks(log_a), axis=-2)
    _, S_fin = _chunk_state_scan(kc, vc, b, S0)
    return S_fin

def _gla_output(o, r, norm_g):
    B, H, L, dv = o.shape
    o = o.transpose(0, 2, 1, 3)
    o = o * lax.rsqrt(jnp.mean(jnp.square(o), axis=-1, keepdims=True) + LN_EPS)
    o = o.reshape(B, L, H * dv) * norm_g
    return (o * jax.nn.silu(r.astype(jnp.float32))).astype(r.dtype)

def _flip(t):
    return jnp.flip(t, axis=2)

def _mixer(h, hc, w_in, pool_w, pool_scale, gate_up_f, gate_bias_f, gate_up_b, gate_bias_b,
           norm_g, w_out, ctx_out):
    B = h.shape[0]
    gates = (gate_up_f, gate_bias_f, gate_up_b, gate_bias_b)
    u, q, k, v, r, la_f, la_b = _project(h, w_in, *gates)
    uc, qc, kc, vc, rc, lac_f, lac_b = _project(hc, w_in, *gates)
    S0 = jnp.zeros((B, GLA_HEADS, GLA_DK, GLA_DV), jnp.float32)
    yc = None
    if ctx_out:
        oc_f, S_f = _gla_direction(qc, kc, vc, lac_f, S0)
        oc_b, S_b = _gla_direction(_flip(qc), _flip(kc), _flip(vc), _flip(lac_b), S0)
        yc = jnp.concatenate([_pool_mixer(uc, pool_w, pool_scale),
                              _gla_output(oc_f + _flip(oc_b), rc, norm_g)], axis=-1) @ w_out
    else:
        S_f = _gla_final_state(kc, vc, lac_f, S0)
        S_b = _gla_final_state(_flip(kc), _flip(vc), _flip(lac_b), S0)
    o_f, _ = _gla_direction(q, k, v, la_f, S_f)
    o_b, _ = _gla_direction(_flip(q), _flip(k), _flip(v), _flip(la_b), S_b)
    y = jnp.concatenate([_pool_mixer(u, pool_w, pool_scale),
                         _gla_output(o_f + _flip(o_b), r, norm_g)], axis=-1) @ w_out
    return y, yc

def setup_inputs(seed: int = 0) -> dict:
    key = jax.random.key(seed)
    ks = jax.random.split(key, 24)
    f32 = jnp.float32

    def nrm(k, shape, s):
        return jax.random.normal(k, shape, f32) * s

    D = D_MODEL
    return {
        'x': nrm(ks[0], (BATCH, SEQ, D), 1.0),
        'c': nrm(ks[1], (BATCH, D), 1.0),
        'ctx': nrm(ks[2], (BATCH, CTX_LEN, D), 1.0),
        'c_ctx': nrm(ks[3], (D,), 1.0),
        'w_ada': nrm(ks[4], (DEPTH, D, N_MOD * D), 0.5 * D ** -0.5),
        'b_ada': nrm(ks[5], (DEPTH, N_MOD * D), 0.02),
        'ln_g': 1.0 + nrm(ks[6], (DEPTH, 3, D), 0.05),
        'ln_b': nrm(ks[7], (DEPTH, 3, D), 0.02),
        'ffa_w_in': nrm(ks[8], (DEPTH, D, 2 * D_FF), D ** -0.5),
        'ffa_w_out': nrm(ks[9], (DEPTH, D_FF, D), D_FF ** -0.5 * DN_BETA),
        'mix_w_in': nrm(ks[10], (DEPTH, D, IN_COLS), D ** -0.5),
        'pool_w': nrm(ks[11], (DEPTH, len(POOL_WINDOWS), POOL_GROUP, POOL_GROUP), POOL_GROUP ** -0.5),
        'pool_scale': 1.0 + nrm(ks[12], (DEPTH, POOL_WIDTH), 0.1),
        'gate_up_f': nrm(ks[13], (DEPTH, GATE_RANK, GLA_KW), GATE_RANK ** -0.5),
        'gate_bias_f': jax.random.uniform(ks[14], (DEPTH, GLA_KW), f32, 0.5, 3.0),
        'gate_up_b': nrm(ks[15], (DEPTH, GATE_RANK, GLA_KW), GATE_RANK ** -0.5),
        'gate_bias_b': jax.random.uniform(ks[16], (DEPTH, GLA_KW), f32, 0.5, 3.0),
        'gla_norm_g': 1.0 + nrm(ks[17], (DEPTH, GLA_WIDTH), 0.05),
        'mix_w_out': nrm(ks[18], (DEPTH, D_MIX, D), D_MIX ** -0.5 * DN_BETA),
        'ffb_w_in': nrm(ks[19], (DEPTH, D, 2 * D_FF), D ** -0.5),
        'ffb_w_out': nrm(ks[20], (DEPTH, D_FF, D), D_FF ** -0.5 * DN_BETA),
    }

def reference(x, c, ctx, c_ctx, w_ada, b_ada, ln_g, ln_b, ffa_w_in, ffa_w_out, mix_w_in,
              pool_w, pool_scale, gate_up_f, gate_bias_f, gate_up_b, gate_bias_b,
              gla_norm_g, mix_w_out, ffb_w_in, ffb_w_out):
    L = x.shape[1]
    h = _layernorm(x + _pos_embed_2d(L, x.dtype))
    hc = _layernorm(ctx)
    for l in range(DEPTH):
        last = l == DEPTH - 1
        mx = _ada(c, w_ada[l], b_ada[l])
        mc = _ada(c_ctx, w_ada[l], b_ada[l])
        h = _post_norm(h, 0.5 * mx[2] * _swiglu(_modulate(h, mx[0], mx[1]), ffa_w_in[l], ffa_w_out[l]),
                       ln_g[l, 0], ln_b[l, 0])
        hc = _post_norm(hc, 0.5 * mc[2] * _swiglu(_modulate(hc, mc[0], mc[1]), ffa_w_in[l], ffa_w_out[l]),
                        ln_g[l, 0], ln_b[l, 0])
        y, yc = _mixer(_modulate(h, mx[3], mx[4]), _modulate(hc, mc[3], mc[4]), mix_w_in[l],
                       pool_w[l], pool_scale[l], gate_up_f[l], gate_bias_f[l], gate_up_b[l],
                       gate_bias_b[l], gla_norm_g[l], mix_w_out[l], not last)
        h = _post_norm(h, mx[5] * y, ln_g[l, 1], ln_b[l, 1])
        h = _post_norm(h, 0.5 * mx[8] * _swiglu(_modulate(h, mx[6], mx[7]), ffb_w_in[l], ffb_w_out[l]),
                       ln_g[l, 2], ln_b[l, 2])
        if not last:
            hc = _post_norm(hc, mc[5] * yc, ln_g[l, 1], ln_b[l, 1])
            hc = _post_norm(hc, 0.5 * mc[8] * _swiglu(_modulate(hc, mc[6], mc[7]), ffb_w_in[l], ffb_w_out[l]),
                            ln_g[l, 2], ln_b[l, 2])
    return h


_drawn_inputs = setup_inputs


def setup_inputs(seed=0):
    import zlib

    import numpy as np

    out = dict(_drawn_inputs(seed))
    spreads = {}
    factors = {'ctx': 2.801,
     'b_ada': 4.882,
     'pool_scale': 6.356,
     'gate_up_f': 3.463,
     'gate_bias_f': 2.826,
     'gate_up_b': 3.878,
     'gate_bias_b': 2.702,
     'gla_norm_g': 8.0}
    for name, (base, spread) in spreads.items():
        noise = np.random.default_rng([zlib.crc32(name.encode()), seed]).standard_normal(out[name].shape)
        drawn = base * np.exp(spread * noise) if base else spread * noise
        out[name] = __import__('jax').numpy.asarray(drawn.astype(out[name].dtype))
    for name, factor in factors.items():
        out[name] = (out[name] * factor).astype(out[name].dtype)
    return out
```

```python
from contextlib import ExitStack

import concourse.bass as bass
from concourse import mybir

F32 = mybir.dt.float32
F32R = mybir.dt.float32r
U8 = mybir.dt.uint8
ALU = mybir.AluOpType
ACT = mybir.ActivationFunctionType
ds = bass.ds

P = 128
DEPTH = 2
D = 1024
KT = D // P
LAT = 256
TOK = 512
FF = 2816
FT = FF // P
CHUNK = 64
N_MOD = 9
FULLS = DEPTH * N_MOD * KT // 2
HALVES = 2 * FULLS
WB = KT * 2 * P
START_BLOCKS = 2 * KT // 2
START_SLOTS = 5
EPS = 1e-6
ALPHA = (2.0 * DEPTH) ** 0.25
KPARTS = [(0, 8), (8, 16), (16, FT)]
WINDOWS = (2, 4, 8, 16)
PAD = 8
UPW = LAT + 2 * PAD
IN_BLOCKS = 9
N_CH = TOK // CHUNK
CHUNK_ORDER = ((4, 5, 6, 7, 0, 1, 2, 3), (7, 6, 5, 4, 3, 2, 1, 0))


class Stage:

    def __init__(self, run, totals, sems, scratch=None, w=0, shift=0, scale=0, last=False):
        self.run, self.totals, self.sems = run, totals, sems
        self.q, self.scratch, self.w, self.shift, self.scale, self.last = run, scratch, w, shift, scale, last

    def sig(self, name):
        return self.sems[name]

    def at(self, name, value):
        return self.sems[name], self.run * self.totals[name] + value


class Phase:

    def __init__(self, f, l, n, a, lins):
        self.f, self.l = f, l
        self.n, self.a = n, a
        self.lin, self.ln = lins
        self.w = LAT if l == DEPTH - 1 and f == "b" else TOK
        self.gate = l * N_MOD + {"a": 2, "mix": 5, "b": 8}[f]
        self.gate_scale = 1.0 if f == "mix" else 0.5


def build(nc, io):
    with ExitStack() as ctx:
        arena = ctx.enter_context(nc.sbuf_tensor("arena", [P, 212800 // 4], F32))
        base = 16512
        at = [base]

        def sb(name, shape, dt, offset=None):
            size = 4
            for s in shape[1:]:
                size *= s
            if dt == U8:
                size //= 4
            size = -(-size // 32) * 32
            if offset is None:
                offset = at[0]
                at[0] += size
                assert at[0] <= 229344, at[0]
            return nc.alloc_sbuf_tensor_at(name, shape, dt, offset=offset)

        def sem(name):
            return ctx.enter_context(nc.semaphore(name))

        H = sb("H", [P, KT, TOK], F32)
        x_off = at[0]
        XH = sb("XH", [P, KT, TOK], F32R)
        XL = sb("XL", [P, KT, TOK], F32R)
        a_off = at[0]
        AH = sb("AH", [P, FT, TOK], F32R)
        AL = sb("AL", [P, FT, TOK], F32R)
        a_end = at[0]
        RAW = [sb(f"RAW{i}", [P, WB], F32) for i in range(2)]
        WH = [sb(f"WH{i}", [P, WB], F32R) for i in range(2)]
        WL = [sb(f"WL{i}", [P, WB], F32R) for i in range(2)]
        SRAW = sb("SRAW", [P, D], F32)
        SWH = sb("SWH", [P, D], F32R)
        SWL = sb("SWL", [P, D], F32R)
        SG = sb("SG", [P, TOK], F32)
        AF = sb("AF", [P, TOK], F32)
        MODS = sb("MODS", [P, 2 * FULLS, 2], F32)
        BADA = sb("BADA", [P, 2 * FULLS], F32)
        LNG = sb("LNG", [P, 1 + 3 * DEPTH, KT], F32)
        LNB = sb("LNB", [P, 1 + 3 * DEPTH, KT], F32)
        CA = sb("CA", [P, KT, 2], F32)
        CB = sb("CB", [P, KT, 2], F32)
        CHA = sb("CHA", [P, KT, 2], F32)
        CHB = sb("CHB", [P, KT, 2], F32)
        CG = sb("CG", [P, KT, 2], F32)
        COND = sb("COND", [P, KT, 2], F32)
        CSIL = sb("CSIL", [P, KT, 2], F32)
        S4 = sb("S4", [P, KT * 4 + P], F32R)
        ROWS = sb("ROWS", [4, 2 * P], F32)
        FOLD = sb("FOLD", [4, 2], F32)
        TRI = sb("TRI", [P, 4, P], F32)
        IDENT = sb("IDENT", [P, P], F32)
        ONES = sb("ONES", [P, P], F32)
        MASK = sb("MASK", [P, 2, P], U8)
        COLS = sb("COLS", [P, DEPTH, 2, 4], F32)
        EPSC = sb("EPSC", [P, 8], F32)

        off = [a_off]

        def over(name, shape, dt=F32, offset=None):
            size = 4
            for s in shape[1:]:
                size *= s
            if offset is None:
                offset = off[0]
                off[0] += -(-size // 32) * 32
                assert off[0] <= a_end, (name, off[0] - a_end)
            return sb(name, shape, dt, offset)

        up_off = off[0]
        UP = over("UP", [P, 4, 2, UPW])
        AT = over("AT", [P, 4, TOK], offset=up_off)
        PB = over("PB", [P, 2, UPW])
        PC = over("PC", [P, 2, UPW])
        CINV = over("CINV", [P, 4, LAT])
        PW = over("PW", [P, 4, P])
        GU = over("GU", [33, TOK])
        GD = over("GD", [33, TOK])
        kq_off = off[0]
        KTT = over("KTT", [P, 2, TOK])
        QTT = over("QTT", [P, 2, TOK])
        RT = over("RT", [P, 4, TOK], offset=kq_off)
        KN = over("KN", [P, 4, 256])
        vn_off = off[0]
        VN = over("VN", [P, 4, TOK])
        la_off = off[0]
        LA = over("LA", [P, 4, TOK])
        KE = over("KE", [P, 4, TOK], offset=la_off)
        SQH = over("SQH", [P, 4, TOK], offset=la_off)
        QF = [over(f"QF{d}", [P, 2, TOK]) for d in range(2)]
        KF = [over(f"KF{d}", [P, 2, TOK]) for d in range(2)]
        et_off = off[0]
        ET = [over(f"ET{i}", [P, TOK]) for i in range(2)]
        TFB = [over(f"TFB{i}", [P, TOK], offset=et_off + 2048 * i) for i in range(2)]
        SS = [over(f"SS{d}", [P, 7, 2, P]) for d in range(2)]
        DEC = over("DEC", [P, 2, 2, N_CH])
        ln_sq, ln_acc = {}, {}
        for kind, o in (("x", x_off + KT * TOK * 4), ("a", vn_off)):
            ln_sq[kind] = [over(f"LSQ{kind}{i}", [P, TOK], offset=o + 2048 * i) for i in range(2)]
            ln_acc[kind] = [over(f"LAC{kind}{i}", [P, TOK], offset=o + 4096 + 2048 * i) for i in range(2)]
        MU = over("MU", [P, TOK], offset=a_off)
        RS = over("RS", [P, TOK], offset=a_off + 2048)
        M = [over(f"M{i}", [P, 2, TOK], offset=a_off + 4096 + 4096 * i) for i in range(2)]
        START = [over(f"START{i}", [P, WB], offset=vn_off + 8192 + 4 * WB * i) for i in range(START_SLOTS)]
        assert vn_off + 8192 + 4 * WB * START_SLOTS <= a_end
        POSR = over("POSR", [P, 4, 4], offset=a_off + 16384)
        POSC = over("POSC", [P, 4, 64], offset=a_off + 16384 + 64)

        BANK = [ctx.enter_context(nc.psum_tensor(f"bank{i}", [P, TOK], F32)) for i in range(8)]
        PAIR = [BANK[0:2], BANK[2:4]]
        B_ROWS, B_COLS, B_SC = BANK[4], BANK[5], BANK[6:8]

        ln_totals = dict(half=4, z=12, sq=8, added=8, stats=2, mu=1, var=1, ln=1, std=1, zc=3, zn=4, mfull=4,
                         xh=4, xl=4, h=1)
        ffn_totals = dict(sg=FT, af=FT, ah=FT)
        mix_totals = dict(aux_in=48, pads=1, gd=1, up=2, u12=1, kv=2, v_in=2, rt=4, gp=4, et=16, et_used=16,
                          knp=2, kn=2, bp=4, enp=4, u=14, state=14, pooled=4, pm=4, ym=4, xh=8, xl=8,
                          sc=8, cp=8, at=4, o=4, osq=4, ms=4, ln=4, std=4, yg=4, yh=4)
        stage_sems = [{s: sem(f"{k}_{s}") for s in t}
                      for k, t in (("ln", ln_totals), ("ffn", ffn_totals), ("mix", mix_totals))]

        def stage(kind, run, **more):
            sems, totals = stage_sems[kind], (ln_totals, ffn_totals, mix_totals)[kind]
            return Stage(run, totals, sems, **more)

        cond_in = sem("cond_in")
        consts_in = sem("consts_in")
        x_in = sem("x_in")
        raw_full = [sem(f"raw_full{i}") for i in range(2)]
        hi_done = sem("hi_done")
        lo_done = sem("lo_done")
        block_done = sem("block_done")
        pair_free = [sem(f"pair_free{i}") for i in range(2)]
        side_full = sem("side_full")
        side_hi = sem("side_hi")
        side_lo = sem("side_lo")
        side_done = sem("side_done")
        start_full = [sem(f"start_full{i}") for i in range(START_SLOTS)]
        rows_ready = sem("rows_ready")
        rows_out = sem("rows_out")
        cols_ready = sem("cols_ready")
        mods_done = sem("mods_done")
        sil_ready = sem("sil_ready")
        s4_hi = sem("s4_hi")
        s4_ready = sem("s4_ready")
        s4_tail = sem("s4_tail")
        eps_set = sem("eps_set")
        mask_ready = sem("mask_ready")
        dve_chain = sem("dve_chain")
        act_chain = sem("act_chain")
        out_done = sem("out_done")

        def new_ln(scratch, q, width, shift, scale, last=False):
            return stage(0, q, scratch=scratch, w=width, shift=shift, scale=scale, last=last)

        n, a, f_index = 0, 0, 0
        lns = [new_ln("a", 0, TOK, 0, 1)]
        phases = []
        for l in range(DEPTH):
            last = l == DEPTH - 1
            for f in ("a", "mix", "b"):
                m = l * N_MOD
                shift = m + {"a": 3, "mix": 6, "b": 9}[f]
                q = 1 + 3 * l + ("a", "mix", "b").index(f)
                p = Phase(f, l, n, a, lins=(lns[-1], new_ln("a" if f == "mix" else "x", q,
                                                            LAT if last and f != "a" else TOK,
                                                            shift, shift + 1, last and f == "b")))
                lns.append(p.ln)
                if f == "mix":
                    p.sides = [2] * (6 if last else 7) + [0] * (3 if last else 2)
                    p.nt = 2 if last else 4
                    p.s = stage(2, l)
                    n, a = n + IN_BLOCKS + 4, a + sum(p.sides)
                else:
                    p.G = FT * f_index
                    p.loops = [(0, 1, 1), (1, 4, 1), (4, 11, 0)] if last and f == "b" else [(0, 1, 1), (1, 11, 1)]
                    p.out_sides = 6 if f == "a" else 0 if last else 2
                    p.a_out = a + 2 * sum((e - b) * s for b, e, s in p.loops)
                    p.s = stage(1, f_index)
                    f_index += 1
                    n, a = n + FT + 12, p.a_out + 2 * p.out_sides
                phases.append(p)
        H0 = 2 * START_BLOCKS
        F0 = START_BLOCKS
        assert a == HALVES - H0
        N_BLOCKS = n

        def run_turns(engine, first, end, turn_of):
            if end - first == 1:
                turn_of(first)
            else:
                with engine.Fori(first, end) as i:
                    turn_of(i)

        def mods_ready(engine, m):
            engine.wait_ge(mods_done, (m + 1) * KT // 2)

        def mod(m):
            return MODS[:, m * KT:(m + 1) * KT, :]

        def by_tile(s4):
            return s4[:, 0:KT * 4].rearrange("p (k c) -> p k c", c=4)

        def turn(k):
            return k // 2

        def wout_loops(p):
            return [(0, 1), (1, 2)] if p.n + FT + 12 == N_BLOCKS else [(0, 2)]

        block = ctx.enter_context(nc.Block())

        @block.sync
        def _(sp):
            def load_main(k, slot, src, size=WB):
                if not (isinstance(k, int) and k < 2):
                    sp.wait_ge(lo_done, k - 1)
                sp.dma_start(RAW[slot][:, 0:size], src).then_inc(raw_full[slot], 16)

            def load_side(k):
                sp.wait_ge(side_lo, k + 1)
                sp.dma_start(SRAW[:, :], io["w_ada"][ds(k + H0, 1), :, :]
                             .rearrange("h p n -> p (h n)")).then_inc(side_full, 16)

            def load_start(b):
                if b >= START_SLOTS:
                    sp.wait_ge(rows_ready, b - START_SLOTS + 1)
                sp.dma_start(START[b % START_SLOTS][:, :].rearrange("p (h n) -> p h n", h=2),
                             io["w_ada"][2 * b:2 * b + 2, :, :].rearrange("h p n -> p h n")
                             ).then_inc(start_full[b % START_SLOTS], 16)

            sp.dma_start(COND[:, :, :], io["cond"]).then_inc(cond_in, 16)
            load_start(0)
            load_start(1)
            sp.dma_start(H[:, :, :], io["x"]).then_inc(x_in, 16)
            for dst, name in ((IDENT[:, :], "ident"), (BADA[:, :], "b_ada"), (LNG[:, :, :], "ln_g"),
                              (LNB[:, :, :], "ln_b"), (ONES[:, :], "ones"), (POSR[:, :, :], "pos_r"),
                              (POSC[:, :, :], "pos_c"), (TRI[:, :, :], "tri"),
                              (COLS[:, :, :, :], "cols"), (FOLD[:, :], "fold")):
                sp.dma_start(dst, io[name]).then_inc(consts_in, 16)
            for b in range(2, START_BLOCKS):
                load_start(b)

            def ffn(p):
                w_in, w_out = io["ff_in_" + p.f], io["ff_out_" + p.f]
                for first, end, side in p.loops:
                    def two_blocks(i):
                        for b in range(2):
                            load_main(p.n + b + 2 * i, (p.n + b) % 2,
                                      w_in[p.l, ds(2 * i + b, 1), :, :].rearrange("j p n -> p (j n)"))
                            if side:
                                load_side(p.a + b + 2 * i)

                    run_turns(sp, first, end, two_blocks)
                with sp.Fori(0, 2) as i:
                    for b in range(6):
                        lo, hi = KPARTS[b % 3]
                        load_main(p.n + FT + b + 6 * i, (p.n + FT + b) % 2,
                                  w_out[p.l, ds(2 * i + b // 3, 1), :, lo * 256:hi * 256]
                                  .rearrange("j p n -> p (j n)"), (hi - lo) * 256)
                        if b < p.out_sides:
                            load_side(p.a_out + b + p.out_sides * i)

            def mixer(p):
                k = p.a
                for b in range(IN_BLOCKS):
                    size = WB if b < IN_BLOCKS - 1 else WB // 2
                    load_main(p.n + b, (p.n + b) % 2, io["mix_in"][p.l, :, b * WB:b * WB + size], size)
                    if b == 1:
                        sp.wait_ge(*p.lin.at("xl", 4))
                        sp.dma_start(GU[:, :], io["gate_up"][p.l]).then_inc(p.s.sig("aux_in"), 16)
                        sp.dma_start(CINV[:, :, :], io["cinv"]).then_inc(p.s.sig("aux_in"), 16)
                        sp.dma_start(PW[:, :, :], io["pool_w"][p.l]).then_inc(p.s.sig("aux_in"), 16)
                    for _ in range(p.sides[b]):
                        load_side(k)
                        k += 1
                for b in range(4):
                    load_main(p.n + IN_BLOCKS + b, (p.n + IN_BLOCKS + b) % 2, io["mix_out"][p.l, b])

            for p in phases:
                (mixer if p.f == "mix" else ffn)(p)
            for q in range(4):
                sp.wait_ge(*lns[-1].at("mfull", q + 1))
                sp.dma_start(io["out"][:, 2 * q:2 * q + 2, :], M[q % 2][:, :, 0:LAT]).then_inc(out_done, 16)
                sp.wait_ge(out_done, 16 * (q + 1))

        @block.scalar
        def _(act):
            links = [0]

            def link(ins):
                links[0] += 1
                ins.then_inc(act_chain, 1)
                act.wait_ge(act_chain, links[0])

            def split_hi(k, t, slot):
                act.wait_ge(raw_full[slot], 16 * t + 16)
                if not (isinstance(k, int) and k < 2):
                    act.wait_ge(block_done, k - 1)
                act.copy(WH[slot][:, :], RAW[slot][:, :]).then_inc(hi_done, 1)

            def side_high(k):
                act.wait_ge(side_full, 16 * k + 16)
                if not (isinstance(k, int) and k == 0):
                    act.wait_ge(side_done, k)
                act.copy(SWH[:, :], SRAW[:, :]).then_inc(side_hi, 1)

            def rows_evac(g):
                act.wait_ge(side_done, 2 * g + 2)
                act.wait_ge(cols_ready, F0 + g)
                act.copy(ROWS[:, :], B_ROWS[0:4, 0:2 * P]).then_inc(rows_out, 1)

            def square(ln, t, par):
                act.wait_ge(*ln.at("z", t + 5))
                act.wait_ge(*ln.at("added", t + 1))
                act.activation(ln_sq[ln.scratch][par][:, 0:ln.w],
                               H[:, ds(t, 1), 0:ln.w].rearrange("p a n -> p (a n)"),
                               ACT.Square).then_inc(ln.sig("sq"), 1)

            def layernorm(ln):
                w, streams = ln.w, range(ln.w // LAT)
                act.preload_act_table_set("natural_log_exp_and_others")
                act.wait_ge(*ln.at("stats", 1))
                act.copy(MU[:, 0:w], B_SC[0][:, 0:w]).then_inc(ln.sig("mu"), 1)
                act.wait_ge(*ln.at("var", 1))
                act.activation(RS[:, 0:w], RS[:, 0:w], ACT.Ln).then_inc(ln.sig("ln"), 1)
                act.wait_ge(*ln.at("ln", 1))
                act.activation(RS[:, 0:w], RS[:, 0:w], ACT.Exp, scale=-0.5).then_inc(ln.sig("std"), 1)
                for q in range(4):
                    act.wait_ge(*ln.at("zn", q + 1))
                    if q >= 2 and ln.last:
                        act.wait_ge(out_done, 16 * (q - 1))
                    elif q >= 2:
                        act.wait_ge(*ln.at("xl", q - 1))
                    for t in range(2):
                        for s in streams:
                            c = slice(s * LAT, s * LAT + LAT)
                            ins = act.activation(M[q % 2][:, t, c], H[:, 2 * q + t, c], ACT.Identity,
                                                 bias=CB[:, 2 * q + t, s:s + 1], scale=CA[:, 2 * q + t, s:s + 1])
                    ins.then_inc(ln.sig("mfull"), 1)
                    if not ln.last:
                        act.wait_ge(*ln.at("mfull", q + 1))
                        act.copy(XH[:, 2 * q:2 * q + 2, 0:w], M[q % 2][:, :, 0:w]).then_inc(ln.sig("xh"), 1)

            act.wait_ge(cond_in, 16)
            act.activation(CSIL[:, :, :], COND[:, :, :], ACT.Silu).then_inc(sil_ready, 1)
            act.wait_ge(sil_ready, 1)
            act.copy(by_tile(S4)[:, :, 0:2], CSIL[:, :, :]).then_inc(s4_hi, 1)

            def start_rows(b):
                act.wait_ge(rows_ready, b + 1)
                if b:
                    act.wait_ge(cols_ready, b)
                act.copy(ROWS[0:2, :], BANK[b % 2][0:2, 0:2 * P]).then_inc(rows_out, 1)

            start_rows(0)
            start_rows(1)
            start_rows(2)
            for t in range(KT):
                square(lns[0], t, t % 2)
            for b in range(3, START_BLOCKS):
                start_rows(b)
            split_hi(0, 0, 0)
            layernorm(lns[0])

            def ffn(p):
                w = p.w
                for first, end, side in p.loops:
                    def two_blocks(i):
                        act.preload_act_table_set("silu_and_others")
                        for b in range(2):
                            k = p.n + b
                            if side:
                                side_high(p.a + b + 2 * i)
                            split_hi(k + 1 + 2 * i, turn(k + 1) + i, (k + 1) % 2)
                            if side and b:
                                rows_evac(turn(p.a) + i)
                            act.wait_ge(block_done, k + 1 + 2 * i)
                            act.activation(SG[:, 0:w], PAIR[b][0][:, 0:w], ACT.Silu).then_inc(p.s.sig("sg"), 1)
                            act.wait_ge(*p.s.at("af", b + 1 + 2 * i))
                            act.copy(AH[:, ds(2 * i + b, 1), 0:w].rearrange("p a n -> p (a n)"),
                                     AF[:, 0:w]).then_inc(p.s.sig("ah"), 1)

                    run_turns(act, first, end, two_blocks)
                for first, end in wout_loops(p):
                    with act.Fori(first, end) as i:
                        for b in range(6):
                            k = p.n + FT + b
                            if b < p.out_sides:
                                side_high(p.a_out + b + p.out_sides * i)
                            if not (first == 1 and b == 5):
                                split_hi(k + 1 + 6 * i, turn(k + 1) + 3 * i, (k + 1) % 2)
                            if b < p.out_sides and b % 2:
                                rows_evac(turn(p.a_out + b) + turn(p.out_sides) * i)
                            if b % 3 == 2:
                                for h in range(2):
                                    square(p.ln, 4 * i + 2 * (b // 3) + h, h)
                layernorm(p.ln)

            def mixer(p):
                s = p.s
                wq = p.nt * P
                ets = [0]
                side = [p.a]

                def step(b):
                    k = p.n + b + 1
                    if not p.sides[b]:
                        split_hi(k, turn(k), k % 2)
                    else:
                        side_high(side[0])
                        split_hi(k, turn(k), k % 2)
                        side_high(side[0] + 1)
                        rows_evac(turn(side[0]))
                        side[0] += 2
                    act.wait_ge(block_done, p.n + b + 1)

                def exp_buffer():
                    if ets[0] >= 2:
                        act.wait_ge(*s.at("et_used", ets[0] - 1))
                    ets[0] += 1
                    return ET[(ets[0] - 1) % 2]

                def gates(t):
                    act.wait_ge(*s.at("gp", t + 1))
                    e = exp_buffer()
                    link(act.activation(e[:, :], B_SC[t % 2][:, :], ACT.Abs))
                    link(act.activation(e[:, :], e[:, :], ACT.Exp, scale=-1.0))
                    act.activation(e[:, :], e[:, :], ACT.Ln, bias=1.0).then_inc(s.sig("et"), 1)

                def decays(j):
                    act.wait_ge(*s.at("bp", j + 1))
                    act.activation(exp_buffer()[:, :], B_SC[j % 2][:, :], ACT.Exp).then_inc(s.sig("et"), 1)
                    act.activation(exp_buffer()[:, :], B_SC[j % 2][:, :], ACT.Exp, scale=-1.0).then_inc(s.sig("et"), 1)

                def end_decays(t):
                    act.wait_ge(*s.at("enp", t + 1))
                    act.activation(exp_buffer()[:, :], B_SC[t % 2][:, :], ACT.Exp).then_inc(s.sig("et"), 1)

                def padded(t):
                    return UP[:, t, 0:wq // LAT, PAD:PAD + LAT]

                def by_stream(bank):
                    return bank[:, 0:wq].rearrange("p (s n) -> p s n", n=LAT)

                step(0)
                act.wait_ge(*p.lin.at("xl", 4))
                act.copy(GD[0:32, :], PAIR[0][0][0:32, :]).then_inc(s.sig("gd"), 1)
                act.wait_ge(*s.at("pads", 1))
                act.copy(padded(0), by_stream(PAIR[0][1])).then_inc(s.sig("up"), 1)
                step(1)
                act.copy(KTT[:, 0, :], PAIR[1][0][:, :])
                act.copy(KTT[:, 1, :], PAIR[1][1][:, :]).then_inc(s.sig("kv"), 1)
                act.preload_act_table_set("natural_log_exp_and_others")
                gates(0)
                gates(1)
                step(2)
                act.activation(QTT[:, 0, 0:wq], PAIR[0][0][:, 0:wq], ACT.Copy, scale=0.125)
                act.activation(QTT[:, 1, 0:wq], PAIR[0][1][:, 0:wq], ACT.Copy, scale=0.125).then_inc(s.sig("kv"), 1)
                gates(2)
                gates(3)
                step(3)
                for t in range(2):
                    act.wait_ge(*s.at("knp", t + 1))
                    act.copy(KN[:, 2 * t:2 * t + 2, :],
                             B_SC[t][:, :].rearrange("p (t n) -> p t n", n=256)).then_inc(s.sig("kn"), 1)
                step(4)
                decays(0)
                decays(1)
                step(5)
                decays(2)
                decays(3)
                step(6)
                act.copy(padded(3), by_stream(PAIR[0][0])).then_inc(s.sig("up"), 1)
                act.wait_ge(*s.at("et_used", 12))
                act.copy(RT[:, 0, 0:wq], PAIR[0][1][:, 0:wq]).then_inc(s.sig("rt"), 1)
                end_decays(0)
                end_decays(1)
                step(7)
                act.copy(RT[:, 1, 0:wq], PAIR[1][0][:, 0:wq])
                act.copy(RT[:, 2, 0:wq], PAIR[1][1][:, 0:wq]).then_inc(s.sig("rt"), 1)
                end_decays(2)
                end_decays(3)
                step(8)
                act.copy(RT[:, 3, 0:wq], PAIR[0][0][:, 0:wq]).then_inc(s.sig("rt"), 1)
                act.wait_ge(*s.at("rt", 3))
                act.activation(RT[:, :, 0:wq], RT[:, :, 0:wq], ACT.Silu).then_inc(s.sig("rt"), 1)
                act.preload_act_table_set("natural_log_exp_and_others")
                for t in range(4):
                    act.wait_ge(*s.at("pm", t + 1))
                    flat = UP[:, t, :, :].rearrange("p s n -> p (s n)")[:, 0:wq]
                    act.activation(flat, PAIR[(9 + t // 2) % 2][t % 2][:, 0:wq], ACT.Copy,
                                   scale=COLS[:, p.l, 0, t:t + 1]).then_inc(s.sig("ym"), 1)
                    act.wait_ge(*s.at("ym", t + 1))
                    act.copy(XH[:, t, 0:wq], flat).then_inc(s.sig("xh"), 1)
                for h in range(4):
                    act.wait_ge(*s.at("o", h + 1))
                    act.activation(SQH[:, h, 0:wq], PAIR[(11 + h // 2) % 2][h % 2][:, 0:wq],
                                   ACT.Square).then_inc(s.sig("osq"), 1)
                for h in range(4):
                    act.wait_ge(*s.at("ms", h + 1))
                    act.activation(SQH[:, h, 0:wq], B_SC[h % 2][:, 0:wq], ACT.Ln, bias=EPSC[:, 0:1],
                                   scale=float(KT)).then_inc(s.sig("ln"), 1)
                    act.wait_ge(*s.at("ln", h + 1))
                    act.activation(SQH[:, h, 0:wq], SQH[:, h, 0:wq], ACT.Exp, scale=-0.5).then_inc(s.sig("std"), 1)
                for h in range(4):
                    act.wait_ge(*s.at("yh", h + 1))
                    act.copy(XH[:, 4 + h, 0:wq], SQH[:, h, 0:wq]).then_inc(s.sig("xh"), 1)
                for b in range(4):
                    k = p.n + IN_BLOCKS + b
                    split_hi(k + 1, turn(k + 1), (k + 1) % 2)
                    for h in range(2):
                        square(p.ln, 2 * b + h, h)
                layernorm(p.ln)

            for p in phases:
                (mixer if p.f == "mix" else ffn)(p)

        @block.vector
        def _(dve):
            links = [0]

            def link(ins):
                links[0] += 1
                ins.then_inc(dve_chain, 1)
                dve.wait_ge(dve_chain, links[0])

            def split_lo(k, slot):
                dve.wait_ge(hi_done, k + 1)
                dve.tensor_tensor(WL[slot][:, :], RAW[slot][:, :], WH[slot][:, :].bitcast(F32),
                                  ALU.subtract).then_inc(lo_done, 1)

            def side_low(k):
                dve.wait_ge(side_hi, k + 1)
                dve.tensor_tensor(SWL[:, :], SRAW[:, :], SWH[:, :].bitcast(F32),
                                  ALU.subtract).then_inc(side_lo, 1)

            def fold(f):
                dve.wait_ge(cols_ready, f + 1)
                dve.tensor_tensor(MODS[:, ds(2 * f, 2), :], B_COLS[:, 0:4].rearrange("p (a c) -> p a c", c=2),
                                  BADA[:, ds(2 * f, 2)].unsqueeze(2).broadcast_to([P, 2, 2]),
                                  ALU.add).then_inc(mods_done, 1)

            def gates_ready(p):
                mods_ready(dve, p.gate)
                dve.tensor_scalar(CG[:, :, :], mod(p.gate), p.gate_scale, None, ALU.mult).then_inc(p.ln.sig("z"), 4)
                dve.wait_ge(*p.ln.at("z", 4))
                dve.wait_ge(*p.lin.at("h", 1))

            def residual(p, t, bank):
                for s in range(p.ln.w // LAT):
                    c = slice(s * LAT, s * LAT + LAT)
                    h = H[:, ds(t, 1), c].rearrange("p a n -> p (a n)")
                    g = CG[:, ds(t, 1), s:s + 1].rearrange("p a n -> p (a n)")
                    ins = dve.scalar_tensor_tensor(h, bank[:, c], g, h, op0=ALU.mult, op1=ALU.add)
                ins.then_inc(p.ln.sig("z"), 1)

            def layernorm(ln):
                w = ln.w
                g, b = (v[:, ln.q, :].unsqueeze(2).broadcast_to([P, KT, 2]) for v in (LNG, LNB))
                if ln.last:
                    dve.tensor_copy(CA[:, :, :], g)
                    link(dve.tensor_copy(CB[:, :, :], b))
                else:
                    mods_ready(dve, ln.scale)
                    dve.scalar_tensor_tensor(CA[:, :, :], mod(ln.scale), 1.0, g, op0=ALU.add, op1=ALU.mult)
                    link(dve.scalar_tensor_tensor(CB[:, :, :], mod(ln.scale), 1.0, b, op0=ALU.add, op1=ALU.mult))
                    dve.tensor_scalar(CHA[:, :, :], g, ALPHA, None, ALU.mult)
                    dve.tensor_scalar(CHB[:, :, :], b, ALPHA, None, ALU.mult)
                    link(dve.tensor_tensor(CB[:, :, :], CB[:, :, :], mod(ln.shift), ALU.add))
                dve.wait_ge(*ln.at("mu", 1))
                link(dve.tensor_tensor(RS[:, 0:w], MU[:, 0:w], MU[:, 0:w], ALU.mult))
                dve.wait_ge(*ln.at("stats", 2))
                dve.scalar_tensor_tensor(RS[:, 0:w], B_SC[1][:, 0:w], EPS, RS[:, 0:w], op0=ALU.add,
                                         op1=ALU.subtract).then_inc(ln.sig("var"), 1)

                def low(q):
                    dve.wait_ge(*ln.at("xh", q + 1))
                    dve.tensor_tensor(XL[:, 2 * q:2 * q + 2, 0:w], M[q % 2][:, :, 0:w],
                                      XH[:, 2 * q:2 * q + 2, 0:w].bitcast(F32), ALU.subtract).then_inc(ln.sig("xl"), 1)

                z0 = H[:, 0:2, 0:w]
                link(dve.tensor_tensor(z0, z0, MU[:, 0:w].unsqueeze(1).broadcast_to([P, 2, w]), ALU.subtract))
                dve.wait_ge(*ln.at("std", 1))
                for q in range(4):
                    z = H[:, 2 * q:2 * q + 2, 0:w]
                    if q:
                        dve.wait_ge(*ln.at("zc", q))
                    dve.tensor_tensor(z, z, RS[:, 0:w].unsqueeze(1).broadcast_to([P, 2, w]),
                                      ALU.mult).then_inc(ln.sig("zn"), 1)
                    if q and not ln.last:
                        low(q - 1)
                if not ln.last:
                    low(3)

            dve.memset(EPSC[:, 0:1], EPS).then_inc(eps_set, 1)
            for i, free in enumerate((side_lo, *pair_free)):
                dve.memset(EPSC[:, 1 + i:2 + i], 0.0).then_inc(free, 1)
            dve.memset(EPSC[:, 4:5], 0.0).then_inc(lns[0].sig("half"), 4)
            dve.memset(S4[:, KT * 4:].bitcast(F32), 0.0).then_inc(s4_tail, 1)
            dve.wait_ge(s4_hi, 1)
            dve.tensor_tensor(by_tile(S4)[:, :, 2:4], CSIL[:, :, :], by_tile(S4)[:, :, 0:2].bitcast(F32),
                              ALU.subtract).then_inc(s4_ready, 1)
            dve.wait_ge(x_in, 16)
            dve.wait_ge(consts_in, 10 * 16)
            dve.tensor_scalar(MASK[:, :, :], TRI[:, 0:2, :], 0.0, None, ALU.is_gt).then_inc(mask_ready, 1)
            for t in range(4):
                z = H[:, t, 0:LAT].rearrange("p (r c) -> p r c", c=64)
                dve.tensor_tensor(z, z, POSR[:, t, :].unsqueeze(2).broadcast_to([P, 4, 64]), ALU.add)
            for t in range(4):
                z = H[:, 4 + t, 0:LAT].rearrange("p (r c) -> p r c", c=64)
                ins = dve.tensor_tensor(z, z, POSC[:, t, :].unsqueeze(1).broadcast_to([P, 4, 64]), ALU.add)
            ins.then_inc(lns[0].sig("z"), 12)
            for b in range(START_BLOCKS):
                fold(b)
            split_lo(0, 0)
            layernorm(lns[0])

            def ffn(p):
                w = p.w
                for first, end, side in p.loops:
                    def two_blocks(i):
                        for b in range(2):
                            k = p.n + b
                            if side:
                                side_low(p.a + b + 2 * i)
                            split_lo(k + 1 + 2 * i, (k + 1) % 2)
                            dve.wait_ge(*p.s.at("sg", b + 1 + 2 * i))
                            dve.wait_ge(pair_free[1 - b], turn(p.G) + 1 + b + i)
                            dve.tensor_tensor(AF[:, 0:w], SG[:, 0:w], PAIR[b][1][:, 0:w],
                                              ALU.mult).then_inc(p.s.sig("af"), 1)
                            dve.wait_ge(*p.s.at("ah", b + 1 + 2 * i))
                            ah = AH[:, ds(2 * i + b, 1), 0:w].rearrange("p a n -> p (a n)")
                            al = AL[:, ds(2 * i + b, 1), 0:w].rearrange("p a n -> p (a n)")
                            dve.tensor_tensor(al, AF[:, 0:w], ah.bitcast(F32),
                                              ALU.subtract).then_inc(pair_free[b], 1)
                            if side and b:
                                fold(turn(p.a) + F0 + i)

                    run_turns(dve, first, end, two_blocks)
                gates_ready(p)
                for first, end in wout_loops(p):
                    with dve.Fori(first, end) as i:
                        for b in range(6):
                            k = p.n + FT + b
                            if b < p.out_sides:
                                side_low(p.a_out + b + p.out_sides * i)
                            if not (first == 1 and b == 5):
                                split_lo(k + 1 + 6 * i, (k + 1) % 2)
                            if b % 3 == 2:
                                dve.wait_ge(*p.ln.at("half", 2 * i + b // 3 + 1))
                                residual(p, 4 * i + 2 * (b // 3), PAIR[b // 3][0])
                                dve.wait_ge(block_done, k + 1 + 6 * i)
                                residual(p, 4 * i + 2 * (b // 3) + 1, PAIR[b // 3][1])
                            if b < p.out_sides and b % 2:
                                fold(turn(p.a_out + b) + F0 + turn(p.out_sides) * i)
                layernorm(p.ln)

            def mixer(p):
                s = p.s
                wq, nt = p.nt * P, p.nt
                ns = wq // LAT
                side = [p.a]

                def step(b):
                    k = p.n + b + 1
                    if not p.sides[b]:
                        split_lo(k, k % 2)
                    else:
                        side_low(side[0])
                        split_lo(k, k % 2)
                        side_low(side[0] + 1)
                        fold(turn(side[0]) + F0)
                        side[0] += 2
                    dve.wait_ge(block_done, p.n + b + 1)

                def log_gates(t):
                    dve.wait_ge(*s.at("et", t + 1))
                    dve.scalar_tensor_tensor(LA[:, t, :], B_SC[t % 2][:, :], 0.0, ET[t % 2][:, :],
                                             op0=ALU.min, op1=ALU.subtract).then_inc(s.sig("et_used"), 1)

                def scaled(j):
                    c, d = j // 2, j % 2
                    dve.wait_ge(*s.at("et", 4 + 2 * j + 1))
                    dve.wait_ge(*s.at("kv", 2))
                    dve.tensor_tensor(QF[d][:, c, 0:wq], QTT[:, c, 0:wq], ET[0][:, 0:wq], ALU.mult)
                    dve.tensor_copy(DEC[:, d, c, :], ET[0][:, (CHUNK - 1 if d == 0 else 0)::CHUNK]).then_inc(s.sig("et_used"), 1)
                    dve.wait_ge(*s.at("et", 4 + 2 * j + 2))
                    dve.tensor_tensor(KF[d][:, c, :], KTT[:, c, :], ET[1][:, :], ALU.mult).then_inc(s.sig("et_used"), 1)

                def end_keys(t):
                    dve.wait_ge(*s.at("et", 12 + t + 1))
                    dve.wait_ge(*s.at("kn", 2))
                    dve.tensor_tensor(KE[:, t, :].rearrange("p (d n) -> p d n", d=2),
                                      ET[t % 2][:, :].rearrange("p (d n) -> p d n", d=2),
                                      KN[:, t, :].unsqueeze(1).broadcast_to([P, 2, 256]),
                                      ALU.mult).then_inc(s.sig("et_used"), 1)

                def values(v):
                    for t in range(2):
                        ins = dve.tensor_copy(VN[:, 2 * t:2 * t + 2, 256 * v:256 * v + 256],
                                              PAIR[(3 + v) % 2][t][:, :].rearrange("p (t n) -> p t n", n=256))
                    ins.then_inc(s.sig("v_in"), 1)

                def pool(t):
                    window = WINDOWS[t]
                    src, dst, v = UP[:, t, 0:ns, :], PB, 1
                    while v < window:
                        lo, hi = PAD - window // 2, PAD + LAT + window // 2 - 2 * v
                        link(dve.tensor_tensor(dst[:, 0:ns, lo:hi], src[:, :, lo:hi], src[:, :, lo + v:hi + v], ALU.add))
                        src, dst, v = dst[:, 0:ns, :], PC if dst is PB else PB, 2 * v
                    lo = PAD - window // 2
                    mean = dst[:, 0:ns, PAD:PAD + LAT]
                    link(dve.tensor_tensor(mean, src[:, :, lo:lo + LAT],
                                           CINV[:, t, :].unsqueeze(1).broadcast_to([P, ns, LAT]), ALU.mult))
                    u = UP[:, t, 0:ns, PAD:PAD + LAT]
                    dve.tensor_tensor(u, mean, u, ALU.subtract).then_inc(s.sig("pooled"), 1)

                dve.wait_ge(*p.lin.at("xl", 4))
                dve.memset(UP[:, :, :, 0:PAD], 0.0)
                dve.memset(UP[:, :, :, PAD + LAT:UPW], 0.0)
                dve.memset(GD[32:33, :], 1.0).then_inc(s.sig("pads"), 1)
                step(0)
                step(1)
                log_gates(0)
                log_gates(1)
                step(2)
                log_gates(2)
                log_gates(3)
                step(3)
                values(0)
                step(4)
                values(1)
                scaled(0)
                scaled(1)
                step(5)
                for t in range(2):
                    ins = dve.tensor_copy(UP[:, 1 + t, 0:ns, PAD:PAD + LAT],
                                          PAIR[1][t][:, 0:wq].rearrange("p (s n) -> p s n", n=LAT))
                ins.then_inc(s.sig("u12"), 1)
                scaled(2)
                scaled(3)
                step(6)
                end_keys(0)
                end_keys(1)
                step(7)
                end_keys(2)
                end_keys(3)
                dve.wait_ge(*s.at("aux_in", 48))
                dve.wait_ge(*s.at("up", 1))
                dve.wait_ge(*s.at("u12", 1))
                pool(0)
                pool(1)
                step(8)
                for i in range(7):
                    for d in range(2):
                        dve.wait_ge(*s.at("u", 2 * i + d + 1))
                        if i:
                            dve.wait_ge(*s.at("state", 2 * (i - 1) + d + 1))
                        for c in range(2):
                            u = B_SC[d][:, c * P:(c + 1) * P]
                            if i == 0:
                                ins = dve.tensor_copy(SS[d][:, i, c, :], u)
                            else:
                                ch = CHUNK_ORDER[d][i]
                                ins = dve.scalar_tensor_tensor(SS[d][:, i, c, :], SS[d][:, i - 1, c, :],
                                                               DEC[:, d, c, ch:ch + 1], u,
                                                               op0=ALU.mult, op1=ALU.add)
                        ins.then_inc(s.sig("state"), 1)
                pool(2)
                dve.wait_ge(*s.at("up", 2))
                pool(3)
                for t in range(4):
                    dve.wait_ge(*s.at("xh", t + 1))
                    flat = UP[:, t, :, :].rearrange("p s n -> p (s n)")[:, 0:wq]
                    dve.tensor_tensor(XL[:, t, 0:wq], flat, XH[:, t, 0:wq].bitcast(F32),
                                      ALU.subtract).then_inc(s.sig("xl"), 1)
                for d in range(2):
                    ins = dve.memset(TFB[d][:, :], 0.0)
                link(ins)
                dve.wait_ge(mask_ready, 1)
                for h in range(4):
                    if h:
                        dve.wait_ge(*s.at("at", h))
                    for d in range(2):
                        dve.wait_ge(*s.at("sc", 2 * h + d + 1))
                        dve.copy_predicated(TFB[d][:, 0:wq].rearrange("p (t n) -> p t n", n=P),
                                            MASK[:, d, :].unsqueeze(1).broadcast_to([P, nt, P]),
                                            B_SC[d][:, 0:wq].rearrange("p (t n) -> p t n", n=P)).then_inc(s.sig("cp"), 1)
                    dve.wait_ge(*s.at("cp", 2 * h + 2))
                    dve.tensor_tensor(AT[:, h, 0:wq], TFB[0][:, 0:wq], TFB[1][:, 0:wq], ALU.add).then_inc(s.sig("at"), 1)
                for h in range(4):
                    y = SQH[:, h, 0:wq]
                    dve.wait_ge(*s.at("std", h + 1))
                    link(dve.tensor_tensor(y, PAIR[(11 + h // 2) % 2][h % 2][:, 0:wq], y, ALU.mult))
                    dve.wait_ge(*s.at("rt", 4))
                    dve.scalar_tensor_tensor(y, y, COLS[:, p.l, 1, h:h + 1], RT[:, h, 0:wq],
                                             op0=ALU.mult, op1=ALU.mult).then_inc(s.sig("yh"), 1)
                for h in range(4):
                    dve.wait_ge(*s.at("xh", 4 + h + 1))
                    dve.tensor_tensor(XL[:, 4 + h, 0:wq], SQH[:, h, 0:wq], XH[:, 4 + h, 0:wq].bitcast(F32),
                                      ALU.subtract).then_inc(s.sig("xl"), 1)
                gates_ready(p)
                for b in range(4):
                    k = p.n + IN_BLOCKS + b
                    split_lo(k + 1, (k + 1) % 2)
                    dve.wait_ge(*p.ln.at("half", b + 1))
                    residual(p, 2 * b, PAIR[b % 2][0])
                    dve.wait_ge(block_done, k + 1)
                    residual(p, 2 * b + 1, PAIR[b % 2][1])
                layernorm(p.ln)

            for p in phases:
                (mixer if p.f == "mix" else ffn)(p)

        @block.gpsimd
        def _(pool):
            def layernorm(ln):
                acc, w = ln_acc[ln.scratch], ln.w
                for a in acc:
                    pool.memset(a[:, :], 0.0).then_inc(ln.sig("added"), 1)
                with pool.Fori(0, 3) as i:
                    for b in range(2):
                        pool.wait_ge(*ln.at("z", 2 * i + b + 5))
                        pool.wait_ge(*ln.at("added", 2 * i + b + 2))
                        pool.tensor_tensor(acc[0][:, 0:w], acc[0][:, 0:w],
                                           H[:, ds(2 * i + b, 1), 0:w].rearrange("p a n -> p (a n)"), ALU.add)
                        pool.wait_ge(*ln.at("sq", 2 * i + b + 1))
                        pool.tensor_tensor(acc[1][:, 0:w], acc[1][:, 0:w], ln_sq[ln.scratch][b][:, 0:w],
                                           ALU.add).then_inc(ln.sig("added"), 1)
                pool.wait_ge(*ln.at("mu", 1))
                for q in range(1, 4):
                    z = H[:, 2 * q:2 * q + 2, 0:w]
                    pool.tensor_tensor(z, z, MU[:, 0:w].unsqueeze(1).broadcast_to([P, 2, w]),
                                       ALU.subtract).then_inc(ln.sig("zc"), 1)
                if ln.last:
                    return
                for q in range(4):
                    pool.wait_ge(*ln.at("mfull", q + 1))
                    for t in (2 * q, 2 * q + 1):
                        for s in range(w // LAT):
                            c = slice(s * LAT, s * LAT + LAT)
                            ins = pool.tensor_scalar(H[:, t, c], H[:, t, c], CHA[:, t, s:s + 1],
                                                     CHB[:, t, s:s + 1], ALU.mult, ALU.add)
                ins.then_inc(ln.sig("h"), 1)

            layernorm(lns[0])
            for p in phases:
                if p.f == "mix":
                    pool.wait_ge(*p.s.at("o", 4))
                else:
                    pool.wait_ge(block_done, p.n + FT)
                layernorm(p.ln)

        @block.tensor
        def _(pe):
            def three(out, wh, wl, xh, xl, start, stop):
                pe.matmul(out, wh, xh, start=start, stop=False)
                pe.matmul(out, wh, xl, start=False, stop=False)
                return pe.matmul(out, wl, xh, start=False, stop=stop)

            def columns(f, rows=4):
                pe.wait_ge(rows_out, f + 1)
                if not (isinstance(f, int) and f == 0):
                    pe.wait_ge(mods_done, f)
                for j in range(2):
                    ins = pe.matmul(B_COLS[:, 2 * j:2 * j + 2], ROWS[0:rows, j * P:(j + 1) * P], FOLD[0:rows, :],
                                    start=True, stop=True)
                ins.then_inc(cols_ready, 1)

            def side(g, half):
                pe.wait_ge(side_lo, 2 * g + half + 2)
                if half == 0:
                    pe.wait_ge(rows_out, F0 + g)
                for x, part in enumerate((SWH, SWL)):
                    for j in range(KT // 2):
                        r = 4 * (half * KT // 2 + j)
                        ins = pe.matmul(B_ROWS[:, 0:2 * P], S4[:, r:r + P], part[:, j * 2 * P:(j + 1) * 2 * P],
                                        start=(half == 0 and x == 0 and j == 0),
                                        stop=(half == 1 and x == 1 and j == KT // 2 - 1))
                ins.then_inc(side_done, 1)

            def stats(ln):
                acc, w = ln_acc[ln.scratch], ln.w
                pe.wait_ge(*ln.at("added", 8))
                pe.matmul(B_SC[0][:, 0:w], ONES[:, :], acc[0][:, 0:w], start=True, stop=False)
                pe.matmul(B_SC[1][:, 0:w], ONES[:, :], acc[1][:, 0:w], start=True, stop=False)
                for t in (6, 7):
                    pe.wait_ge(*ln.at("z", t + 5))
                    ins = pe.matmul(B_SC[0][:, 0:w], ONES[:, :], H[:, t, 0:w], start=False, stop=t == 7)
                    if t == 7:
                        ins.then_inc(ln.sig("stats"), 1)
                    pe.wait_ge(*ln.at("sq", t + 1))
                    ins = pe.matmul(B_SC[1][:, 0:w], ONES[:, :], ln_sq[ln.scratch][t - 6][:, 0:w],
                                    start=False, stop=t == 7)
                ins.then_inc(ln.sig("stats"), 1)

            pe.wait_ge(sil_ready, 1)
            for b in range(START_BLOCKS):
                pe.wait_ge(start_full[b % START_SLOTS], 16 * (b // START_SLOTS) + 16)
                if b >= 2:
                    pe.wait_ge(rows_out, b - 1)
                for k in range(KT):
                    ins = pe.matmul(BANK[b % 2][0:2, 0:2 * P], CSIL[:, k, :],
                                    START[b % START_SLOTS][:, k * 2 * P:(k + 1) * 2 * P],
                                    start=k == 0, stop=k == KT - 1)
                ins.then_inc(rows_ready, 1)
                if b == 1:
                    pe.wait_ge(consts_in, 10 * 16)
                if b:
                    columns(b - 1, 2)
            columns(START_BLOCKS - 1, 2)
            pe.wait_ge(s4_ready, 1)
            pe.wait_ge(s4_tail, 1)
            stats(lns[0])

            def products(by_row):
                if by_row:
                    return [(h, k) for k in range(KT) for h in range(2)]
                return [(h, k) for h in range(2) for k in range(KT)]

            def ffn(p):
                w = p.w
                for first, end, sided in p.loops:
                    def two_blocks(i):
                        for b in range(2):
                            slot = (p.n + b) % 2
                            pe.wait_ge(lo_done, p.n + b + 1 + 2 * i)
                            pe.wait_ge(pair_free[b], turn(p.G + b) + 1 + i)
                            first_block = end == 1 and b == 0
                            for h, k in products(first_block):
                                if first_block and h == 0 and k % 2 == 0:
                                    pe.wait_ge(*p.lin.at("xl", k // 2 + 1))
                                if sided and (h, k) == (1, 4):
                                    side(turn(p.a) + i, b)
                                c = slice(k * 256 + h * P, k * 256 + (h + 1) * P)
                                ins = three(PAIR[b][h][:, 0:w], WH[slot][:, c], WL[slot][:, c],
                                            XH[:, k, 0:w], XL[:, k, 0:w], k == 0, k == KT - 1)
                            ins.then_inc(block_done, 1)
                            if sided and b:
                                columns(turn(p.a) + F0 + i)

                    run_turns(pe, first, end, two_blocks)
                w = p.ln.w
                with pe.Fori(0, 2) as i:
                    for b in range(6):
                        slot = (p.n + FT + b) % 2
                        lo, hi = KPARTS[b % 3]
                        pe.wait_ge(lo_done, p.n + FT + b + 1 + 6 * i)
                        for j in range(2):
                            pe.wait_ge(pair_free[j], turn(p.G + hi - 2 + j) + 2)
                        if b % 3 == 0:
                            pe.wait_ge(*p.ln.at("z", 4 * i + 2 * (b // 3) + 2))
                        for h in range(2):
                            for k in range(lo, hi):
                                if h == 1 and k == lo + 4 and b < p.out_sides:
                                    side(turn(p.a_out + b) + turn(p.out_sides) * i, b % 2)
                                c = slice((k - lo) * 256 + h * P, (k - lo) * 256 + (h + 1) * P)
                                ins = three(PAIR[b // 3][h][:, 0:w], WH[slot][:, c], WL[slot][:, c],
                                            AH[:, k, 0:w], AL[:, k, 0:w], k == 0, k == FT - 1)
                            if h == 0 and b % 3 == 2:
                                ins.then_inc(p.ln.sig("half"), 1)
                        ins.then_inc(block_done, 1)
                        if b < p.out_sides and b % 2:
                            columns(turn(p.a_out + b) + F0 + turn(p.out_sides) * i)
                stats(p.ln)

            def mixer(p):
                s = p.s
                wq, nt = p.nt * P, p.nt
                side_at = [p.a]

                def side_half(b, half):
                    if p.sides[b]:
                        side(turn(side_at[0]), half)

                def side_columns(b):
                    if p.sides[b]:
                        columns(turn(side_at[0]) + F0)
                        side_at[0] += 2

                def project(b, widths):
                    slot, row = (p.n + b) % 2, P * len(widths)
                    pe.wait_ge(lo_done, p.n + b + 1)
                    for h, k in products(b == 0)[0:KT * len(widths)]:
                        w = widths[h]
                        if b == 0 and h == 0 and k % 2 == 0:
                            pe.wait_ge(*p.lin.at("xl", k // 2 + 1))
                        if (h, k) == (1, 0):
                            side_half(b, 0)
                        if (h, k) == (1, 7):
                            side_half(b, 1)
                        c = slice(k * row + h * P, k * row + (h + 1) * P)
                        ins = three(PAIR[b % 2][h][:, 0:w], WH[slot][:, c], WL[slot][:, c],
                                    XH[:, k, 0:w], XL[:, k, 0:w], k == 0, k == KT - 1)
                    ins.then_inc(block_done, 1)
                    side_columns(b)

                def project_tokens(b):
                    slot = (p.n + b) % 2
                    pe.wait_ge(lo_done, p.n + b + 1)
                    for t in range(4):
                        x = slice(t * P, (t + 1) * P)
                        for k in range(KT):
                            c = slice(k * 256, (k + 1) * 256)
                            ins = three(PAIR[b % 2][t // 2][:, (t % 2) * 256:(t % 2) * 256 + 256],
                                        XH[:, k, x], XL[:, k, x], WH[slot][:, c], WL[slot][:, c],
                                        k == 0, k == KT - 1)
                        if t == 1:
                            side_half(b, 0)
                        if t == 2:
                            side_half(b, 1)
                    ins.then_inc(block_done, 1)
                    side_columns(b)

                def gates(t):
                    pe.wait_ge(*s.at("gd", 1))
                    pe.wait_ge(*s.at("pads", 1))
                    pe.wait_ge(*s.at("aux_in", 48))
                    if t >= 2:
                        pe.wait_ge(*s.at("et_used", t - 1))
                    pe.matmul(B_SC[t % 2][:, :], GD[:, t * P:(t + 1) * P], GU[:, :],
                              start=True, stop=True).then_inc(s.sig("gp"), 1)

                def turn_keys(t):
                    pe.wait_ge(*s.at("et_used", 3 + t))
                    for j in range(2):
                        for c in range(2):
                            x = (2 * t + j) * P
                            ins = pe.transpose(B_SC[t][:, j * 256 + c * P:j * 256 + (c + 1) * P],
                                               KTT[:, c, x:x + P], IDENT[:, :])
                    ins.then_inc(s.sig("knp"), 1)

                def cumulate(j):
                    c, d = j // 2, j % 2
                    if j < 2:
                        pe.wait_ge(*s.at("kn", j + 1))
                    else:
                        pe.wait_ge(*s.at("et", 4 + 2 * (j - 1)))
                    for t in range(4):
                        ins = pe.matmul(B_SC[d][:, t * P:(t + 1) * P], LA[:, t, d * 256 + c * P:d * 256 + (c + 1) * P],
                                        TRI[:, d, :], start=True, stop=True)
                    ins.then_inc(s.sig("bp"), 1)

                def to_chunk_end(t):
                    pe.wait_ge(*s.at("et", 10 + t + (t < 2) * t if t < 2 else 11 + t))
                    for d in range(2):
                        ins = pe.matmul(B_SC[t % 2][:, d * 256:(d + 1) * 256], TRI[:, 2 + d, :],
                                        LA[:, t, d * 256:(d + 1) * 256], start=True, stop=True)
                    ins.then_inc(s.sig("enp"), 1)

                def updates(i, d):
                    ch = CHUNK_ORDER[d][i]
                    t, r = ch // 2, slice((ch % 2) * CHUNK, (ch % 2 + 1) * CHUNK)
                    if i:
                        pe.wait_ge(*s.at("state", 2 * (i - 1) + d + 1))
                    for c in range(2):
                        for o in range(2):
                            x = d * 256 + c * P + o * 64
                            h = 2 * c + o
                            ins = pe.matmul(B_SC[d][o * 64:(o + 1) * 64, c * P:(c + 1) * P],
                                            KE[r, t, x:x + 64], VN[r, t, h * P:(h + 1) * P],
                                            start=True, stop=True)
                    ins.then_inc(s.sig("u"), 1)

                def pooled(t):
                    pe.wait_ge(*s.at("pooled", t + 1))
                    pe.wait_ge(*s.at("rt", 2 if t < 2 else 3))
                    pe.matmul(PAIR[(9 + t // 2) % 2][t % 2][:, 0:wq], PW[:, t, :],
                              UP[:, t, 0:wq // LAT, PAD:PAD + LAT], start=True, stop=True).then_inc(s.sig("pm"), 1)

                def scores(h):
                    c, r = h // 2, slice((h % 2) * 64, (h % 2 + 1) * 64)
                    for d in range(2):
                        if h:
                            pe.wait_ge(*s.at("cp", 2 * (h - 1) + d + 1))
                        for t in range(nt):
                            x = slice(t * P, (t + 1) * P)
                            ins = pe.matmul(B_SC[d][:, x], KF[d][r, c, x], QF[d][r, c, x], start=True, stop=True)
                        ins.then_inc(s.sig("sc"), 1)

                def outputs(h):
                    c, r = h // 2, slice((h % 2) * 64, (h % 2 + 1) * 64)
                    bank = PAIR[(11 + c) % 2][h % 2]
                    pe.wait_ge(*s.at("ym", 2 * c + 2))
                    pe.wait_ge(*s.at("at", h + 1))
                    for t in range(nt):
                        x = slice(t * P, (t + 1) * P)
                        pe.matmul(bank[:, x], VN[:, t, h * P:(h + 1) * P], AT[:, h, x],
                                  start=(t == 0), stop=False, skip_group_check=True)
                    for d in range(2):
                        for i in range(1, 8):
                            ch = CHUNK_ORDER[d][i]
                            if ch // 2 < nt:
                                x = slice(ch * CHUNK, (ch + 1) * CHUNK)
                                ins = pe.matmul(bank[:, x], SS[d][r, i - 1, c, :], QF[d][r, c, x],
                                                start=False, stop=(d == 1 and i == 7), skip_group_check=True)
                    ins.then_inc(s.sig("o"), 1)

                project(0, (TOK, wq))
                project(1, (TOK, TOK))
                gates(0)
                gates(1)
                pe.wait_ge(*s.at("gd", 1))
                pe.wait_ge(*s.at("up", 1))
                project(2, (wq, wq))
                gates(2)
                gates(3)
                pe.wait_ge(*s.at("kv", 1))
                project_tokens(3)
                turn_keys(0)
                turn_keys(1)
                pe.wait_ge(*s.at("kv", 2))
                project_tokens(4)
                cumulate(0)
                cumulate(1)
                pe.wait_ge(*s.at("v_in", 1))
                project(5, (wq, wq))
                cumulate(2)
                cumulate(3)
                pe.wait_ge(*s.at("v_in", 2))
                project(6, (wq, wq))
                to_chunk_end(0)
                to_chunk_end(1)
                pe.wait_ge(*s.at("u12", 1))
                project(7, (wq, wq))
                to_chunk_end(2)
                to_chunk_end(3)
                pe.wait_ge(*s.at("up", 2))
                pe.wait_ge(*s.at("rt", 1))
                project(8, (wq,))
                pe.wait_ge(*s.at("et_used", 16))
                for i in range(7):
                    for d in range(2):
                        updates(i, d)
                for t in range(4):
                    pooled(t)
                pe.wait_ge(*s.at("state", 14))
                scores(0)
                for h in range(4):
                    if h < 3:
                        scores(h + 1)
                    outputs(h)
                for h in range(4):
                    pe.wait_ge(*s.at("osq", h + 1))
                    if h >= 2:
                        pe.wait_ge(*s.at("std", h - 1))
                    else:
                        pe.wait_ge(*s.at("cp", 7 + h))
                    pe.matmul(B_SC[h % 2][:, 0:wq], ONES[:, :], SQH[:, h, 0:wq], start=True,
                              stop=True).then_inc(s.sig("ms"), 1)
                w = p.ln.w
                pe.wait_ge(*s.at("xl", 8))
                for b in range(4):
                    slot = (p.n + IN_BLOCKS + b) % 2
                    pe.wait_ge(lo_done, p.n + IN_BLOCKS + b + 1)
                    pe.wait_ge(*p.ln.at("z", 2 * b + 2))
                    for h in range(2):
                        for k in range(KT):
                            c = slice(k * 256 + h * P, k * 256 + (h + 1) * P)
                            ins = three(PAIR[b % 2][h][:, 0:w], WH[slot][:, c], WL[slot][:, c],
                                        XH[:, k, 0:w], XL[:, k, 0:w], k == 0, k == KT - 1)
                        if h == 0:
                            ins.then_inc(p.ln.sig("half"), 1)
                    ins.then_inc(block_done, 1)
                stats(p.ln)

            for p in phases:
                (mixer if p.f == "mix" else ffn)(p)


def kernel(**inputs):
    import numpy as np
    import concourse.bacc as bacc
    from concourse.bass_utils import run_bass_kernel_spmd as run

    v = {k: np.asarray(x) for k, x in inputs.items()}
    f32 = np.float32

    def feature_major(a):
        return np.ascontiguousarray(a.T.reshape(-1, P, a.shape[0]).transpose(1, 0, 2))

    def columns(a):
        return np.ascontiguousarray(a.reshape(-1, KT, P).transpose(2, 0, 1))

    def blocks(w, j, n):
        L, K, _ = w.shape
        return np.ascontiguousarray(w.reshape(L, K // P, P, j, n).transpose(0, 3, 2, 1, 4)
                                    .reshape(L, j, P, K // P * n))

    arrays = {}
    arrays["x"] = feature_major(np.concatenate([v["x"][0], v["ctx"][0]], axis=0))
    arrays["cond"] = feature_major(np.stack([v["c"][0], v["c_ctx"]]))
    w = blocks(v["w_ada"], N_MOD * KT // 2, 2 * P).reshape(FULLS, P, 2, D).transpose(0, 2, 1, 3)
    arrays["w_ada"] = np.ascontiguousarray(w.reshape(HALVES, P, D))
    arrays["b_ada"] = np.ascontiguousarray(v["b_ada"].reshape(2 * FULLS, P).T)
    one, zero = np.ones((1, D), f32), np.zeros((1, D), f32)
    arrays["ln_g"] = columns(np.concatenate([one, v["ln_g"].reshape(-1, D)]))
    arrays["ln_b"] = columns(np.concatenate([zero, v["ln_b"].reshape(-1, D)]))
    for f, name in (("a", "ffa"), ("b", "ffb")):
        w = v[name + "_w_in"].reshape(DEPTH, D, 2, FT, P).transpose(0, 1, 3, 2, 4)
        arrays["ff_in_" + f] = blocks(w.reshape(DEPTH, D, 2 * FF), FT, 256)
        arrays["ff_out_" + f] = blocks(v[name + "_w_out"], 4, 256)
    w = v["mix_w_in"]
    u, q, k, vv, r, gd = (w[..., a:b] for a, b in ((0, 512), (512, 768), (768, 1024), (1024, 1536),
                                                  (1536, 2048), (2048, 2080)))
    order = np.concatenate([gd, r[..., :96], u[..., :P], k, q, vv, u[..., P:], r[..., :3 * P]], axis=-1)
    full = blocks(order, IN_BLOCKS - 1, 256).transpose(0, 2, 1, 3).reshape(DEPTH, P, -1)
    arrays["mix_in"] = np.ascontiguousarray(np.concatenate([full, blocks(r[..., 3 * P:], 1, P)[:, 0]], axis=-1))
    arrays["mix_out"] = blocks(v["mix_w_out"], 4, 256)
    arrays["pool_w"] = np.ascontiguousarray(v["pool_w"].transpose(0, 2, 1, 3))
    gu = np.zeros((DEPTH, 33, TOK), f32)
    gu[:, 0:16, 0:256], gu[:, 16:32, 256:] = v["gate_up_f"], v["gate_up_b"]
    gu[:, 32, 0:256], gu[:, 32, 256:] = v["gate_bias_f"], v["gate_bias_b"]
    arrays["gate_up"] = gu
    cols = np.stack([v["pool_scale"].reshape(DEPTH, 4, P), v["gla_norm_g"].reshape(DEPTH, 4, P)], axis=1)
    arrays["cols"] = np.ascontiguousarray(cols.transpose(3, 0, 1, 2))

    omega = 1.0 / (10000.0 ** (np.arange(256, dtype=f32) / f32(256)))

    def enc(n):
        a = np.arange(n, dtype=f32)[:, None] * omega.astype(f32)
        return feature_major(np.concatenate([np.sin(a), np.cos(a)], axis=-1).astype(f32))

    arrays["pos_r"], arrays["pos_c"] = enc(4), enc(64)
    arrays["ident"] = np.eye(P, dtype=f32)
    arrays["fold"] = np.concatenate([np.eye(2, dtype=f32)] * 2)
    arrays["ones"] = np.full((P, P), 1.0 / D, f32)
    j, i = np.arange(P)[:, None], np.arange(P)[None, :]
    same = j // CHUNK == i // CHUNK
    tri = np.stack([same & (j <= i), same & (j >= i), same & (j > i), same & (j < i)], axis=1)
    arrays["tri"] = np.ascontiguousarray(tri.astype(f32) / f32(16.0))
    t = np.arange(LAT)
    count = np.stack([np.minimum(t + w - 1 - w // 2, LAT - 1) - np.maximum(t - w // 2, 0) + 1 for w in WINDOWS])
    arrays["cinv"] = np.ascontiguousarray(np.broadcast_to(f32(1.0) / count.astype(f32), (P, 4, LAT)))

    nc = bacc.Bacc("TRN2", target_bir_lowering=False, num_devices=1)
    io = {n: nc.dram_tensor("in_" + n, a.shape, mybir.dt.from_np(a.dtype), kind="ExternalInput").ap()
          for n, a in arrays.items()}
    io["out"] = nc.dram_tensor("out", (P, KT, LAT), F32, kind="ExternalOutput").ap()
    build(nc, io)
    got = run(nc, [{"in_" + n: a for n, a in arrays.items()}], core_ids=[0])
    out = np.asarray(got.results[0]["out"])
    return np.ascontiguousarray(out.transpose(2, 1, 0).reshape(1, LAT, D))
```

```python
from contextlib import ExitStack

import concourse.bass as bass
from concourse import mybir

F32 = mybir.dt.float32
F32R = mybir.dt.float32r
U8 = mybir.dt.uint8
ALU = mybir.AluOpType
ACT = mybir.ActivationFunctionType
ds = bass.ds

P = 128
DEPTH = 2
D = 1024
KT = D // P
LAT = 256
TOK = 512
FF = 2816
FT = FF // P
CHUNK = 64
N_MOD = 9
FULLS = DEPTH * N_MOD * KT // 2
HALVES = 2 * FULLS
WB = KT * 2 * P
START_BLOCKS = 2 * KT // 2
START_SLOTS = 5
EPS = 1e-6
ALPHA = (2.0 * DEPTH) ** 0.25
KPARTS = [(0, 8), (8, 16), (16, FT)]
PIECES = ((0, 1), (1, 1), (2, 2), (4, 2), (6, 2))
WINDOWS = (2, 4, 8, 16)
PAD = 8
UPW = LAT + 2 * PAD
IN_BLOCKS = 9
N_CH = TOK // CHUNK
CHUNK_ORDER = ((4, 5, 6, 7, 0, 1, 2, 3), (7, 6, 5, 4, 3, 2, 1, 0))


class Stage:

    def __init__(self, run, totals, sems, scratch=None, w=0, shift=0, scale=0, last=False):
        self.run, self.totals, self.sems = run, totals, sems
        self.q, self.scratch, self.w, self.shift, self.scale, self.last = run, scratch, w, shift, scale, last

    def sig(self, name):
        return self.sems[name]

    def at(self, name, value):
        return self.sems[name], self.run * self.totals[name] + value


class Phase:

    def __init__(self, f, l, n, a, lins):
        self.f, self.l = f, l
        self.n, self.a = n, a
        self.lin, self.ln = lins
        self.w = LAT if l == DEPTH - 1 and f == "b" else TOK
        self.gate = l * N_MOD + {"a": 2, "mix": 5, "b": 8}[f]
        self.gate_scale = 1.0 if f == "mix" else 0.5


def build(nc, io):
    with ExitStack() as ctx:
        arena = ctx.enter_context(nc.sbuf_tensor("arena", [P, 212800 // 4], F32))
        base = 16512
        at = [base]

        def sb(name, shape, dt, offset=None):
            size = 4
            for s in shape[1:]:
                size *= s
            if dt == U8:
                size //= 4
            size = -(-size // 32) * 32
            if offset is None:
                offset = at[0]
                at[0] += size
                assert at[0] <= 229344, at[0]
            return nc.alloc_sbuf_tensor_at(name, shape, dt, offset=offset)

        def sem(name):
            return ctx.enter_context(nc.semaphore(name))

        H = sb("H", [P, KT, TOK], F32)
        x_off = at[0]
        XH = sb("XH", [P, KT, TOK], F32R)
        XL = sb("XL", [P, KT, TOK], F32R)
        a_off = at[0]
        AH = sb("AH", [P, FT, TOK], F32R)
        AL = sb("AL", [P, FT, TOK], F32R)
        a_end = at[0]
        RAW = [sb(f"RAW{i}", [P, WB], F32) for i in range(2)]
        WH = [sb(f"WH{i}", [P, WB], F32R) for i in range(2)]
        WL = [sb(f"WL{i}", [P, WB], F32R) for i in range(2)]
        SRAW = sb("SRAW", [P, D], F32)
        SWH = sb("SWH", [P, D], F32R)
        SWL = sb("SWL", [P, D], F32R)
        SG = sb("SG", [P, TOK], F32)
        AF = sb("AF", [P, TOK], F32)
        MODS = sb("MODS", [P, 2 * FULLS, 2], F32)
        BADA = sb("BADA", [P, 2 * FULLS], F32)
        LNG = sb("LNG", [P, 1 + 3 * DEPTH, KT], F32)
        LNB = sb("LNB", [P, 1 + 3 * DEPTH, KT], F32)
        CA = sb("CA", [P, KT, 2], F32)
        CB = sb("CB", [P, KT, 2], F32)
        CHA = sb("CHA", [P, KT, 2], F32)
        CHB = sb("CHB", [P, KT, 2], F32)
        CG = sb("CG", [P, KT, 2], F32)
        COND = sb("COND", [P, KT, 2], F32)
        CSIL = sb("CSIL", [P, KT, 2], F32)
        S4 = sb("S4", [P, KT * 4 + P], F32R)
        ROWS = sb("ROWS", [4, 2 * P], F32)
        FOLD = sb("FOLD", [4, 2], F32)
        TRI = sb("TRI", [P, 4, P], F32)
        IDENT = sb("IDENT", [P, P], F32)
        ONES = sb("ONES", [P, P], F32)
        MASK = sb("MASK", [P, 2, P], U8)
        COLS = sb("COLS", [P, DEPTH, 2, 4], F32)
        EPSC = sb("EPSC", [P, 8], F32)

        off = [a_off]

        def over(name, shape, dt=F32, offset=None):
            size = 4
            for s in shape[1:]:
                size *= s
            if offset is None:
                offset = off[0]
                off[0] += -(-size // 32) * 32
                assert off[0] <= a_end, (name, off[0] - a_end)
            return sb(name, shape, dt, offset)

        up_off = off[0]
        UP = over("UP", [P, 4, 2, UPW])
        pool_off = off[0]
        PB = over("PB", [P, 2, UPW])
        PC = over("PC", [P, 2, UPW])
        CINV = over("CINV", [P, 4, LAT])
        AT = over("AT", [P, 4, TOK], offset=pool_off)
        assert pool_off + 4 * 4 * TOK <= off[0]
        PW = over("PW", [P, 4, P])
        GU = over("GU", [33, TOK])
        GD = over("GD", [33, TOK])
        kq_off = off[0]
        KTT = over("KTT", [P, 2, TOK])
        QTT = over("QTT", [P, 2, TOK])
        RT = over("RT", [P, 4, TOK], offset=kq_off)
        KN = over("KN", [P, 4, 256])
        vn_off = off[0]
        VN = over("VN", [P, 4, TOK])
        la_off = off[0]
        LA = over("LA", [P, 4, TOK])
        KE = over("KE", [P, 4, TOK], offset=la_off)
        SQH = over("SQH", [P, 4, TOK], offset=la_off)
        QF = [over(f"QF{d}", [P, 2, TOK]) for d in range(2)]
        KF = [over(f"KF{d}", [P, 2, TOK]) for d in range(2)]
        et_off = off[0]
        ET = [over(f"ET{i}", [P, TOK]) for i in range(2)]
        TFB = [over(f"TFB{i}", [P, TOK], offset=et_off + 2048 * i) for i in range(2)]
        SS = [over(f"SS{d}", [P, 7, 2, P]) for d in range(2)]
        DEC = over("DEC", [P, 2, 2, N_CH])
        ln_sq, ln_acc = {}, {}
        for kind, o in (("x", x_off + KT * TOK * 4), ("a", vn_off)):
            ln_sq[kind] = [over(f"LSQ{kind}{i}", [P, TOK], offset=o + 2048 * i) for i in range(2)]
            ln_acc[kind] = [over(f"LAC{kind}{i}", [P, TOK], offset=o + 4096 + 2048 * i) for i in range(2)]
        MU = over("MU", [P, TOK], offset=a_off)
        RS = over("RS", [P, TOK], offset=a_off + 2048)
        M = [over(f"M{i}", [P, 2, TOK], offset=a_off + 4096 + 4096 * i) for i in range(2)]
        START = [over(f"START{i}", [P, WB], offset=vn_off + 8192 + 4 * WB * i) for i in range(START_SLOTS)]
        assert vn_off + 8192 + 4 * WB * START_SLOTS <= a_end
        POSR = over("POSR", [P, 4, 4], offset=a_off + 16384)
        POSC = over("POSC", [P, 4, 64], offset=a_off + 16384 + 64)

        BANK = [ctx.enter_context(nc.psum_tensor(f"bank{i}", [P, TOK], F32)) for i in range(8)]
        PAIR = [BANK[0:2], BANK[2:4]]
        B_ROWS, B_COLS, B_SC = BANK[4], BANK[5], BANK[6:8]
        B_MS = BANK[4:6]

        ln_totals = dict(half=4, z=12, sq=8, added=8, stats=2, mu=1, var=1, ln=1, std=1, zc=3, zn=5, mlow=5, mfull=5,
                         xh=5, xl=5, h=1)
        ffn_totals = dict(sg=FT, af=FT, ah=FT)
        mix_totals = dict(aux_in=48, pads=1, gd=1, up=2, u12=1, kv=2, v_in=2, rt=4, gp=4, et=16, et_used=16,
                          knp=2, kn=2, bp=4, enp=4, u=14, state=14, pooled=4, pm=4, ym=4, xh=8, xl=8,
                          sc=8, cp=8, at=4, o=4, osq=4, ms=4, ln=4, std=4, yg=4, yh=4)
        stage_sems = [{s: sem(f"{k}_{s}") for s in t}
                      for k, t in (("ln", ln_totals), ("ffn", ffn_totals), ("mix", mix_totals))]

        def stage(kind, run, **more):
            sems, totals = stage_sems[kind], (ln_totals, ffn_totals, mix_totals)[kind]
            return Stage(run, totals, sems, **more)

        cond_in = sem("cond_in")
        consts_in = sem("consts_in")
        x_in = sem("x_in")
        raw_full = [sem(f"raw_full{i}") for i in range(2)]
        hi_done = sem("hi_done")
        lo_done = sem("lo_done")
        block_done = sem("block_done")
        pair_free = [sem(f"pair_free{i}") for i in range(2)]
        side_full = sem("side_full")
        side_hi = sem("side_hi")
        side_lo = sem("side_lo")
        side_done = sem("side_done")
        start_full = [sem(f"start_full{i}") for i in range(START_SLOTS)]
        rows_ready = sem("rows_ready")
        rows_out = sem("rows_out")
        cols_ready = sem("cols_ready")
        mods_done = sem("mods_done")
        sil_ready = sem("sil_ready")
        s4_hi = sem("s4_hi")
        s4_ready = sem("s4_ready")
        s4_tail = sem("s4_tail")
        eps_set = sem("eps_set")
        mask_ready = sem("mask_ready")
        dve_chain = sem("dve_chain")
        act_chain = sem("act_chain")
        out_done = sem("out_done")

        def new_ln(scratch, q, width, shift, scale, last=False):
            return stage(0, q, scratch=scratch, w=width, shift=shift, scale=scale, last=last)

        n, a, f_index = 0, 0, 0
        lns = [new_ln("a", 0, TOK, 0, 1)]
        phases = []
        for l in range(DEPTH):
            last = l == DEPTH - 1
            for f in ("a", "mix", "b"):
                m = l * N_MOD
                shift = m + {"a": 3, "mix": 6, "b": 9}[f]
                q = 1 + 3 * l + ("a", "mix", "b").index(f)
                p = Phase(f, l, n, a, lins=(lns[-1], new_ln("a" if f == "mix" else "x", q,
                                                            LAT if last and f != "a" else TOK,
                                                            shift, shift + 1, last and f == "b")))
                lns.append(p.ln)
                if f == "mix":
                    p.sides = [0] + [2] * (6 if last else 7) + [0] * (3 if last else 2)
                    p.nt = 2 if last else 4
                    p.s = stage(2, l)
                    n, a = n + IN_BLOCKS + 4, a + sum(p.sides)
                else:
                    p.G = FT * f_index
                    sided = not (last and f == "b")
                    p.loops = [(0, 1, sided), (1, 11, sided)]
                    p.out_sides = 6 * sided
                    p.a_out = a + 2 * sum((e - b) * s for b, e, s in p.loops)
                    p.s = stage(1, f_index)
                    f_index += 1
                    p.lead = 1 if p.w == TOK else 2
                    n, a = n + FT + 12, p.a_out + 2 * p.out_sides
                phases.append(p)
        H0 = 2 * START_BLOCKS
        F0 = START_BLOCKS
        assert a == HALVES - H0
        N_BLOCKS = n

        def run_turns(engine, first, end, turn_of):
            if end - first == 1:
                turn_of(first)
            else:
                with engine.Fori(first, end) as i:
                    turn_of(i)

        def mods_ready(engine, m):
            engine.wait_ge(mods_done, (m + 1) * KT // 2)

        def mod(m):
            return MODS[:, m * KT:(m + 1) * KT, :]

        def by_tile(s4):
            return s4[:, 0:KT * 4].rearrange("p (k c) -> p k c", c=4)

        def turn(k):
            return k // 2

        def wout_loops(p):
            return [(0, 1), (1, 2)] if p.n + FT + 12 == N_BLOCKS else [(0, 2)]

        block = ctx.enter_context(nc.Block())

        @block.sync
        def _(sp):
            def load_main(k, slot, src, size=WB):
                if not (isinstance(k, int) and k < 2):
                    sp.wait_ge(lo_done, k - 1)
                sp.dma_start(RAW[slot][:, 0:size], src).then_inc(raw_full[slot], 16)

            def load_side(k):
                sp.wait_ge(side_lo, k + 1)
                sp.dma_start(SRAW[:, :], io["w_ada"][ds(k + H0, 1), :, :]
                             .rearrange("h p n -> p (h n)")).then_inc(side_full, 16)

            def load_start(b):
                if b >= START_SLOTS:
                    sp.wait_ge(rows_ready, b - START_SLOTS + 1)
                sp.dma_start(START[b % START_SLOTS][:, :].rearrange("p (h n) -> p h n", h=2),
                             io["w_ada"][2 * b:2 * b + 2, :, :].rearrange("h p n -> p h n")
                             ).then_inc(start_full[b % START_SLOTS], 16)

            sp.dma_start(COND[:, :, :], io["cond"]).then_inc(cond_in, 16)
            load_start(0)
            load_start(1)
            sp.dma_start(H[:, :, :], io["x"]).then_inc(x_in, 16)
            for dst, name in ((IDENT[:, :], "ident"), (BADA[:, :], "b_ada"), (LNG[:, :, :], "ln_g"),
                              (LNB[:, :, :], "ln_b"), (ONES[:, :], "ones"), (POSR[:, :, :], "pos_r"),
                              (POSC[:, :, :], "pos_c"), (TRI[:, :, :], "tri"),
                              (COLS[:, :, :, :], "cols"), (FOLD[:, :], "fold")):
                sp.dma_start(dst, io[name]).then_inc(consts_in, 16)
            for b in range(2, START_BLOCKS):
                load_start(b)

            def ffn(p):
                w_in, w_out = io["ff_in_" + p.f], io["ff_out_" + p.f]
                for first, end, side in p.loops:
                    def two_blocks(i):
                        for b in range(2):
                            load_main(p.n + b + 2 * i, (p.n + b) % 2,
                                      w_in[p.l, ds(2 * i + b, 1), :, :].rearrange("j p n -> p (j n)"))
                            if side:
                                load_side(p.a + b + 2 * i)

                    run_turns(sp, first, end, two_blocks)
                with sp.Fori(0, 2) as i:
                    for b in range(6):
                        lo, hi = KPARTS[b % 3]
                        load_main(p.n + FT + b + 6 * i, (p.n + FT + b) % 2,
                                  w_out[p.l, ds(2 * i + b // 3, 1), :, lo * 256:hi * 256]
                                  .rearrange("j p n -> p (j n)"), (hi - lo) * 256)
                        if b < p.out_sides:
                            load_side(p.a_out + b + p.out_sides * i)

            def mixer(p):
                def load(b):
                    if b < IN_BLOCKS:
                        size = WB if b < IN_BLOCKS - 1 else WB // 2
                        load_main(p.n + b, (p.n + b) % 2, io["mix_in"][p.l, :, b * WB:b * WB + size], size)
                    else:
                        load_main(p.n + b, (p.n + b) % 2, io["mix_out"][p.l, b - IN_BLOCKS])

                k = p.a
                load(0)
                for b in range(IN_BLOCKS):
                    load(b + 1)
                    for _ in range(p.sides[b]):
                        load_side(k)
                        k += 1
                    if b == 1:
                        sp.wait_ge(*p.lin.at("xl", 5))
                        sp.dma_start(GU[:, :], io["gate_up"][p.l]).then_inc(p.s.sig("aux_in"), 16)
                        sp.dma_start(CINV[:, :, :], io["cinv"]).then_inc(p.s.sig("aux_in"), 16)
                        sp.dma_start(PW[:, :, :], io["pool_w"][p.l]).then_inc(p.s.sig("aux_in"), 16)
                for b in range(IN_BLOCKS + 1, IN_BLOCKS + 4):
                    load(b)

            for p in phases:
                (mixer if p.f == "mix" else ffn)(p)
            for q, (t, m) in enumerate(PIECES):
                sp.wait_ge(*lns[-1].at("mfull", q + 1))
                sp.wait_ge(*lns[-1].at("mlow", q + 1))
                sp.dma_start(io["out"][:, t:t + m, :], M[q % 2][:, 0:m, 0:LAT]).then_inc(out_done, 16)
                sp.wait_ge(out_done, 16 * (q + 1))

        @block.scalar
        def _(act):
            links = [0]

            def link(ins):
                links[0] += 1
                ins.then_inc(act_chain, 1)
                act.wait_ge(act_chain, links[0])

            def split_hi(k, t, slot):
                act.wait_ge(raw_full[slot], 16 * t + 16)
                if not (isinstance(k, int) and k < 2):
                    act.wait_ge(block_done, k - 1)
                act.copy(WH[slot][:, :], RAW[slot][:, :]).then_inc(hi_done, 1)

            def side_high(k):
                act.wait_ge(side_full, 16 * k + 16)
                if not (isinstance(k, int) and k == 0):
                    act.wait_ge(side_done, k)
                act.copy(SWH[:, :], SRAW[:, :]).then_inc(side_hi, 1)

            def rows_evac(g):
                act.wait_ge(side_done, 2 * g + 2)
                act.wait_ge(cols_ready, F0 + g)
                act.copy(ROWS[:, :], B_ROWS[0:4, 0:2 * P]).then_inc(rows_out, 1)

            def square(ln, t, par):
                act.wait_ge(*ln.at("z", t + 5))
                act.wait_ge(*ln.at("added", t + 1))
                act.activation(ln_sq[ln.scratch][par][:, 0:ln.w],
                               H[:, ds(t, 1), 0:ln.w].rearrange("p a n -> p (a n)"),
                               ACT.Square).then_inc(ln.sig("sq"), 1)

            def layernorm(ln):
                w = ln.w
                act.preload_act_table_set("natural_log_exp_and_others")
                act.wait_ge(*ln.at("stats", 1))
                act.copy(MU[:, 0:w], B_SC[0][:, 0:w]).then_inc(ln.sig("mu"), 1)
                act.wait_ge(*ln.at("var", 1))
                act.activation(RS[:, 0:w], RS[:, 0:w], ACT.Ln).then_inc(ln.sig("ln"), 1)
                act.wait_ge(*ln.at("ln", 1))
                act.activation(RS[:, 0:w], RS[:, 0:w], ACT.Exp, scale=-0.5).then_inc(ln.sig("std"), 1)
                for q, (t, m) in enumerate(PIECES):
                    act.wait_ge(*ln.at("zn", q + 1))
                    if q >= 2 and ln.last:
                        act.wait_ge(out_done, 16 * (q - 1))
                    elif q >= 2:
                        act.wait_ge(*ln.at("xl", q - 1))
                    c, s = slice(w // 2, w), w // TOK
                    for j in range(m):
                        ins = act.activation(M[q % 2][:, j, c], H[:, t + j, c], ACT.Identity,
                                             bias=CB[:, t + j, s:s + 1], scale=CA[:, t + j, s:s + 1])
                    ins.then_inc(ln.sig("mfull"), 1)
                    if not ln.last:
                        act.wait_ge(*ln.at("mfull", q + 1))
                        act.wait_ge(*ln.at("mlow", q + 1))
                        act.copy(XH[:, t:t + m, 0:w], M[q % 2][:, 0:m, 0:w]).then_inc(ln.sig("xh"), 1)

            act.wait_ge(cond_in, 16)
            act.activation(CSIL[:, :, :], COND[:, :, :], ACT.Silu).then_inc(sil_ready, 1)
            act.wait_ge(sil_ready, 1)
            act.copy(by_tile(S4)[:, :, 0:2], CSIL[:, :, :]).then_inc(s4_hi, 1)

            def start_rows(b):
                act.wait_ge(rows_ready, b + 1)
                if b:
                    act.wait_ge(cols_ready, b)
                act.copy(ROWS[0:2, :], BANK[b % 2][0:2, 0:2 * P]).then_inc(rows_out, 1)

            for b in range(START_BLOCKS):
                start_rows(b)
                for t in range(2 * b - 4, 2 * b - 2):
                    if 0 <= t < KT:
                        square(lns[0], t, t % 2)
            split_hi(0, 0, 0)
            layernorm(lns[0])

            def ffn(p):
                w = p.w
                if p.lead == 2:
                    split_hi(p.n + 1, turn(p.n + 1), (p.n + 1) % 2)
                for first, end, side in p.loops:
                    def two_blocks(i):
                        act.preload_act_table_set("silu_and_others")
                        for b in range(2):
                            k = p.n + b
                            if side:
                                side_high(p.a + b + 2 * i)
                            if p.lead == 1:
                                split_hi(k + 1 + 2 * i, turn(k + 1) + i, (k + 1) % 2)
                            if side and b:
                                rows_evac(turn(p.a) + i)
                            act.wait_ge(block_done, k + 1 + 2 * i)
                            act.activation(SG[:, 0:w], PAIR[b][0][:, 0:w], ACT.Silu).then_inc(p.s.sig("sg"), 1)
                            if p.lead == 2:
                                split_hi(k + 2 + 2 * i, turn(k + 2) + i, k % 2)
                            act.wait_ge(*p.s.at("af", b + 1 + 2 * i))
                            act.copy(AH[:, ds(2 * i + b, 1), 0:w].rearrange("p a n -> p (a n)"),
                                     AF[:, 0:w]).then_inc(p.s.sig("ah"), 1)

                    run_turns(act, first, end, two_blocks)
                for first, end in wout_loops(p):
                    with act.Fori(first, end) as i:
                        for b in range(6):
                            k = p.n + FT + b
                            if b < p.out_sides:
                                side_high(p.a_out + b + p.out_sides * i)
                            if not (first == 1 and b + p.lead > 5):
                                split_hi(k + p.lead + 6 * i, turn(k + p.lead) + 3 * i, (k + p.lead) % 2)
                            if b < p.out_sides and b % 2:
                                rows_evac(turn(p.a_out + b) + turn(p.out_sides) * i)
                            if b % 3 == 2:
                                for h in range(2):
                                    square(p.ln, 4 * i + 2 * (b // 3) + h, h)
                layernorm(p.ln)

            def mixer(p):
                s = p.s
                wq = p.nt * P
                ets = [0]
                side = [p.a]

                def step(b):
                    k = p.n + b + 1
                    if p.sides[b]:
                        side_high(side[0] + 1)
                    split_hi(k, turn(k), k % 2)
                    if p.sides[b + 1]:
                        side_high(side[0] + p.sides[b])
                    if p.sides[b]:
                        rows_evac(turn(side[0]))
                        side[0] += 2
                    act.wait_ge(block_done, p.n + b + 1)

                def exp_buffer():
                    if ets[0] >= 2:
                        act.wait_ge(*s.at("et_used", ets[0] - 1))
                    ets[0] += 1
                    return ET[(ets[0] - 1) % 2]

                def gates(t):
                    act.wait_ge(*s.at("gp", t + 1))
                    e = exp_buffer()
                    link(act.activation(e[:, :], B_SC[t % 2][:, :], ACT.Abs))
                    link(act.activation(e[:, :], e[:, :], ACT.Exp, scale=-1.0))
                    act.activation(e[:, :], e[:, :], ACT.Ln, bias=1.0).then_inc(s.sig("et"), 1)

                def decays(j):
                    act.wait_ge(*s.at("bp", j + 1))
                    act.activation(exp_buffer()[:, :], B_SC[j % 2][:, :], ACT.Exp).then_inc(s.sig("et"), 1)
                    act.activation(exp_buffer()[:, :], B_SC[j % 2][:, :], ACT.Exp, scale=-1.0).then_inc(s.sig("et"), 1)

                def end_decays(t):
                    act.wait_ge(*s.at("enp", t + 1))
                    act.activation(exp_buffer()[:, :], B_SC[t % 2][:, :], ACT.Exp).then_inc(s.sig("et"), 1)

                def padded(t):
                    return UP[:, t, 0:wq // LAT, PAD:PAD + LAT]

                def by_stream(bank):
                    return bank[:, 0:wq].rearrange("p (s n) -> p s n", n=LAT)

                step(0)
                act.wait_ge(*p.lin.at("xl", 5))
                act.copy(GD[0:32, :], PAIR[0][0][0:32, :]).then_inc(s.sig("gd"), 1)
                act.wait_ge(*s.at("pads", 1))
                act.copy(padded(0), by_stream(PAIR[0][1])).then_inc(s.sig("up"), 1)
                step(1)
                act.copy(KTT[:, 0, :], PAIR[1][0][:, :])
                act.copy(KTT[:, 1, :], PAIR[1][1][:, :]).then_inc(s.sig("kv"), 1)
                act.preload_act_table_set("natural_log_exp_and_others")
                gates(0)
                gates(1)
                step(2)
                act.activation(QTT[:, 0, 0:wq], PAIR[0][0][:, 0:wq], ACT.Copy, scale=0.125)
                act.activation(QTT[:, 1, 0:wq], PAIR[0][1][:, 0:wq], ACT.Copy, scale=0.125).then_inc(s.sig("kv"), 1)
                gates(2)
                gates(3)
                step(3)
                for t in range(2):
                    act.wait_ge(*s.at("knp", t + 1))
                    act.copy(KN[:, 2 * t:2 * t + 2, :],
                             B_SC[t][:, :].rearrange("p (t n) -> p t n", n=256)).then_inc(s.sig("kn"), 1)
                step(4)
                decays(0)
                decays(1)
                step(5)
                decays(2)
                decays(3)
                step(6)
                act.copy(padded(3), by_stream(PAIR[0][0])).then_inc(s.sig("up"), 1)
                act.wait_ge(*s.at("et_used", 12))
                act.copy(RT[:, 0, 0:wq], PAIR[0][1][:, 0:wq]).then_inc(s.sig("rt"), 1)
                end_decays(0)
                end_decays(1)
                step(7)
                act.copy(RT[:, 1, 0:wq], PAIR[1][0][:, 0:wq])
                act.copy(RT[:, 2, 0:wq], PAIR[1][1][:, 0:wq]).then_inc(s.sig("rt"), 1)
                end_decays(2)
                end_decays(3)
                step(8)
                act.copy(RT[:, 3, 0:wq], PAIR[0][0][:, 0:wq]).then_inc(s.sig("rt"), 1)
                for t in range(4):
                    act.wait_ge(*s.at("pm", t + 1))
                    flat = UP[:, t, :, :].rearrange("p s n -> p (s n)")[:, 0:wq]
                    act.activation(flat, PAIR[(9 + t // 2) % 2][t % 2][:, 0:wq], ACT.Copy,
                                   scale=COLS[:, p.l, 0, t:t + 1]).then_inc(s.sig("ym"), 1)
                    act.wait_ge(*s.at("ym", t + 1))
                    act.copy(XH[:, t, 0:wq], flat).then_inc(s.sig("xh"), 1)
                act.wait_ge(*s.at("rt", 3))
                act.activation(RT[:, :, 0:wq], RT[:, :, 0:wq], ACT.Silu).then_inc(s.sig("rt"), 1)
                act.preload_act_table_set("natural_log_exp_and_others")

                def squares(h):
                    act.wait_ge(*s.at("o", h + 1))
                    act.activation(SQH[:, h, 0:wq], PAIR[(11 + h // 2) % 2][h % 2][:, 0:wq],
                                   ACT.Square).then_inc(s.sig("osq"), 1)

                def inverse_roots(h):
                    act.wait_ge(*s.at("ms", h + 1))
                    act.activation(SQH[:, h, 0:wq], B_MS[h % 2][:, 0:wq], ACT.Ln, bias=EPSC[:, 0:1],
                                   scale=float(KT)).then_inc(s.sig("ln"), 1)
                    act.wait_ge(*s.at("ln", h + 1))
                    act.activation(SQH[:, h, 0:wq], SQH[:, h, 0:wq], ACT.Exp, scale=-0.5).then_inc(s.sig("std"), 1)

                def high(h):
                    act.wait_ge(*s.at("yh", h + 1))
                    act.copy(XH[:, 4 + h, 0:wq], SQH[:, h, 0:wq]).then_inc(s.sig("xh"), 1)

                for h in range(6):
                    if h < 4:
                        squares(h)
                    if 1 <= h < 5:
                        inverse_roots(h - 1)
                    if h >= 2:
                        high(h - 2)
                for b in range(4):
                    k = p.n + IN_BLOCKS + b
                    split_hi(k + 1, turn(k + 1), (k + 1) % 2)
                    for h in range(2):
                        square(p.ln, 2 * b + h, h)
                layernorm(p.ln)

            for p in phases:
                (mixer if p.f == "mix" else ffn)(p)

        @block.vector
        def _(dve):
            links = [0]

            def link(ins):
                links[0] += 1
                ins.then_inc(dve_chain, 1)
                dve.wait_ge(dve_chain, links[0])

            def split_lo(k, slot):
                dve.wait_ge(hi_done, k + 1)
                dve.tensor_tensor(WL[slot][:, :], RAW[slot][:, :], WH[slot][:, :].bitcast(F32),
                                  ALU.subtract).then_inc(lo_done, 1)

            def side_low(k):
                dve.wait_ge(side_hi, k + 1)
                dve.tensor_tensor(SWL[:, :], SRAW[:, :], SWH[:, :].bitcast(F32),
                                  ALU.subtract).then_inc(side_lo, 1)

            def fold(f):
                dve.wait_ge(cols_ready, f + 1)
                dve.tensor_tensor(MODS[:, ds(2 * f, 2), :], B_COLS[:, 0:4].rearrange("p (a c) -> p a c", c=2),
                                  BADA[:, ds(2 * f, 2)].unsqueeze(2).broadcast_to([P, 2, 2]),
                                  ALU.add).then_inc(mods_done, 1)

            def gates_ready(p):
                mods_ready(dve, p.gate)
                dve.tensor_scalar(CG[:, :, :], mod(p.gate), p.gate_scale, None, ALU.mult).then_inc(p.ln.sig("z"), 4)
                dve.wait_ge(*p.ln.at("z", 4))
                dve.wait_ge(*p.lin.at("h", 1))

            def residual(p, t, bank):
                for s in range(p.ln.w // LAT):
                    c = slice(s * LAT, s * LAT + LAT)
                    h = H[:, ds(t, 1), c].rearrange("p a n -> p (a n)")
                    g = CG[:, ds(t, 1), s:s + 1].rearrange("p a n -> p (a n)")
                    ins = dve.scalar_tensor_tensor(h, bank[:, c], g, h, op0=ALU.mult, op1=ALU.add)
                ins.then_inc(p.ln.sig("z"), 1)

            def layernorm(ln):
                w = ln.w
                g, b = (v[:, ln.q, :].unsqueeze(2).broadcast_to([P, KT, 2]) for v in (LNG, LNB))
                if ln.last:
                    dve.tensor_copy(CA[:, :, :], g)
                    link(dve.tensor_copy(CB[:, :, :], b))
                else:
                    mods_ready(dve, ln.scale)
                    dve.scalar_tensor_tensor(CA[:, :, :], mod(ln.scale), 1.0, g, op0=ALU.add, op1=ALU.mult)
                    link(dve.scalar_tensor_tensor(CB[:, :, :], mod(ln.scale), 1.0, b, op0=ALU.add, op1=ALU.mult))
                    dve.tensor_scalar(CHA[:, :, :], g, ALPHA, None, ALU.mult)
                    dve.tensor_scalar(CHB[:, :, :], b, ALPHA, None, ALU.mult)
                    link(dve.tensor_tensor(CB[:, :, :], CB[:, :, :], mod(ln.shift), ALU.add))
                dve.wait_ge(*ln.at("mu", 1))
                link(dve.tensor_tensor(RS[:, 0:w], MU[:, 0:w], MU[:, 0:w], ALU.mult))
                dve.wait_ge(*ln.at("stats", 2))
                dve.scalar_tensor_tensor(RS[:, 0:w], B_SC[1][:, 0:w], EPS, RS[:, 0:w], op0=ALU.add,
                                         op1=ALU.subtract).then_inc(ln.sig("var"), 1)

                def low(q):
                    t, m = PIECES[q]
                    dve.wait_ge(*ln.at("xh", q + 1))
                    dve.tensor_tensor(XL[:, t:t + m, 0:w], M[q % 2][:, 0:m, 0:w],
                                      XH[:, t:t + m, 0:w].bitcast(F32), ALU.subtract).then_inc(ln.sig("xl"), 1)

                z0 = H[:, 0:2, 0:w]
                link(dve.tensor_tensor(z0, z0, MU[:, 0:w].unsqueeze(1).broadcast_to([P, 2, w]), ALU.subtract))
                dve.wait_ge(*ln.at("std", 1))
                for q, (t, m) in enumerate(PIECES):
                    z = H[:, t:t + m, 0:w]
                    if t >= 2:
                        dve.wait_ge(*ln.at("zc", t // 2))
                    dve.tensor_tensor(z, z, RS[:, 0:w].unsqueeze(1).broadcast_to([P, m, w]),
                                      ALU.mult).then_inc(ln.sig("zn"), 1)
                    dve.wait_ge(*ln.at("zn", q + 1))
                    if q >= 2 and ln.last:
                        dve.wait_ge(out_done, 16 * (q - 1))
                    elif q >= 2:
                        dve.wait_ge(*ln.at("xl", q - 1))
                    c = slice(0, w // 2)
                    for j in range(m):
                        ins = dve.tensor_scalar(M[q % 2][:, j, c], H[:, t + j, c], CA[:, t + j, 0:1],
                                                CB[:, t + j, 0:1], ALU.mult, ALU.add)
                    ins.then_inc(ln.sig("mlow"), 1)
                    if q and not ln.last:
                        low(q - 1)
                if not ln.last:
                    low(len(PIECES) - 1)

            dve.memset(EPSC[:, 0:1], EPS).then_inc(eps_set, 1)
            for i, free in enumerate((side_lo, *pair_free)):
                dve.memset(EPSC[:, 1 + i:2 + i], 0.0).then_inc(free, 1)
            dve.memset(EPSC[:, 4:5], 0.0).then_inc(lns[0].sig("half"), 4)
            dve.memset(S4[:, KT * 4:].bitcast(F32), 0.0).then_inc(s4_tail, 1)
            dve.wait_ge(s4_hi, 1)
            dve.tensor_tensor(by_tile(S4)[:, :, 2:4], CSIL[:, :, :], by_tile(S4)[:, :, 0:2].bitcast(F32),
                              ALU.subtract).then_inc(s4_ready, 1)
            dve.wait_ge(x_in, 16)
            dve.wait_ge(consts_in, 10 * 16)
            dve.tensor_scalar(MASK[:, :, :], TRI[:, 0:2, :], 0.0, None, ALU.is_gt).then_inc(mask_ready, 1)
            for t in range(4):
                z = H[:, t, 0:LAT].rearrange("p (r c) -> p r c", c=64)
                dve.tensor_tensor(z, z, POSR[:, t, :].unsqueeze(2).broadcast_to([P, 4, 64]), ALU.add)
            for t in range(4):
                z = H[:, 4 + t, 0:LAT].rearrange("p (r c) -> p r c", c=64)
                ins = dve.tensor_tensor(z, z, POSC[:, t, :].unsqueeze(1).broadcast_to([P, 4, 64]), ALU.add)
            ins.then_inc(lns[0].sig("z"), 12)
            for b in range(START_BLOCKS):
                fold(b)
            split_lo(0, 0)
            layernorm(lns[0])

            def ffn(p):
                w = p.w
                if p.lead == 2:
                    split_lo(p.n + 1, (p.n + 1) % 2)
                for first, end, side in p.loops:
                    def two_blocks(i):
                        for b in range(2):
                            k = p.n + b
                            if side:
                                side_low(p.a + b + 2 * i)
                            if p.lead == 1:
                                split_lo(k + 1 + 2 * i, (k + 1) % 2)
                            dve.wait_ge(*p.s.at("sg", b + 1 + 2 * i))
                            dve.wait_ge(pair_free[1 - b], turn(p.G) + 1 + b + i)
                            dve.tensor_tensor(AF[:, 0:w], SG[:, 0:w], PAIR[b][1][:, 0:w],
                                              ALU.mult).then_inc(p.s.sig("af"), 1)
                            if p.lead == 2:
                                split_lo(k + 2 + 2 * i, k % 2)
                            dve.wait_ge(*p.s.at("ah", b + 1 + 2 * i))
                            ah = AH[:, ds(2 * i + b, 1), 0:w].rearrange("p a n -> p (a n)")
                            al = AL[:, ds(2 * i + b, 1), 0:w].rearrange("p a n -> p (a n)")
                            dve.tensor_tensor(al, AF[:, 0:w], ah.bitcast(F32),
                                              ALU.subtract).then_inc(pair_free[b], 1)
                            if side and b:
                                fold(turn(p.a) + F0 + i)

                    run_turns(dve, first, end, two_blocks)
                gates_ready(p)
                for first, end in wout_loops(p):
                    with dve.Fori(first, end) as i:
                        for b in range(6):
                            k = p.n + FT + b
                            if b < p.out_sides:
                                side_low(p.a_out + b + p.out_sides * i)
                            if not (first == 1 and b + p.lead > 5):
                                split_lo(k + p.lead + 6 * i, (k + p.lead) % 2)
                            if b % 3 == 2:
                                dve.wait_ge(*p.ln.at("half", 2 * i + b // 3 + 1))
                                residual(p, 4 * i + 2 * (b // 3), PAIR[b // 3][0])
                                dve.wait_ge(block_done, k + 1 + 6 * i)
                                residual(p, 4 * i + 2 * (b // 3) + 1, PAIR[b // 3][1])
                            if b < p.out_sides and b % 2:
                                fold(turn(p.a_out + b) + F0 + turn(p.out_sides) * i)
                layernorm(p.ln)

            def mixer(p):
                s = p.s
                wq, nt = p.nt * P, p.nt
                ns = wq // LAT
                side = [p.a]

                def step(b, between=()):
                    k = p.n + b + 1
                    if p.sides[b]:
                        side_low(side[0] + 1)
                    split_lo(k, k % 2)
                    for work, t in between:
                        work(t)
                    if p.sides[b + 1]:
                        side_low(side[0] + p.sides[b])
                    if p.sides[b]:
                        fold(turn(side[0]) + F0)
                        side[0] += 2
                    dve.wait_ge(block_done, p.n + b + 1)

                def log_gates(t):
                    dve.wait_ge(*s.at("et", t + 1))
                    dve.scalar_tensor_tensor(LA[:, t, :], B_SC[t % 2][:, :], 0.0, ET[t % 2][:, :],
                                             op0=ALU.min, op1=ALU.subtract).then_inc(s.sig("et_used"), 1)

                def scaled(j):
                    c, d = j // 2, j % 2
                    dve.wait_ge(*s.at("et", 4 + 2 * j + 1))
                    dve.wait_ge(*s.at("kv", 2))
                    dve.tensor_tensor(QF[d][:, c, 0:wq], QTT[:, c, 0:wq], ET[0][:, 0:wq], ALU.mult)
                    dve.tensor_copy(DEC[:, d, c, :], ET[0][:, (CHUNK - 1 if d == 0 else 0)::CHUNK]).then_inc(s.sig("et_used"), 1)
                    dve.wait_ge(*s.at("et", 4 + 2 * j + 2))
                    dve.tensor_tensor(KF[d][:, c, :], KTT[:, c, :], ET[1][:, :], ALU.mult).then_inc(s.sig("et_used"), 1)

                def end_keys(t):
                    dve.wait_ge(*s.at("et", 12 + t + 1))
                    dve.wait_ge(*s.at("kn", 2))
                    dve.tensor_tensor(KE[:, t, :].rearrange("p (d n) -> p d n", d=2),
                                      ET[t % 2][:, :].rearrange("p (d n) -> p d n", d=2),
                                      KN[:, t, :].unsqueeze(1).broadcast_to([P, 2, 256]),
                                      ALU.mult).then_inc(s.sig("et_used"), 1)

                def values(v):
                    for t in range(2):
                        ins = dve.tensor_copy(VN[:, 2 * t:2 * t + 2, 256 * v:256 * v + 256],
                                              PAIR[(3 + v) % 2][t][:, :].rearrange("p (t n) -> p t n", n=256))
                    ins.then_inc(s.sig("v_in"), 1)

                def pool(t):
                    if t:
                        dve.wait_ge(*s.at("pooled", t))
                    window = WINDOWS[t]
                    src, dst, v = UP[:, t, 0:ns, :], PB, 1
                    while v < window:
                        lo, hi = PAD - window // 2, PAD + LAT + window // 2 - 2 * v
                        link(dve.tensor_tensor(dst[:, 0:ns, lo:hi], src[:, :, lo:hi], src[:, :, lo + v:hi + v], ALU.add))
                        src, dst, v = dst[:, 0:ns, :], PC if dst is PB else PB, 2 * v
                    lo = PAD - window // 2
                    mean = dst[:, 0:ns, PAD:PAD + LAT]
                    link(dve.tensor_tensor(mean, src[:, :, lo:lo + LAT],
                                           CINV[:, t, :].unsqueeze(1).broadcast_to([P, ns, LAT]), ALU.mult))
                    u = UP[:, t, 0:ns, PAD:PAD + LAT]
                    dve.tensor_tensor(u, mean, u, ALU.subtract).then_inc(s.sig("pooled"), 1)

                dve.wait_ge(*p.lin.at("xl", 5))
                dve.memset(UP[:, :, :, 0:PAD], 0.0)
                dve.memset(UP[:, :, :, PAD + LAT:UPW], 0.0)
                dve.memset(GD[32:33, :], 1.0).then_inc(s.sig("pads"), 1)
                step(0)
                step(1)
                log_gates(0)
                log_gates(1)
                step(2)
                log_gates(2)
                log_gates(3)
                step(3)
                values(0)
                step(4)
                values(1)
                scaled(0)
                scaled(1)
                step(5)
                for t in range(2):
                    ins = dve.tensor_copy(UP[:, 1 + t, 0:ns, PAD:PAD + LAT],
                                          PAIR[1][t][:, 0:wq].rearrange("p (s n) -> p s n", n=LAT))
                ins.then_inc(s.sig("u12"), 1)
                scaled(2)
                scaled(3)
                dve.wait_ge(*s.at("aux_in", 48))
                dve.wait_ge(*s.at("up", 1))
                dve.wait_ge(*s.at("u12", 1))
                step(6, ((pool, 0), (pool, 1)))
                end_keys(0)
                end_keys(1)
                dve.wait_ge(*s.at("up", 2))
                step(7, ((pool, 2), (pool, 3)))
                end_keys(2)
                end_keys(3)
                dve.wait_ge(*s.at("et_used", 16))
                for d in range(2):
                    ins = dve.memset(TFB[d][:, :], 0.0)
                link(ins)
                for i in range(7):
                    for d in range(2):
                        dve.wait_ge(*s.at("u", 2 * i + d + 1))
                        if i:
                            dve.wait_ge(*s.at("state", 2 * (i - 1) + d + 1))
                        for c in range(2):
                            u = B_SC[d][:, c * P:(c + 1) * P]
                            if i == 0:
                                ins = dve.tensor_copy(SS[d][:, i, c, :], u)
                            else:
                                ch = CHUNK_ORDER[d][i]
                                ins = dve.scalar_tensor_tensor(SS[d][:, i, c, :], SS[d][:, i - 1, c, :],
                                                               DEC[:, d, c, ch:ch + 1], u,
                                                               op0=ALU.mult, op1=ALU.add)
                        ins.then_inc(s.sig("state"), 1)
                def masked(h):
                    if h:
                        dve.wait_ge(*s.at("at", h))
                    for d in range(2):
                        dve.wait_ge(*s.at("sc", 2 * h + d + 1))
                        dve.copy_predicated(TFB[d][:, 0:wq].rearrange("p (t n) -> p t n", n=P),
                                            MASK[:, d, :].unsqueeze(1).broadcast_to([P, nt, P]),
                                            B_SC[d][:, 0:wq].rearrange("p (t n) -> p t n", n=P)).then_inc(s.sig("cp"), 1)
                    dve.wait_ge(*s.at("cp", 2 * h + 2))
                    dve.tensor_tensor(AT[:, h, 0:wq], TFB[0][:, 0:wq], TFB[1][:, 0:wq], ALU.add).then_inc(s.sig("at"), 1)

                def normalise(h):
                    y = SQH[:, h, 0:wq]
                    dve.wait_ge(*s.at("std", h + 1))
                    link(dve.tensor_tensor(y, PAIR[(11 + h // 2) % 2][h % 2][:, 0:wq], y, ALU.mult))
                    dve.wait_ge(*s.at("rt", 4))
                    dve.scalar_tensor_tensor(y, y, COLS[:, p.l, 1, h:h + 1], RT[:, h, 0:wq],
                                             op0=ALU.mult, op1=ALU.mult).then_inc(s.sig("yh"), 1)

                def low(h):
                    dve.wait_ge(*s.at("xh", 4 + h + 1))
                    dve.tensor_tensor(XL[:, 4 + h, 0:wq], SQH[:, h, 0:wq], XH[:, 4 + h, 0:wq].bitcast(F32),
                                      ALU.subtract).then_inc(s.sig("xl"), 1)

                dve.wait_ge(mask_ready, 1)
                masked(0)
                step(8)
                masked(1)
                for t in range(4):
                    dve.wait_ge(*s.at("xh", t + 1))
                    flat = UP[:, t, :, :].rearrange("p s n -> p (s n)")[:, 0:wq]
                    dve.tensor_tensor(XL[:, t, 0:wq], flat, XH[:, t, 0:wq].bitcast(F32),
                                      ALU.subtract).then_inc(s.sig("xl"), 1)
                masked(2)
                normalise(0)
                masked(3)
                for h in range(1, 4):
                    normalise(h)
                    low(h - 1)
                low(3)
                gates_ready(p)
                for b in range(4):
                    k = p.n + IN_BLOCKS + b
                    split_lo(k + 1, (k + 1) % 2)
                    dve.wait_ge(*p.ln.at("half", b + 1))
                    residual(p, 2 * b, PAIR[b % 2][0])
                    dve.wait_ge(block_done, k + 1)
                    residual(p, 2 * b + 1, PAIR[b % 2][1])
                layernorm(p.ln)

            for p in phases:
                (mixer if p.f == "mix" else ffn)(p)

        @block.gpsimd
        def _(pool):
            def layernorm(ln):
                acc, w = ln_acc[ln.scratch], ln.w
                for a in acc:
                    pool.memset(a[:, :], 0.0).then_inc(ln.sig("added"), 1)
                with pool.Fori(0, 3) as i:
                    for b in range(2):
                        pool.wait_ge(*ln.at("z", 2 * i + b + 5))
                        pool.wait_ge(*ln.at("added", 2 * i + b + 2))
                        pool.tensor_tensor(acc[0][:, 0:w], acc[0][:, 0:w],
                                           H[:, ds(2 * i + b, 1), 0:w].rearrange("p a n -> p (a n)"), ALU.add)
                        pool.wait_ge(*ln.at("sq", 2 * i + b + 1))
                        pool.tensor_tensor(acc[1][:, 0:w], acc[1][:, 0:w], ln_sq[ln.scratch][b][:, 0:w],
                                           ALU.add).then_inc(ln.sig("added"), 1)
                pool.wait_ge(*ln.at("mu", 1))
                for q in range(1, 4):
                    z = H[:, 2 * q:2 * q + 2, 0:w]
                    pool.tensor_tensor(z, z, MU[:, 0:w].unsqueeze(1).broadcast_to([P, 2, w]),
                                       ALU.subtract).then_inc(ln.sig("zc"), 1)
                if ln.last:
                    return
                for q, (first, m) in enumerate(PIECES):
                    pool.wait_ge(*ln.at("mfull", q + 1))
                    pool.wait_ge(*ln.at("mlow", q + 1))
                    for t in range(first, first + m):
                        for s in range(w // LAT):
                            c = slice(s * LAT, s * LAT + LAT)
                            ins = pool.tensor_scalar(H[:, t, c], H[:, t, c], CHA[:, t, s:s + 1],
                                                     CHB[:, t, s:s + 1], ALU.mult, ALU.add)
                ins.then_inc(ln.sig("h"), 1)

            layernorm(lns[0])
            for p in phases:
                if p.f == "mix":
                    pool.wait_ge(*p.s.at("o", 4))
                else:
                    pool.wait_ge(block_done, p.n + FT)
                layernorm(p.ln)

        @block.tensor
        def _(pe):
            def three(out, wh, wl, xh, xl, start, stop):
                pe.matmul(out, wh, xh, start=start, stop=False)
                pe.matmul(out, wh, xl, start=False, stop=False)
                return pe.matmul(out, wl, xh, start=False, stop=stop)

            def columns(f, rows=4):
                pe.wait_ge(rows_out, f + 1)
                if not (isinstance(f, int) and f == 0):
                    pe.wait_ge(mods_done, f)
                for j in range(2):
                    ins = pe.matmul(B_COLS[:, 2 * j:2 * j + 2], ROWS[0:rows, j * P:(j + 1) * P], FOLD[0:rows, :],
                                    start=True, stop=True)
                ins.then_inc(cols_ready, 1)

            def side(g, half):
                pe.wait_ge(side_lo, 2 * g + half + 2)
                if half == 0:
                    pe.wait_ge(rows_out, F0 + g)
                for x, part in enumerate((SWH, SWL)):
                    for j in range(KT // 2):
                        r = 4 * (half * KT // 2 + j)
                        ins = pe.matmul(B_ROWS[:, 0:2 * P], S4[:, r:r + P], part[:, j * 2 * P:(j + 1) * 2 * P],
                                        start=(half == 0 and x == 0 and j == 0),
                                        stop=(half == 1 and x == 1 and j == KT // 2 - 1))
                ins.then_inc(side_done, 1)

            def stats_begin(ln):
                acc, w = ln_acc[ln.scratch], ln.w
                pe.wait_ge(*ln.at("added", 8))
                pe.matmul(B_SC[0][:, 0:w], ONES[:, :], acc[0][:, 0:w], start=True, stop=False)
                pe.matmul(B_SC[1][:, 0:w], ONES[:, :], acc[1][:, 0:w], start=True, stop=False)

            def stats_end(ln):
                w = ln.w
                for t in (6, 7):
                    pe.wait_ge(*ln.at("z", t + 5))
                    ins = pe.matmul(B_SC[0][:, 0:w], ONES[:, :], H[:, t, 0:w], start=False, stop=t == 7)
                    if t == 7:
                        ins.then_inc(ln.sig("stats"), 1)
                    pe.wait_ge(*ln.at("sq", t + 1))
                    ins = pe.matmul(B_SC[1][:, 0:w], ONES[:, :], ln_sq[ln.scratch][t - 6][:, 0:w],
                                    start=False, stop=t == 7)
                ins.then_inc(ln.sig("stats"), 1)

            pe.wait_ge(sil_ready, 1)
            for b in range(START_BLOCKS):
                pe.wait_ge(start_full[b % START_SLOTS], 16 * (b // START_SLOTS) + 16)
                if b >= 2:
                    pe.wait_ge(rows_out, b - 1)
                for k in range(KT):
                    ins = pe.matmul(BANK[b % 2][0:2, 0:2 * P], CSIL[:, k, :],
                                    START[b % START_SLOTS][:, k * 2 * P:(k + 1) * 2 * P],
                                    start=k == 0, stop=k == KT - 1)
                ins.then_inc(rows_ready, 1)
                if b == 1:
                    pe.wait_ge(consts_in, 10 * 16)
                if b:
                    columns(b - 1, 2)
            stats_begin(lns[0])
            columns(START_BLOCKS - 1, 2)
            pe.wait_ge(s4_ready, 1)
            pe.wait_ge(s4_tail, 1)
            stats_end(lns[0])

            def input_tile(p, k):
                for q, (t, m) in enumerate(PIECES):
                    if t == k:
                        pe.wait_ge(*p.lin.at("xl", q + 1))

            def products(by_row):
                if by_row:
                    return [(h, k) for k in range(KT) for h in range(2)]
                return [(h, k) for h in range(2) for k in range(KT)]

            def ffn(p):
                w = p.w
                for first, end, sided in p.loops:
                    def two_blocks(i):
                        for b in range(2):
                            slot = (p.n + b) % 2
                            pe.wait_ge(lo_done, p.n + b + 1 + 2 * i)
                            pe.wait_ge(pair_free[b], turn(p.G + b) + 1 + i)
                            first_block = end == 1 and b == 0
                            for h, k in products(first_block):
                                if first_block and h == 0:
                                    input_tile(p, k)
                                if sided and (h, k) == (1, 7 if first_block else 4):
                                    side(turn(p.a) + i, b)
                                c = slice(k * 256 + h * P, k * 256 + (h + 1) * P)
                                ins = three(PAIR[b][h][:, 0:w], WH[slot][:, c], WL[slot][:, c],
                                            XH[:, k, 0:w], XL[:, k, 0:w], k == 0, k == KT - 1)
                            ins.then_inc(block_done, 1)
                            if sided and b:
                                columns(turn(p.a) + F0 + i)

                    run_turns(pe, first, end, two_blocks)
                w = p.ln.w

                def four_tiles(i):
                    for b in range(6):
                        slot = (p.n + FT + b) % 2
                        lo, hi = KPARTS[b % 3]
                        pe.wait_ge(lo_done, p.n + FT + b + 1 + 6 * i)
                        if i == 0 and b < 3:
                            for j in range(2):
                                pe.wait_ge(pair_free[j], turn(p.G + hi - 2 + j) + 2)
                        if b % 3 == 0 and i + b > 0:
                            pe.wait_ge(*p.ln.at("z", 4 * i + 2 * (b // 3) + 2))
                        elif b == 0:
                            pe.wait_ge(pair_free[0], turn(p.G + FT - 2) + 2)
                        for h in range(2):
                            for k in range(lo, hi):
                                if h == 1 and k == lo + 4:
                                    if b < p.out_sides:
                                        side(turn(p.a_out + b) + turn(p.out_sides) * i, b % 2)
                                    if i == 1 and b == 5:
                                        stats_begin(p.ln)
                                c = slice((k - lo) * 256 + h * P, (k - lo) * 256 + (h + 1) * P)
                                ins = three(PAIR[b // 3][h][:, 0:w], WH[slot][:, c], WL[slot][:, c],
                                            AH[:, k, 0:w], AL[:, k, 0:w], k == 0, k == FT - 1)
                            if h == 0 and b % 3 == 2:
                                ins.then_inc(p.ln.sig("half"), 1)
                        ins.then_inc(block_done, 1)
                        if b < p.out_sides and b % 2:
                            columns(turn(p.a_out + b) + F0 + turn(p.out_sides) * i)

                four_tiles(0)
                four_tiles(1)
                stats_end(p.ln)

            def mixer(p):
                s = p.s
                wq, nt = p.nt * P, p.nt
                side_at = [p.a]

                def side_half(b, half):
                    if p.sides[b]:
                        side(turn(side_at[0]), half)

                def side_columns(b):
                    if p.sides[b]:
                        columns(turn(side_at[0]) + F0)
                        side_at[0] += 2

                def project(b, widths):
                    slot, row = (p.n + b) % 2, P * len(widths)
                    pe.wait_ge(lo_done, p.n + b + 1)
                    for h, k in products(b == 0)[0:KT * len(widths)]:
                        w = widths[h]
                        if b == 0 and h == 0:
                            input_tile(p, k)
                        if (h, k) == (0, 4):
                            side_half(b, 0)
                        if (h, k) == (1, 5):
                            side_half(b, 1)
                        if b == IN_BLOCKS - 1 and k >= 4:
                            if k == 4:
                                pe.wait_ge(*s.at("et_used", 16))
                            for d in range(2):
                                updates(k - 4, d)
                        c = slice(k * row + h * P, k * row + (h + 1) * P)
                        ins = three(PAIR[b % 2][h][:, 0:w], WH[slot][:, c], WL[slot][:, c],
                                    XH[:, k, 0:w], XL[:, k, 0:w], k == 0, k == KT - 1)
                    ins.then_inc(block_done, 1)
                    side_columns(b)

                def project_tokens(b):
                    slot = (p.n + b) % 2
                    pe.wait_ge(lo_done, p.n + b + 1)
                    for t in range(4):
                        x = slice(t * P, (t + 1) * P)
                        for k in range(KT):
                            if (t, k) == (1, 0):
                                side_half(b, 0)
                            if (t, k) == (3, 0):
                                side_half(b, 1)
                            c = slice(k * 256, (k + 1) * 256)
                            ins = three(PAIR[b % 2][t // 2][:, (t % 2) * 256:(t % 2) * 256 + 256],
                                        XH[:, k, x], XL[:, k, x], WH[slot][:, c], WL[slot][:, c],
                                        k == 0, k == KT - 1)
                    ins.then_inc(block_done, 1)
                    side_columns(b)

                def gates(t):
                    pe.wait_ge(*s.at("gd", 1))
                    pe.wait_ge(*s.at("pads", 1))
                    pe.wait_ge(*s.at("aux_in", 48))
                    if t >= 2:
                        pe.wait_ge(*s.at("et_used", t - 1))
                    pe.matmul(B_SC[t % 2][:, :], GD[:, t * P:(t + 1) * P], GU[:, :],
                              start=True, stop=True).then_inc(s.sig("gp"), 1)

                def turn_keys(t):
                    pe.wait_ge(*s.at("et_used", 3 + t))
                    for j in range(2):
                        for c in range(2):
                            x = (2 * t + j) * P
                            ins = pe.transpose(B_SC[t][:, j * 256 + c * P:j * 256 + (c + 1) * P],
                                               KTT[:, c, x:x + P], IDENT[:, :])
                    ins.then_inc(s.sig("knp"), 1)

                def cumulate(j):
                    c, d = j // 2, j % 2
                    if j < 2:
                        pe.wait_ge(*s.at("kn", j + 1))
                    else:
                        pe.wait_ge(*s.at("et", 4 + 2 * (j - 1)))
                    for t in range(4):
                        ins = pe.matmul(B_SC[d][:, t * P:(t + 1) * P], LA[:, t, d * 256 + c * P:d * 256 + (c + 1) * P],
                                        TRI[:, d, :], start=True, stop=True)
                    ins.then_inc(s.sig("bp"), 1)

                def to_chunk_end(t):
                    pe.wait_ge(*s.at("et", 10 + t + (t < 2) * t if t < 2 else 11 + t))
                    for d in range(2):
                        ins = pe.matmul(B_SC[t % 2][:, d * 256:(d + 1) * 256], TRI[:, 2 + d, :],
                                        LA[:, t, d * 256:(d + 1) * 256], start=True, stop=True)
                    ins.then_inc(s.sig("enp"), 1)

                def updates(i, d):
                    ch = CHUNK_ORDER[d][i]
                    t, r = ch // 2, slice((ch % 2) * CHUNK, (ch % 2 + 1) * CHUNK)
                    if i:
                        pe.wait_ge(*s.at("state", 2 * (i - 1) + d + 1))
                    for c in range(2):
                        for o in range(2):
                            x = d * 256 + c * P + o * 64
                            h = 2 * c + o
                            ins = pe.matmul(B_SC[d][o * 64:(o + 1) * 64, c * P:(c + 1) * P],
                                            KE[r, t, x:x + 64], VN[r, t, h * P:(h + 1) * P],
                                            start=True, stop=True)
                    ins.then_inc(s.sig("u"), 1)

                def pooled(t):
                    pe.wait_ge(*s.at("pooled", t + 1))
                    pe.wait_ge(*s.at("rt", 2 if t < 2 else 3))
                    pe.matmul(PAIR[(9 + t // 2) % 2][t % 2][:, 0:wq], PW[:, t, :],
                              UP[:, t, 0:wq // LAT, PAD:PAD + LAT], start=True, stop=True).then_inc(s.sig("pm"), 1)

                def scores(h):
                    c, r = h // 2, slice((h % 2) * 64, (h % 2 + 1) * 64)
                    for d in range(2):
                        if h:
                            pe.wait_ge(*s.at("cp", 2 * (h - 1) + d + 1))
                        for t in range(nt):
                            x = slice(t * P, (t + 1) * P)
                            ins = pe.matmul(B_SC[d][:, x], KF[d][r, c, x], QF[d][r, c, x], start=True, stop=True)
                        ins.then_inc(s.sig("sc"), 1)

                def outputs(h):
                    c, r = h // 2, slice((h % 2) * 64, (h % 2 + 1) * 64)
                    bank = PAIR[(11 + c) % 2][h % 2]
                    pe.wait_ge(*s.at("ym", 2 * c + 2))
                    pe.wait_ge(*s.at("at", h + 1))
                    for t in range(nt):
                        x = slice(t * P, (t + 1) * P)
                        pe.matmul(bank[:, x], VN[:, t, h * P:(h + 1) * P], AT[:, h, x],
                                  start=(t == 0), stop=False, skip_group_check=True)
                    for d in range(2):
                        for i in range(1, 8):
                            ch = CHUNK_ORDER[d][i]
                            if ch // 2 < nt:
                                x = slice(ch * CHUNK, (ch + 1) * CHUNK)
                                ins = pe.matmul(bank[:, x], SS[d][r, i - 1, c, :], QF[d][r, c, x],
                                                start=False, stop=(d == 1 and i == 7), skip_group_check=True)
                    ins.then_inc(s.sig("o"), 1)

                project(0, (TOK, wq))
                project(1, (TOK, TOK))
                gates(0)
                gates(1)
                pe.wait_ge(*s.at("gd", 1))
                pe.wait_ge(*s.at("up", 1))
                project(2, (wq, wq))
                gates(2)
                gates(3)
                pe.wait_ge(*s.at("kv", 1))
                project_tokens(3)
                turn_keys(0)
                turn_keys(1)
                pe.wait_ge(*s.at("kv", 2))
                project_tokens(4)
                cumulate(0)
                cumulate(1)
                pe.wait_ge(*s.at("v_in", 1))
                project(5, (wq, wq))
                cumulate(2)
                cumulate(3)
                pe.wait_ge(*s.at("v_in", 2))
                project(6, (wq, wq))
                to_chunk_end(0)
                to_chunk_end(1)
                pe.wait_ge(*s.at("u12", 1))
                project(7, (wq, wq))
                to_chunk_end(2)
                to_chunk_end(3)
                pe.wait_ge(*s.at("up", 2))
                pe.wait_ge(*s.at("rt", 1))
                project(8, (wq,))
                for i in range(4, 7):
                    for d in range(2):
                        updates(i, d)
                    pooled(i - 4)
                pooled(3)
                pe.wait_ge(*s.at("state", 14))

                def mean_squares(h):
                    pe.wait_ge(*s.at("osq", h + 1))
                    if h >= 2:
                        pe.wait_ge(*s.at("std", h - 1))
                    pe.matmul(B_MS[h % 2][:, 0:wq], ONES[:, :], SQH[:, h, 0:wq], start=True,
                              stop=True).then_inc(s.sig("ms"), 1)

                scores(0)
                for h in range(4):
                    if h < 3:
                        scores(h + 1)
                    outputs(h)
                    if h:
                        mean_squares(h - 1)
                mean_squares(3)
                w = p.ln.w
                for b in range(4):
                    slot = (p.n + IN_BLOCKS + b) % 2
                    pe.wait_ge(lo_done, p.n + IN_BLOCKS + b + 1)
                    pe.wait_ge(*p.ln.at("z", 2 * b + 2))
                    for h, k in products(b == 0):
                        if b == 0 and h == 0:
                            pe.wait_ge(*s.at("xl", k + 1))
                        if (b, h, k) == (3, 1, 4):
                            stats_begin(p.ln)
                        c = slice(k * 256 + h * P, k * 256 + (h + 1) * P)
                        ins = three(PAIR[b % 2][h][:, 0:w], WH[slot][:, c], WL[slot][:, c],
                                    XH[:, k, 0:w], XL[:, k, 0:w], k == 0, k == KT - 1)
                        if (h, k) == (0, KT - 1):
                            ins.then_inc(p.ln.sig("half"), 1)
                    ins.then_inc(block_done, 1)
                stats_end(p.ln)

            for p in phases:
                (mixer if p.f == "mix" else ffn)(p)


def kernel(**inputs):
    import numpy as np
    import concourse.bacc as bacc
    from concourse.bass_utils import run_bass_kernel_spmd as run

    v = {k: np.asarray(x) for k, x in inputs.items()}
    f32 = np.float32

    def feature_major(a):
        return np.ascontiguousarray(a.T.reshape(-1, P, a.shape[0]).transpose(1, 0, 2))

    def columns(a):
        return np.ascontiguousarray(a.reshape(-1, KT, P).transpose(2, 0, 1))

    def blocks(w, j, n):
        L, K, _ = w.shape
        return np.ascontiguousarray(w.reshape(L, K // P, P, j, n).transpose(0, 3, 2, 1, 4)
                                    .reshape(L, j, P, K // P * n))

    arrays = {}
    arrays["x"] = feature_major(np.concatenate([v["x"][0], v["ctx"][0]], axis=0))
    arrays["cond"] = feature_major(np.stack([v["c"][0], v["c_ctx"]]))
    w = blocks(v["w_ada"], N_MOD * KT // 2, 2 * P).reshape(FULLS, P, 2, D).transpose(0, 2, 1, 3)
    arrays["w_ada"] = np.ascontiguousarray(w.reshape(HALVES, P, D))
    arrays["b_ada"] = np.ascontiguousarray(v["b_ada"].reshape(2 * FULLS, P).T)
    one, zero = np.ones((1, D), f32), np.zeros((1, D), f32)
    arrays["ln_g"] = columns(np.concatenate([one, v["ln_g"].reshape(-1, D)]))
    arrays["ln_b"] = columns(np.concatenate([zero, v["ln_b"].reshape(-1, D)]))
    for f, name in (("a", "ffa"), ("b", "ffb")):
        w = v[name + "_w_in"].reshape(DEPTH, D, 2, FT, P).transpose(0, 1, 3, 2, 4)
        arrays["ff_in_" + f] = blocks(w.reshape(DEPTH, D, 2 * FF), FT, 256)
        arrays["ff_out_" + f] = blocks(v[name + "_w_out"], 4, 256)
    w = v["mix_w_in"]
    u, q, k, vv, r, gd = (w[..., a:b] for a, b in ((0, 512), (512, 768), (768, 1024), (1024, 1536),
                                                  (1536, 2048), (2048, 2080)))
    order = np.concatenate([gd, r[..., :96], u[..., :P], k, q, vv, u[..., P:], r[..., :3 * P]], axis=-1)
    full = blocks(order, IN_BLOCKS - 1, 256).transpose(0, 2, 1, 3).reshape(DEPTH, P, -1)
    arrays["mix_in"] = np.ascontiguousarray(np.concatenate([full, blocks(r[..., 3 * P:], 1, P)[:, 0]], axis=-1))
    arrays["mix_out"] = blocks(v["mix_w_out"], 4, 256)
    arrays["pool_w"] = np.ascontiguousarray(v["pool_w"].transpose(0, 2, 1, 3))
    gu = np.zeros((DEPTH, 33, TOK), f32)
    gu[:, 0:16, 0:256], gu[:, 16:32, 256:] = v["gate_up_f"], v["gate_up_b"]
    gu[:, 32, 0:256], gu[:, 32, 256:] = v["gate_bias_f"], v["gate_bias_b"]
    arrays["gate_up"] = gu
    cols = np.stack([v["pool_scale"].reshape(DEPTH, 4, P), v["gla_norm_g"].reshape(DEPTH, 4, P)], axis=1)
    arrays["cols"] = np.ascontiguousarray(cols.transpose(3, 0, 1, 2))

    omega = 1.0 / (10000.0 ** (np.arange(256, dtype=f32) / f32(256)))

    def enc(n):
        a = np.arange(n, dtype=f32)[:, None] * omega.astype(f32)
        return feature_major(np.concatenate([np.sin(a), np.cos(a)], axis=-1).astype(f32))

    arrays["pos_r"], arrays["pos_c"] = enc(4), enc(64)
    arrays["ident"] = np.eye(P, dtype=f32)
    arrays["fold"] = np.concatenate([np.eye(2, dtype=f32)] * 2)
    arrays["ones"] = np.full((P, P), 1.0 / D, f32)
    j, i = np.arange(P)[:, None], np.arange(P)[None, :]
    same = j // CHUNK == i // CHUNK
    tri = np.stack([same & (j <= i), same & (j >= i), same & (j > i), same & (j < i)], axis=1)
    arrays["tri"] = np.ascontiguousarray(tri.astype(f32) / f32(16.0))
    t = np.arange(LAT)
    count = np.stack([np.minimum(t + w - 1 - w // 2, LAT - 1) - np.maximum(t - w // 2, 0) + 1 for w in WINDOWS])
    arrays["cinv"] = np.ascontiguousarray(np.broadcast_to(f32(1.0) / count.astype(f32), (P, 4, LAT)))

    nc = bacc.Bacc("TRN2", target_bir_lowering=False, num_devices=1)
    io = {n: nc.dram_tensor("in_" + n, a.shape, mybir.dt.from_np(a.dtype), kind="ExternalInput").ap()
          for n, a in arrays.items()}
    io["out"] = nc.dram_tensor("out", (P, KT, LAT), F32, kind="ExternalOutput").ap()
    build(nc, io)
    got = run(nc, [{"in_" + n: a for n, a in arrays.items()}], core_ids=[0])
    out = np.asarray(got.results[0]["out"])
    return np.ascontiguousarray(out.transpose(2, 1, 0).reshape(1, LAT, D))
```

```python
from contextlib import ExitStack

import concourse.bass as bass
from concourse import mybir

F32 = mybir.dt.float32
F32R = mybir.dt.float32r
U8 = mybir.dt.uint8
ALU = mybir.AluOpType
ACT = mybir.ActivationFunctionType
ds = bass.ds

P = 128
DEPTH = 2
D = 1024
KT = D // P
LAT = 256
TOK = 512
FF = 2816
FT = FF // P
N_MOD = 9
FULLS = DEPTH * N_MOD * KT // 2
HALVES = 2 * FULLS
WB = KT * 2 * P
START_BLOCKS = 2 * KT // 2
START_SLOTS = 5
EPS = 1e-6
ALPHA = (2.0 * DEPTH) ** 0.25
KPARTS = [(0, 8), (8, 16), (16, FT)]
PIECES = ((0, 1), (1, 1), (2, 2), (4, 2), (6, 2))
WARM_LN, WARM_HEADS = 20, 16
WINDOWS = (2, 4, 8, 16)
PAD = 8
UPW = LAT + 2 * PAD
IN_BLOCKS = 9
N_CH = TOK // P
MID = P // 2
CHUNK_ORDER = ((2, 3, 0, 1), (3, 2, 1, 0))
MID_COL = (MID - 1, MID)
END_COL = (P - 1, 0)


class Stage:

    def __init__(self, run, totals, sems, scratch=None, w=0, shift=0, scale=0, last=False):
        self.run, self.totals, self.sems = run, totals, sems
        self.q, self.scratch, self.w, self.shift, self.scale, self.last = run, scratch, w, shift, scale, last

    def sig(self, name):
        return self.sems[name]

    def at(self, name, value):
        return self.sems[name], self.run * self.totals[name] + value


class Phase:

    def __init__(self, f, l, n, a, lins):
        self.f, self.l = f, l
        self.n, self.a = n, a
        self.lin, self.ln = lins
        self.lin.block = n + 1
        self.w = LAT if l == DEPTH - 1 and f == "b" else TOK
        self.gate = l * N_MOD + {"a": 2, "mix": 5, "b": 8}[f]
        self.gate_scale = 1.0 if f == "mix" else 0.5


def build(nc, io):
    with ExitStack() as ctx:
        arena = ctx.enter_context(nc.sbuf_tensor("arena", [P, 212800 // 4], F32))
        base = 16512
        at = [base]

        def sb(name, shape, dt, offset=None):
            size = 4
            for s in shape[1:]:
                size *= s
            if dt == U8:
                size //= 4
            size = -(-size // 32) * 32
            if offset is None:
                offset = at[0]
                at[0] += size
                assert at[0] <= 229344, at[0]
            return nc.alloc_sbuf_tensor_at(name, shape, dt, offset=offset)

        def sem(name):
            return ctx.enter_context(nc.semaphore(name))

        H = sb("H", [P, KT, TOK], F32)
        x_off = at[0]
        XH = sb("XH", [P, KT, TOK], F32R)
        XL = sb("XL", [P, KT, TOK], F32R)
        a_off = at[0]
        AH = sb("AH", [P, FT, TOK], F32R)
        AL = sb("AL", [P, FT, TOK], F32R)
        a_end = at[0]
        RAW = [sb(f"RAW{i}", [P, WB], F32) for i in range(2)]
        WH = [sb(f"WH{i}", [P, WB], F32R) for i in range(2)]
        WL = [sb(f"WL{i}", [P, WB], F32R) for i in range(2)]
        SRAW = sb("SRAW", [P, D], F32)
        SWH = sb("SWH", [P, D], F32R)
        SWL = sb("SWL", [P, D], F32R)
        SG = sb("SG", [P, TOK], F32)
        AF = sb("AF", [P, TOK], F32)
        MODS = sb("MODS", [P, 2 * FULLS, 2], F32)
        BADA = sb("BADA", [P, 2 * FULLS], F32)
        LNG = sb("LNG", [P, 1 + 3 * DEPTH, KT], F32)
        LNB = sb("LNB", [P, 1 + 3 * DEPTH, KT], F32)
        CA = sb("CA", [P, KT, 2], F32)
        CB = sb("CB", [P, KT, 2], F32)
        CHA = sb("CHA", [P, KT, 2], F32)
        CHB = sb("CHB", [P, KT, 2], F32)
        CG = sb("CG", [P, KT, 2], F32)
        COND = sb("COND", [P, KT, 2], F32)
        CSIL = sb("CSIL", [P, KT, 2], F32)
        S4 = sb("S4", [P, KT * 4 + P], F32R)
        ROWS = sb("ROWS", [36, P], F32)
        FOLD = sb("FOLD", [36, 4], F32)
        TRI = sb("TRI", [P, 4, P], F32)
        IDENT = sb("IDENT", [P, P], F32)
        ONES = sb("ONES", [P, P], F32)
        MASK = sb("MASK", [P, 2, P], U8)
        COLS = sb("COLS", [P, DEPTH, 2, 4], F32)
        EPSC = sb("EPSC", [P, 8], F32)

        off = [a_off]

        def over(name, shape, dt=F32, offset=None):
            size = 4
            for s in shape[1:]:
                size *= s
            if offset is None:
                offset = off[0]
                off[0] += -(-size // 32) * 32
                assert off[0] <= a_end, (name, off[0] - a_end)
            return sb(name, shape, dt, offset)

        UP = over("UP", [P, 4, 2, UPW])
        pool_off = off[0]
        PB = over("PB", [P, 2, UPW])
        PC = over("PC", [P, 2, UPW])
        CINV = over("CINV", [P, 4, LAT])
        AT = over("AT", [P, 4, TOK], offset=pool_off)
        assert pool_off + 4 * 4 * TOK <= off[0]
        PW = over("PW", [P, 4, P])
        GU = over("GU", [33, TOK])
        GD = over("GD", [33, TOK])
        kq_off = off[0]
        KTT = over("KTT", [P, 2, TOK])
        QTT = over("QTT", [P, 2, TOK])
        RT = over("RT", [P, 4, TOK], offset=kq_off)
        KN = over("KN", [P, 4, 256])
        vn_off = off[0]
        VN = over("VN", [P, 4, TOK])
        la_off = off[0]
        LA = over("LA", [P, 4, TOK])
        KE = over("KE", [P, 4, TOK], offset=la_off)
        SQH = over("SQH", [P, 4, TOK], offset=la_off)
        QF = [over(f"QF{d}", [P, 2, TOK]) for d in range(2)]
        KF = [over(f"KF{d}", [P, 2, TOK]) for d in range(2)]
        et_off = off[0]
        ET = [over(f"ET{i}", [P, TOK]) for i in range(2)]
        TFB = [over(f"TFB{i}", [P, TOK], offset=et_off + 2048 * i) for i in range(2)]
        SS = [over(f"SS{d}", [P, 2 * (N_CH - 1), 2, P]) for d in range(2)]
        DEC = over("DEC", [P, 2, 2, N_CH])
        DMID = over("DMID", [P, 2, 2, N_CH])
        ln_sq, ln_acc = {}, {}
        for kind, o in (("x", x_off + KT * TOK * 4), ("a", vn_off)):
            ln_sq[kind] = [over(f"LSQ{kind}{i}", [P, TOK], offset=o + 2048 * i) for i in range(2)]
            ln_acc[kind] = [over(f"LAC{kind}{i}", [P, TOK], offset=o + 4096 + 2048 * i) for i in range(2)]
        MU = over("MU", [P, TOK], offset=a_off)
        RS = over("RS", [P, TOK], offset=a_off + 2048)
        M = [over(f"M{i}", [P, 2, TOK], offset=a_off + 4096 + 4096 * i) for i in range(2)]
        START = [over(f"START{i}", [P, WB], offset=vn_off + 8192 + 4 * WB * i) for i in range(START_SLOTS)]
        assert vn_off + 8192 + 4 * WB * START_SLOTS <= a_end
        OUT = over("OUT", [P, KT, LAT], offset=x_off)
        POSR = over("POSR", [P, 4, 4], offset=a_off + 16384)
        POSC = over("POSC", [P, 4, 64], offset=a_off + 16384 + 64)

        BANK = [ctx.enter_context(nc.psum_tensor(f"bank{i}", [P, TOK], F32)) for i in range(8)]
        PAIR = [BANK[0:2], BANK[2:4]]
        B_ROWS, B_COLS, B_SC = BANK[4], BANK[5], BANK[6:8]
        B_MS = BANK[4:6]

        ln_totals = dict(half=4, z=12, sq=8, added=8, stats=2, mu=1, var=1, ln=1, std=1, zc=3, zn=4, zlast=1, mlow=5, mfull=5,
                         xh=5, xl=5, h=1)
        ffn_totals = dict(sg=FT, af=FT, ah=FT)
        mix_totals = dict(aux_in=48, pads=1, gd=1, up=2, u12=1, kv=2, v_in=2, rt=4, gp=4, et=16, et_used=16,
                          knp=2, kn=2, bp=4, enp=4, u=6, state=6, scaled=6, pooled=4, pm=4, ym=4, xh=8, xl=8,
                          sc=8, cp=8, at=4, o=4, osq=4, ms=4, ln=4, std=4, yg=4, yh=4)
        stage_sems = [{s: sem(f"{k}_{s}") for s in t}
                      for k, t in (("ln", ln_totals), ("ffn", ffn_totals), ("mix", mix_totals))]

        def stage(kind, run, **more):
            sems, totals = stage_sems[kind], (ln_totals, ffn_totals, mix_totals)[kind]
            return Stage(run, totals, sems, **more)

        cond_in = sem("cond_in")
        consts_in = sem("consts_in")
        x_in = sem("x_in")
        raw_full = [sem(f"raw_full{i}") for i in range(2)]
        hi_done = sem("hi_done")
        lo_done = sem("lo_done")
        block_done = sem("block_done")
        pair_free = [sem(f"pair_free{i}") for i in range(2)]
        side_full = sem("side_full")
        side_hi = sem("side_hi")
        side_lo = sem("side_lo")
        side_done = sem("side_done")
        start_full = [sem(f"start_full{i}") for i in range(START_SLOTS)]
        rows_ready = sem("rows_ready")
        rows_clear = sem("rows_clear")
        rows_out = sem("rows_out")
        cols_ready = sem("cols_ready")
        mods_done = sem("mods_done")
        sil_ready = sem("sil_ready")
        s4_hi = sem("s4_hi")
        s4_ready = sem("s4_ready")
        s4_tail = sem("s4_tail")
        eps_set = sem("eps_set")
        mask_ready = sem("mask_ready")
        dve_chain = sem("dve_chain")
        act_chain = sem("act_chain")
        pool_chain = sem("pool_chain")
        out_done = sem("out_done")

        def new_ln(scratch, q, width, shift, scale, last=False):
            return stage(0, q, scratch=scratch, w=width, shift=shift, scale=scale, last=last)

        n, a, f_index = 0, 0, 0
        lns = [new_ln("a", 0, TOK, 0, 1)]
        phases = []
        for l in range(DEPTH):
            last = l == DEPTH - 1
            for f in ("a", "mix", "b"):
                m = l * N_MOD
                shift = m + {"a": 3, "mix": 6, "b": 9}[f]
                q = 1 + 3 * l + ("a", "mix", "b").index(f)
                p = Phase(f, l, n, a, lins=(lns[-1], new_ln("a" if f == "mix" else "x", q,
                                                            LAT if last and f != "a" else TOK,
                                                            shift, shift + 1, last and f == "b")))
                lns.append(p.ln)
                if f == "mix":
                    p.sides = [0, 2, 0, 2, 2, 2, 0, 0, 0, 0] if last else [0] + [2] * 7 + [0, 0]
                    p.out_sides = 0 if last else 4
                    p.nt = 2 if last else 4
                    p.s = stage(2, l)
                    n, a = n + IN_BLOCKS + 4, a + sum(p.sides) + p.out_sides
                else:
                    p.G = FT * f_index
                    sided = not (last and f == "b")
                    p.loops = [(0, 1, sided), (1, 11, sided)]
                    p.out_sides = 6 * sided
                    p.a_out = a + 2 * sum((e - b) * s for b, e, s in p.loops)
                    p.s = stage(1, f_index)
                    f_index += 1
                    p.lead = 1 if p.w == TOK else 2
                    n, a = n + FT + 12, p.a_out + 2 * p.out_sides
                phases.append(p)
        H0 = 2 * START_BLOCKS
        F0 = START_BLOCKS
        assert a == HALVES - H0
        N_BLOCKS = n

        def run_turns(engine, first, end, turn_of):
            if end - first == 1:
                turn_of(first)
            else:
                with engine.Fori(first, end) as i:
                    turn_of(i)

        def normed(ln, q, j):
            return OUT[:, PIECES[q][0] + j, :] if ln.last else M[q % 2][:, j, :]

        def normalised(engine, ln, q):
            if q < len(PIECES) - 1:
                engine.wait_ge(*ln.at("zn", q + 1))
            else:
                engine.wait_ge(*ln.at("zlast", 1))

        def mods_ready(engine, m):
            engine.wait_ge(mods_done, (m + 1) * KT // 2)

        def mod(m):
            return MODS[:, m * KT:(m + 1) * KT, :]

        def by_tile(s4):
            return s4[:, 0:KT * 4].rearrange("p (k c) -> p k c", c=4)

        def turn(k):
            return k // 2

        def wout_loops(p):
            return [(0, 1), (1, 2)] if p.n + FT + 12 == N_BLOCKS else [(0, 2)]

        block = ctx.enter_context(nc.Block())

        @block.sync
        def _(sp):
            def load_main(k, slot, src, size=WB):
                if not (isinstance(k, int) and k < 2):
                    sp.wait_ge(lo_done, k - 1)
                sp.dma_start(RAW[slot][:, 0:size], src).then_inc(raw_full[slot], 16)

            def load_side(k):
                sp.wait_ge(side_lo, k + 1)
                sp.dma_start(SRAW[:, :], io["w_ada"][ds(k + H0, 1), :, :]
                             .rearrange("h p n -> p (h n)")).then_inc(side_full, 16)

            def load_start(b):
                if b >= START_SLOTS:
                    sp.wait_ge(rows_ready, b - START_SLOTS + 1)
                sp.dma_start(START[b % START_SLOTS][:, :].rearrange("p (h n) -> p h n", h=2),
                             io["w_ada"][2 * b:2 * b + 2, :, :].rearrange("h p n -> p h n")
                             ).then_inc(start_full[b % START_SLOTS], 16)

            sp.dma_start(COND[:, :, :], io["cond"]).then_inc(cond_in, 16)
            load_start(0)
            load_start(1)
            sp.dma_start(H[:, :, :], io["x"]).then_inc(x_in, 16)
            for dst, name in ((IDENT[:, :], "ident"), (BADA[:, :], "b_ada"), (LNG[:, :, :], "ln_g"),
                              (LNB[:, :, :], "ln_b"), (ONES[:, :], "ones"), (POSR[:, :, :], "pos_r"),
                              (POSC[:, :, :], "pos_c"), (TRI[:, :, :], "tri"),
                              (COLS[:, :, :, :], "cols"), (FOLD[:, :], "fold")):
                sp.dma_start(dst, io[name]).then_inc(consts_in, 16)
            for b in range(2, START_BLOCKS):
                load_start(b)

            def ffn(p):
                w_in, w_out = io["ff_in_" + p.f], io["ff_out_" + p.f]
                for first, end, side in p.loops:
                    def two_blocks(i):
                        for b in range(2):
                            load_main(p.n + b + 2 * i, (p.n + b) % 2,
                                      w_in[p.l, ds(2 * i + b, 1), :, :].rearrange("j p n -> p (j n)"))
                            if side:
                                load_side(p.a + b + 2 * i)

                    run_turns(sp, first, end, two_blocks)
                with sp.Fori(0, 2) as i:
                    for b in range(6):
                        lo, hi = KPARTS[b % 3]
                        load_main(p.n + FT + b + 6 * i, (p.n + FT + b) % 2,
                                  w_out[p.l, ds(2 * i + b // 3, 1), :, lo * 256:hi * 256]
                                  .rearrange("j p n -> p (j n)"), (hi - lo) * 256)
                        if b < p.out_sides:
                            load_side(p.a_out + b + p.out_sides * i)

            def mixer(p):
                def load(b):
                    if b < IN_BLOCKS:
                        size = WB if b < IN_BLOCKS - 1 else WB // 2
                        load_main(p.n + b, (p.n + b) % 2, io["mix_in"][p.l, :, b * WB:b * WB + size], size)
                    else:
                        load_main(p.n + b, (p.n + b) % 2, io["mix_out"][p.l, b - IN_BLOCKS])

                k = p.a
                load(0)
                for b in range(IN_BLOCKS):
                    load(b + 1)
                    for _ in range(p.sides[b]):
                        load_side(k)
                        k += 1
                    if b == 1:
                        sp.wait_ge(*p.lin.at("xl", 5))
                        sp.dma_start(GU[:, :], io["gate_up"][p.l]).then_inc(p.s.sig("aux_in"), 16)
                        sp.dma_start(CINV[:, :, :], io["cinv"]).then_inc(p.s.sig("aux_in"), 16)
                        sp.dma_start(PW[:, :, :], io["pool_w"][p.l]).then_inc(p.s.sig("aux_in"), 16)
                for b in range(IN_BLOCKS, IN_BLOCKS + 4):
                    if b > IN_BLOCKS:
                        load(b)
                    if p.out_sides:
                        load_side(k)
                        k += 1

            for p in phases:
                (mixer if p.f == "mix" else ffn)(p)
            for q, (t, m) in enumerate(PIECES):
                sp.wait_ge(*lns[-1].at("mfull", q + 1))
                sp.wait_ge(*lns[-1].at("mlow", q + 1))
                sp.dma_start(io["out"][:, t:t + m, :], OUT[:, t:t + m, :]).then_inc(out_done, 16)
            sp.wait_ge(out_done, 16 * len(PIECES))

        @block.scalar
        def _(act):
            links = [0]

            def link(ins):
                links[0] += 1
                ins.then_inc(act_chain, 1)
                act.wait_ge(act_chain, links[0])

            def split_hi(k, t, slot):
                act.wait_ge(raw_full[slot], 16 * t + 16)
                if not (isinstance(k, int) and k < 2):
                    act.wait_ge(block_done, k - 1)
                act.copy(WH[slot][:, :], RAW[slot][:, :]).then_inc(hi_done, 1)

            def split_hi_part(k, half):
                slot, c = k % 2, slice(half * WB // 2, (half + 1) * WB // 2)
                if half == 0:
                    act.wait_ge(raw_full[slot], 16 * turn(k) + 16)
                    if k >= 2:
                        act.wait_ge(block_done, k - 1)
                ins = act.copy(WH[slot][:, c], RAW[slot][:, c])
                if half == 1:
                    ins.then_inc(hi_done, 1)

            def side_high(k):
                act.wait_ge(side_full, 16 * k + 16)
                if not (isinstance(k, int) and k == 0):
                    act.wait_ge(side_done, k)
                act.copy(SWH[:, :], SRAW[:, :]).then_inc(side_hi, 1)

            def rows_evac(g):
                act.wait_ge(side_done, 2 * g + 2)
                act.wait_ge(cols_ready, F0 + g)
                act.copy(ROWS[0:4, :], B_ROWS[0:4, 0:P])
                act.copy(ROWS[32:36, :], B_ROWS[0:4, P:2 * P]).then_inc(rows_out, 1)

            def square(ln, t, par):
                act.wait_ge(*ln.at("z", t + 5))
                act.wait_ge(*ln.at("added", t + 1))
                act.activation(ln_sq[ln.scratch][par][:, 0:ln.w],
                               H[:, ds(t, 1), 0:ln.w].rearrange("p a n -> p (a n)"),
                               ACT.Square).then_inc(ln.sig("sq"), 1)

            def layernorm(ln):
                w = ln.w
                if not ln.last:
                    split_hi_part(ln.block, 0)
                act.wait_ge(*ln.at("stats", 1))
                act.copy(MU[:, 0:w], B_SC[0][:, 0:w]).then_inc(ln.sig("mu"), 1)
                if not ln.last:
                    split_hi_part(ln.block, 1)
                act.wait_ge(*ln.at("var", 1))
                act.activation(RS[:, 0:w], RS[:, 0:w], ACT.Ln).then_inc(ln.sig("ln"), 1)
                act.wait_ge(*ln.at("ln", 1))
                act.activation(RS[:, 0:w], RS[:, 0:w], ACT.Exp, scale=-0.5).then_inc(ln.sig("std"), 1)
                for q, (t, m) in enumerate(PIECES):
                    normalised(act, ln, q)
                    if q >= 2 and not ln.last:
                        act.wait_ge(*ln.at("xl", q - 1))
                    c, s = slice(w // 2, w), w // TOK
                    for j in range(m):
                        ins = act.activation(normed(ln, q, j)[:, c], H[:, t + j, c], ACT.Identity,
                                             bias=CB[:, t + j, s:s + 1], scale=CA[:, t + j, s:s + 1])
                    ins.then_inc(ln.sig("mfull"), 1)
                    if not ln.last:
                        act.wait_ge(*ln.at("mfull", q + 1))
                        act.wait_ge(*ln.at("mlow", q + 1))
                        act.copy(XH[:, t:t + m, 0:w], M[q % 2][:, 0:m, 0:w]).then_inc(ln.sig("xh"), 1)

            act.wait_ge(cond_in, 16)
            act.activation(CSIL[:, :, :], COND[:, :, :], ACT.Silu).then_inc(sil_ready, 1)
            act.wait_ge(eps_set, 1)
            act.wait_ge(rows_clear, 1)
            act.wait_ge(sil_ready, 1)
            act.copy(by_tile(S4)[:, :, 0:2], CSIL[:, :, :]).then_inc(s4_hi, 1)

            def start_rows(b):
                act.wait_ge(rows_ready, b + 1)
                if b:
                    act.wait_ge(cols_ready, b)
                act.copy(ROWS[0:2, :], BANK[b % 2][0:2, 0:P])
                act.copy(ROWS[32:34, :], BANK[b % 2][0:2, P:2 * P]).then_inc(rows_out, 1)

            for b in range(START_BLOCKS):
                start_rows(b)
                if b == 1:
                    act.preload_act_table_set("natural_log_exp_and_others")
                for t in range(2 * b - 4, 2 * b - 2):
                    if 0 <= t < KT:
                        square(lns[0], t, t % 2)
            split_hi(0, 0, 0)
            layernorm(lns[0])

            def ffn(p):
                w = p.w
                for first, end, side in p.loops:
                    def two_blocks(i):
                        act.preload_act_table_set("silu_and_others")
                        for b in range(2):
                            k = p.n + b
                            if side:
                                side_high(p.a + b + 2 * i)
                            if p.lead == 1 and not (end == 1 and b == 0):
                                split_hi(k + 1 + 2 * i, turn(k + 1) + i, (k + 1) % 2)
                            if side and b:
                                rows_evac(turn(p.a) + i)
                            act.wait_ge(block_done, k + 1 + 2 * i)
                            act.activation(SG[:, 0:w], PAIR[b][0][:, 0:w], ACT.Silu).then_inc(p.s.sig("sg"), 1)
                            if p.lead == 2:
                                split_hi(k + 2 + 2 * i, turn(k + 2) + i, k % 2)
                            act.wait_ge(*p.s.at("af", b + 1 + 2 * i))
                            act.copy(AH[:, ds(2 * i + b, 1), 0:w].rearrange("p a n -> p (a n)"),
                                     AF[:, 0:w]).then_inc(p.s.sig("ah"), 1)

                    run_turns(act, first, end, two_blocks)
                act.preload_act_table_set("natural_log_exp_and_others")
                for first, end in wout_loops(p):
                    with act.Fori(first, end) as i:
                        for b in range(6):
                            k = p.n + FT + b
                            if b < p.out_sides:
                                side_high(p.a_out + b + p.out_sides * i)
                            if not (first == 1 and b + p.lead > 5):
                                split_hi(k + p.lead + 6 * i, turn(k + p.lead) + 3 * i, (k + p.lead) % 2)
                            if b < p.out_sides and b % 2:
                                rows_evac(turn(p.a_out + b) + turn(p.out_sides) * i)
                            if b % 3 == 2:
                                for h in range(2):
                                    square(p.ln, 4 * i + 2 * (b // 3) + h, h)
                layernorm(p.ln)

            def mixer(p):
                s = p.s
                wq = p.nt * P
                ets = [0]
                side = [p.a]

                def step(b):
                    k = p.n + b + 1
                    if p.sides[b]:
                        side_high(side[0] + 1)
                    if b:
                        split_hi(k, turn(k), k % 2)
                    if p.sides[b + 1]:
                        side_high(side[0] + p.sides[b])
                    if p.sides[b]:
                        rows_evac(turn(side[0]))
                        side[0] += 2
                    act.wait_ge(block_done, p.n + b + 1)

                def exp_buffer():
                    if ets[0] >= 2:
                        act.wait_ge(*s.at("et_used", ets[0] - 1))
                    ets[0] += 1
                    return ET[(ets[0] - 1) % 2]

                def gates(t):
                    act.wait_ge(*s.at("gp", t + 1))
                    e = exp_buffer()
                    link(act.activation(e[:, :], B_SC[t % 2][:, :], ACT.Abs))
                    link(act.activation(e[:, :], e[:, :], ACT.Exp, scale=-1.0))
                    act.activation(e[:, :], e[:, :], ACT.Ln, bias=1.0).then_inc(s.sig("et"), 1)

                def decays(j):
                    act.wait_ge(*s.at("bp", j + 1))
                    act.activation(exp_buffer()[:, :], B_SC[j % 2][:, :], ACT.Exp).then_inc(s.sig("et"), 1)
                    act.activation(exp_buffer()[:, :], B_SC[j % 2][:, :], ACT.Exp, scale=-1.0).then_inc(s.sig("et"), 1)

                def end_decays(t):
                    act.wait_ge(*s.at("enp", t + 1))
                    act.activation(exp_buffer()[:, :], B_SC[t % 2][:, :], ACT.Exp).then_inc(s.sig("et"), 1)

                def padded(t):
                    return UP[:, t, 0:wq // LAT, PAD:PAD + LAT]

                def by_stream(bank):
                    return bank[:, 0:wq].rearrange("p (s n) -> p s n", n=LAT)

                step(0)
                act.wait_ge(*p.lin.at("xl", 5))
                act.copy(GD[0:32, :], PAIR[0][0][0:32, :]).then_inc(s.sig("gd"), 1)
                act.wait_ge(*s.at("pads", 1))
                act.copy(padded(0), by_stream(PAIR[0][1])).then_inc(s.sig("up"), 1)
                step(1)
                act.copy(KTT[:, 0, :], PAIR[1][0][:, :])
                act.copy(KTT[:, 1, :], PAIR[1][1][:, :]).then_inc(s.sig("kv"), 1)
                act.preload_act_table_set("natural_log_exp_and_others")
                gates(0)
                gates(1)
                step(2)
                act.activation(QTT[:, 0, 0:wq], PAIR[0][0][:, 0:wq], ACT.Copy, scale=0.125)
                act.activation(QTT[:, 1, 0:wq], PAIR[0][1][:, 0:wq], ACT.Copy, scale=0.125).then_inc(s.sig("kv"), 1)
                gates(2)
                gates(3)
                step(3)
                for t in range(2):
                    act.wait_ge(*s.at("knp", t + 1))
                    act.copy(KN[:, 2 * t:2 * t + 2, :],
                             B_SC[t][:, :].rearrange("p (t n) -> p t n", n=256)).then_inc(s.sig("kn"), 1)
                step(4)
                decays(0)
                decays(1)
                step(5)
                decays(2)
                decays(3)
                step(6)
                act.copy(padded(3), by_stream(PAIR[0][0])).then_inc(s.sig("up"), 1)
                act.wait_ge(*s.at("et_used", 12))
                act.copy(RT[:, 0, 0:wq], PAIR[0][1][:, 0:wq]).then_inc(s.sig("rt"), 1)
                end_decays(0)
                end_decays(1)
                step(7)
                act.copy(RT[:, 1, 0:wq], PAIR[1][0][:, 0:wq])
                act.copy(RT[:, 2, 0:wq], PAIR[1][1][:, 0:wq]).then_inc(s.sig("rt"), 1)
                end_decays(2)
                end_decays(3)
                step(8)
                if p.out_sides:
                    side_high(side[0])
                act.copy(RT[:, 3, 0:wq], PAIR[0][0][:, 0:wq]).then_inc(s.sig("rt"), 1)
                for t in range(4):
                    act.wait_ge(*s.at("pm", t + 1))
                    flat = UP[:, t, :, :].rearrange("p s n -> p (s n)")[:, 0:wq]
                    act.activation(flat, PAIR[(9 + t // 2) % 2][t % 2][:, 0:wq], ACT.Copy,
                                   scale=COLS[:, p.l, 0, t:t + 1]).then_inc(s.sig("ym"), 1)
                    act.wait_ge(*s.at("ym", t + 1))
                    act.copy(XH[:, t, 0:wq], flat).then_inc(s.sig("xh"), 1)
                act.wait_ge(*s.at("rt", 3))
                act.activation(RT[:, :, 0:wq], RT[:, :, 0:wq], ACT.Silu).then_inc(s.sig("rt"), 1)
                act.preload_act_table_set("natural_log_exp_and_others")

                def squares(h):
                    act.wait_ge(*s.at("o", h + 1))
                    act.activation(SQH[:, h, 0:wq], PAIR[(11 + h // 2) % 2][h % 2][:, 0:wq],
                                   ACT.Square).then_inc(s.sig("osq"), 1)

                def inverse_roots(h):
                    act.wait_ge(*s.at("ms", h + 1))
                    act.activation(SQH[:, h, 0:wq], B_MS[h % 2][:, 0:wq], ACT.Ln, bias=EPSC[:, 0:1],
                                   scale=float(KT)).then_inc(s.sig("ln"), 1)
                    act.wait_ge(*s.at("ln", h + 1))
                    act.activation(SQH[:, h, 0:wq], SQH[:, h, 0:wq], ACT.Exp, scale=-0.5).then_inc(s.sig("std"), 1)

                def high(h):
                    act.wait_ge(*s.at("yh", h + 1))
                    act.copy(XH[:, 4 + h, 0:wq], SQH[:, h, 0:wq]).then_inc(s.sig("xh"), 1)

                for h in range(6):
                    if h < 4:
                        squares(h)
                    if 1 <= h < 5:
                        inverse_roots(h - 1)
                    if h >= 2:
                        high(h - 2)
                for b in range(4):
                    k = p.n + IN_BLOCKS + b
                    if p.out_sides and b:
                        side_high(side[0] + b)
                    split_hi(k + 1, turn(k + 1), (k + 1) % 2)
                    if p.out_sides and b % 2:
                        rows_evac(turn(side[0] + b))
                    for h in range(2):
                        square(p.ln, 2 * b + h, h)
                layernorm(p.ln)

            for p in phases:
                (mixer if p.f == "mix" else ffn)(p)

        @block.vector
        def _(dve):
            links = [0]

            def link(ins):
                links[0] += 1
                ins.then_inc(dve_chain, 1)
                dve.wait_ge(dve_chain, links[0])

            def split_lo(k, slot):
                dve.wait_ge(hi_done, k + 1)
                dve.tensor_tensor(WL[slot][:, :], RAW[slot][:, :], WH[slot][:, :].bitcast(F32),
                                  ALU.subtract).then_inc(lo_done, 1)

            def side_low(k):
                dve.wait_ge(side_hi, k + 1)
                dve.tensor_tensor(SWL[:, :], SRAW[:, :], SWH[:, :].bitcast(F32),
                                  ALU.subtract).then_inc(side_lo, 1)

            def fold(f):
                dve.wait_ge(cols_ready, f + 1)
                dve.tensor_tensor(MODS[:, ds(2 * f, 2), :], B_COLS[:, 0:4].rearrange("p (a c) -> p a c", c=2),
                                  BADA[:, ds(2 * f, 2)].unsqueeze(2).broadcast_to([P, 2, 2]),
                                  ALU.add).then_inc(mods_done, 1)

            def gates_ready(p):
                mods_ready(dve, p.gate)
                dve.tensor_scalar(CG[:, :, :], mod(p.gate), p.gate_scale, None, ALU.mult).then_inc(p.ln.sig("z"), 4)
                dve.wait_ge(*p.ln.at("z", 4))
                dve.wait_ge(*p.lin.at("h", 1))

            def residual(p, t, bank):
                for s in range(p.ln.w // LAT):
                    c = slice(s * LAT, s * LAT + LAT)
                    h = H[:, ds(t, 1), c].rearrange("p a n -> p (a n)")
                    g = CG[:, ds(t, 1), s:s + 1].rearrange("p a n -> p (a n)")
                    ins = dve.scalar_tensor_tensor(h, bank[:, c], g, h, op0=ALU.mult, op1=ALU.add)
                ins.then_inc(p.ln.sig("z"), 1)

            def layernorm(ln):
                w = ln.w
                g, b = (v[:, ln.q, :].unsqueeze(2).broadcast_to([P, KT, 2]) for v in (LNG, LNB))
                if ln.last:
                    dve.tensor_copy(CA[:, :, :], g)
                    link(dve.tensor_copy(CB[:, :, :], b))
                else:
                    mods_ready(dve, ln.scale)
                    dve.scalar_tensor_tensor(CA[:, :, :], mod(ln.scale), 1.0, g, op0=ALU.add, op1=ALU.mult)
                    link(dve.scalar_tensor_tensor(CB[:, :, :], mod(ln.scale), 1.0, b, op0=ALU.add, op1=ALU.mult))
                    dve.tensor_scalar(CHA[:, :, :], g, ALPHA, None, ALU.mult)
                    dve.tensor_scalar(CHB[:, :, :], b, ALPHA, None, ALU.mult)
                    link(dve.tensor_tensor(CB[:, :, :], CB[:, :, :], mod(ln.shift), ALU.add))
                dve.wait_ge(*ln.at("mu", 1))
                link(dve.tensor_tensor(RS[:, 0:w], MU[:, 0:w], MU[:, 0:w], ALU.mult))
                dve.wait_ge(*ln.at("stats", 2))
                link(dve.scalar_tensor_tensor(RS[:, 0:w], B_SC[1][:, 0:w], EPS, RS[:, 0:w], op0=ALU.add,
                                              op1=ALU.subtract))
                dve.tensor_scalar(RS[:, 0:w], RS[:, 0:w], EPS, None, ALU.max).then_inc(ln.sig("var"), 1)

                def low(q):
                    t, m = PIECES[q]
                    dve.wait_ge(*ln.at("xh", q + 1))
                    dve.tensor_tensor(XL[:, t:t + m, 0:w], M[q % 2][:, 0:m, 0:w],
                                      XH[:, t:t + m, 0:w].bitcast(F32), ALU.subtract).then_inc(ln.sig("xl"), 1)

                z0 = H[:, 0:2, 0:w]
                link(dve.tensor_tensor(z0, z0, MU[:, 0:w].unsqueeze(1).broadcast_to([P, 2, w]), ALU.subtract))
                dve.wait_ge(*ln.at("std", 1))
                for q, (t, m) in enumerate(PIECES):
                    z = H[:, t:t + m, 0:w]
                    if t >= 2:
                        dve.wait_ge(*ln.at("zc", t // 2))
                    if q < len(PIECES) - 1:
                        dve.tensor_tensor(z, z, RS[:, 0:w].unsqueeze(1).broadcast_to([P, m, w]),
                                          ALU.mult).then_inc(ln.sig("zn"), 1)
                    elif not ln.last:
                        low(q - 1)
                    normalised(dve, ln, q)
                    if q >= 2 and not ln.last:
                        dve.wait_ge(*ln.at("xl", q - 1))
                    c = slice(0, w // 2)
                    for j in range(m):
                        ins = dve.tensor_scalar(normed(ln, q, j)[:, c], H[:, t + j, c], CA[:, t + j, 0:1],
                                                CB[:, t + j, 0:1], ALU.mult, ALU.add)
                    ins.then_inc(ln.sig("mlow"), 1)
                    if 0 < q < len(PIECES) - 1 and not ln.last:
                        low(q - 1)
                if not ln.last:
                    low(len(PIECES) - 1)
                    split_lo(ln.block, ln.block % 2)

            dve.memset(ROWS[:, :], 0.0).then_inc(rows_clear, 1)
            dve.memset(EPSC[:, 0:1], EPS).then_inc(eps_set, 1)
            for i, free in enumerate((side_lo, *pair_free)):
                dve.memset(EPSC[:, 1 + i:2 + i], 0.0).then_inc(free, 1)
            dve.memset(EPSC[:, 4:5], 0.0).then_inc(lns[0].sig("half"), 4)
            dve.memset(S4[:, KT * 4:].bitcast(F32), 0.0).then_inc(s4_tail, 1)
            dve.wait_ge(s4_hi, 1)
            dve.tensor_tensor(by_tile(S4)[:, :, 2:4], CSIL[:, :, :], by_tile(S4)[:, :, 0:2].bitcast(F32),
                              ALU.subtract).then_inc(s4_ready, 1)
            dve.wait_ge(x_in, 16)
            dve.wait_ge(consts_in, 10 * 16)
            dve.tensor_scalar(MASK[:, :, :], TRI[:, 2:4, :], 0.0, None, ALU.is_equal).then_inc(mask_ready, 1)
            for t in range(4):
                z = H[:, t, 0:LAT].rearrange("p (r c) -> p r c", c=64)
                dve.tensor_tensor(z, z, POSR[:, t, :].unsqueeze(2).broadcast_to([P, 4, 64]), ALU.add)
            for t in range(4):
                z = H[:, 4 + t, 0:LAT].rearrange("p (r c) -> p r c", c=64)
                ins = dve.tensor_tensor(z, z, POSC[:, t, :].unsqueeze(1).broadcast_to([P, 4, 64]), ALU.add)
            ins.then_inc(lns[0].sig("z"), 12)
            for b in range(START_BLOCKS):
                fold(b)
            split_lo(0, 0)
            layernorm(lns[0])

            def ffn(p):
                w = p.w
                for first, end, side in p.loops:
                    def two_blocks(i):
                        for b in range(2):
                            k = p.n + b
                            if side:
                                side_low(p.a + b + 2 * i)
                            if p.lead == 1 and not (end == 1 and b == 0):
                                split_lo(k + 1 + 2 * i, (k + 1) % 2)
                            dve.wait_ge(*p.s.at("sg", b + 1 + 2 * i))
                            dve.wait_ge(pair_free[1 - b], turn(p.G) + 1 + b + i)
                            dve.tensor_tensor(AF[:, 0:w], SG[:, 0:w], PAIR[b][1][:, 0:w],
                                              ALU.mult).then_inc(p.s.sig("af"), 1)
                            if p.lead == 2:
                                split_lo(k + 2 + 2 * i, k % 2)
                            dve.wait_ge(*p.s.at("ah", b + 1 + 2 * i))
                            ah = AH[:, ds(2 * i + b, 1), 0:w].rearrange("p a n -> p (a n)")
                            al = AL[:, ds(2 * i + b, 1), 0:w].rearrange("p a n -> p (a n)")
                            dve.tensor_tensor(al, AF[:, 0:w], ah.bitcast(F32),
                                              ALU.subtract).then_inc(pair_free[b], 1)
                            if side and b:
                                fold(turn(p.a) + F0 + i)

                    run_turns(dve, first, end, two_blocks)
                gates_ready(p)
                for first, end in wout_loops(p):
                    with dve.Fori(first, end) as i:
                        for b in range(6):
                            k = p.n + FT + b
                            if b < p.out_sides:
                                side_low(p.a_out + b + p.out_sides * i)
                            if not (first == 1 and b + p.lead > 5):
                                split_lo(k + p.lead + 6 * i, (k + p.lead) % 2)
                            if b % 3 == 2:
                                dve.wait_ge(*p.ln.at("half", 2 * i + b // 3 + 1))
                                residual(p, 4 * i + 2 * (b // 3), PAIR[b // 3][0])
                                dve.wait_ge(block_done, k + 1 + 6 * i)
                                residual(p, 4 * i + 2 * (b // 3) + 1, PAIR[b // 3][1])
                            if b < p.out_sides and b % 2:
                                fold(turn(p.a_out + b) + F0 + turn(p.out_sides) * i)
                layernorm(p.ln)

            def mixer(p):
                s = p.s
                wq, nt = p.nt * P, p.nt
                ns = wq // LAT
                side = [p.a]

                def step(b):
                    k = p.n + b + 1
                    if p.sides[b]:
                        side_low(side[0] + 1)
                    if b:
                        split_lo(k, k % 2)
                    if p.sides[b + 1]:
                        side_low(side[0] + p.sides[b])
                    if p.sides[b]:
                        fold(turn(side[0]) + F0)
                        side[0] += 2
                    dve.wait_ge(block_done, p.n + b + 1)

                def log_gates(t):
                    dve.wait_ge(*s.at("et", t + 1))
                    dve.scalar_tensor_tensor(LA[:, t, :], B_SC[t % 2][:, :], 0.0, ET[t % 2][:, :],
                                             op0=ALU.min, op1=ALU.subtract).then_inc(s.sig("et_used"), 1)

                def scaled(j):
                    c, d = j // 2, j % 2
                    dve.wait_ge(*s.at("et", 4 + 2 * j + 1))
                    dve.wait_ge(*s.at("kv", 2))
                    link(dve.tensor_copy(DMID[:, d, c, :], ET[0][:, MID_COL[d]::P]))
                    dve.tensor_tensor(DEC[:, d, c, :], ET[0][:, END_COL[d]::P], DMID[:, d, c, :], ALU.mult)
                    link(dve.tensor_tensor(QF[d][:, c, 0:wq], QTT[:, c, 0:wq], ET[0][:, 0:wq], ALU.mult))
                    m = slice(MID_COL[d], wq, P)
                    dve.tensor_copy(QF[d][:, c, m], QTT[:, c, m]).then_inc(s.sig("et_used"), 1)
                    dve.wait_ge(*s.at("et", 4 + 2 * j + 2))
                    link(dve.tensor_tensor(KF[d][:, c, :], KTT[:, c, :], ET[1][:, :], ALU.mult))
                    m = slice(MID_COL[d], TOK, P)
                    dve.tensor_copy(KF[d][:, c, m], KTT[:, c, m]).then_inc(s.sig("et_used"), 1)

                def end_keys(t):
                    dve.wait_ge(*s.at("et", 12 + t + 1))
                    dve.wait_ge(*s.at("kn", 2))
                    dve.tensor_tensor(KE[:, t, :].rearrange("p (d n) -> p d n", d=2),
                                      ET[t % 2][:, :].rearrange("p (d n) -> p d n", d=2),
                                      KN[:, t, :].unsqueeze(1).broadcast_to([P, 2, 256]),
                                      ALU.mult).then_inc(s.sig("et_used"), 1)

                def values(v):
                    for t in range(2):
                        ins = dve.tensor_copy(VN[:, 2 * t:2 * t + 2, 256 * v:256 * v + 256],
                                              PAIR[(3 + v) % 2][t][:, :].rearrange("p (t n) -> p t n", n=256))
                    ins.then_inc(s.sig("v_in"), 1)

                dve.wait_ge(*p.lin.at("xl", 5))
                dve.memset(UP[:, :, :, 0:PAD], 0.0)
                dve.memset(UP[:, :, :, PAD + LAT:UPW], 0.0)
                dve.memset(GD[32:33, :], 1.0).then_inc(s.sig("pads"), 1)
                step(0)
                step(1)
                log_gates(0)
                log_gates(1)
                step(2)
                log_gates(2)
                log_gates(3)
                step(3)
                values(0)
                step(4)
                values(1)
                scaled(0)
                scaled(1)
                step(5)
                for t in range(2):
                    ins = dve.tensor_copy(UP[:, 1 + t, 0:ns, PAD:PAD + LAT],
                                          PAIR[1][t][:, 0:wq].rearrange("p (s n) -> p s n", n=LAT))
                ins.then_inc(s.sig("u12"), 1)
                scaled(2)
                scaled(3)
                step(6)
                end_keys(0)
                end_keys(1)
                step(7)
                end_keys(2)
                end_keys(3)
                dve.wait_ge(*s.at("et_used", 16))
                for d in range(2):
                    ins = dve.memset(TFB[d][:, :], 0.0)
                link(ins)
                for i in range(N_CH - 1):
                    for d in range(2):
                        dve.wait_ge(*s.at("u", 2 * i + d + 1))
                        if i:
                            dve.wait_ge(*s.at("state", 2 * (i - 1) + d + 1))
                        ch = CHUNK_ORDER[d][i]
                        for c in range(2):
                            u = B_SC[d][:, c * P:(c + 1) * P]
                            if i == 0:
                                ins = dve.tensor_copy(SS[d][:, i, c, :], u)
                            else:
                                ins = dve.scalar_tensor_tensor(SS[d][:, i, c, :], SS[d][:, i - 1, c, :],
                                                               DEC[:, d, c, ch:ch + 1], u,
                                                               op0=ALU.mult, op1=ALU.add)
                        ins.then_inc(s.sig("state"), 1)
                    for d in range(2):
                        dve.wait_ge(*s.at("state", 2 * i + d + 1))
                        ch = CHUNK_ORDER[d][i + 1]
                        for c in range(2):
                            ins = dve.tensor_scalar(SS[d][:, N_CH - 1 + i, c, :], SS[d][:, i, c, :],
                                                    DMID[:, d, c, ch:ch + 1], None, ALU.mult)
                        ins.then_inc(s.sig("scaled"), 1)
                def masked(h):
                    if h:
                        dve.wait_ge(*s.at("at", h))
                    for d in range(2):
                        dve.wait_ge(*s.at("sc", 2 * h + d + 1))
                        dve.copy_predicated(TFB[d][:, 0:wq].rearrange("p (t n) -> p t n", n=P),
                                            MASK[:, d, :].unsqueeze(1).broadcast_to([P, nt, P]),
                                            B_SC[d][:, 0:wq].rearrange("p (t n) -> p t n", n=P)).then_inc(s.sig("cp"), 1)
                    dve.wait_ge(*s.at("cp", 2 * h + 2))
                    dve.tensor_tensor(AT[:, h, 0:wq], TFB[0][:, 0:wq], TFB[1][:, 0:wq], ALU.add).then_inc(s.sig("at"), 1)

                def normalise(h):
                    y = SQH[:, h, 0:wq]
                    dve.wait_ge(*s.at("std", h + 1))
                    link(dve.tensor_tensor(y, PAIR[(11 + h // 2) % 2][h % 2][:, 0:wq], y, ALU.mult))
                    dve.wait_ge(*s.at("rt", 4))
                    dve.scalar_tensor_tensor(y, y, COLS[:, p.l, 1, h:h + 1], RT[:, h, 0:wq],
                                             op0=ALU.mult, op1=ALU.mult).then_inc(s.sig("yh"), 1)

                def low(h):
                    dve.wait_ge(*s.at("xh", 4 + h + 1))
                    dve.tensor_tensor(XL[:, 4 + h, 0:wq], SQH[:, h, 0:wq], XH[:, 4 + h, 0:wq].bitcast(F32),
                                      ALU.subtract).then_inc(s.sig("xl"), 1)

                dve.wait_ge(mask_ready, 1)
                dve.wait_ge(*s.at("pooled", 4))
                masked(0)
                step(8)
                if p.out_sides:
                    side_low(side[0])
                masked(1)
                for t in range(4):
                    dve.wait_ge(*s.at("xh", t + 1))
                    flat = UP[:, t, :, :].rearrange("p s n -> p (s n)")[:, 0:wq]
                    dve.tensor_tensor(XL[:, t, 0:wq], flat, XH[:, t, 0:wq].bitcast(F32),
                                      ALU.subtract).then_inc(s.sig("xl"), 1)
                masked(2)
                normalise(0)
                masked(3)
                for h in range(1, 4):
                    normalise(h)
                    low(h - 1)
                low(3)
                gates_ready(p)
                for b in range(4):
                    k = p.n + IN_BLOCKS + b
                    if p.out_sides and b:
                        side_low(side[0] + b)
                    split_lo(k + 1, (k + 1) % 2)
                    dve.wait_ge(*p.ln.at("half", b + 1))
                    residual(p, 2 * b, PAIR[b % 2][0])
                    dve.wait_ge(block_done, k + 1)
                    residual(p, 2 * b + 1, PAIR[b % 2][1])
                    if p.out_sides and b % 2:
                        fold(turn(side[0] + b) + F0)
                layernorm(p.ln)

            for p in phases:
                (mixer if p.f == "mix" else ffn)(p)

        @block.gpsimd
        def _(pool):
            def layernorm(ln):
                acc, w = ln_acc[ln.scratch], ln.w
                for a in acc:
                    pool.memset(a[:, :], 0.0).then_inc(ln.sig("added"), 1)
                with pool.Fori(0, 3) as i:
                    for b in range(2):
                        pool.wait_ge(*ln.at("z", 2 * i + b + 5))
                        pool.wait_ge(*ln.at("added", 2 * i + b + 2))
                        pool.tensor_tensor(acc[0][:, 0:w], acc[0][:, 0:w],
                                           H[:, ds(2 * i + b, 1), 0:w].rearrange("p a n -> p (a n)"), ALU.add)
                        pool.wait_ge(*ln.at("sq", 2 * i + b + 1))
                        pool.tensor_tensor(acc[1][:, 0:w], acc[1][:, 0:w], ln_sq[ln.scratch][b][:, 0:w],
                                           ALU.add).then_inc(ln.sig("added"), 1)
                pool.wait_ge(*ln.at("mu", 1))
                for q in range(1, 4):
                    z = H[:, 2 * q:2 * q + 2, 0:w]
                    pool.tensor_tensor(z, z, MU[:, 0:w].unsqueeze(1).broadcast_to([P, 2, w]),
                                       ALU.subtract).then_inc(ln.sig("zc"), 1)
                pool.wait_ge(*ln.at("std", 1))
                pool.wait_ge(*ln.at("zc", 3))
                pool.tensor_tensor(z, z, RS[:, 0:w].unsqueeze(1).broadcast_to([P, 2, w]),
                                   ALU.mult).then_inc(ln.sig("zlast"), 1)
                if ln.last:
                    return
                for q, (first, m) in enumerate(PIECES):
                    pool.wait_ge(*ln.at("mfull", q + 1))
                    pool.wait_ge(*ln.at("mlow", q + 1))
                    for t in range(first, first + m):
                        for s in range(w // LAT):
                            c = slice(s * LAT, s * LAT + LAT)
                            ins = pool.tensor_scalar(H[:, t, c], H[:, t, c], CHA[:, t, s:s + 1],
                                                     CHB[:, t, s:s + 1], ALU.mult, ALU.add)
                ins.then_inc(ln.sig("h"), 1)

            links = [0]

            def link(ins):
                links[0] += 1
                ins.then_inc(pool_chain, 1)
                pool.wait_ge(pool_chain, links[0])

            def window_means(p, t):
                s, ns = p.s, p.nt * P // LAT
                if t:
                    pool.wait_ge(*s.at("pooled", t))
                window = WINDOWS[t]
                src, dst, v = UP[:, t, 0:ns, :], PB, 1
                while v < window:
                    lo, hi = PAD - window // 2, PAD + LAT + window // 2 - 2 * v
                    link(pool.tensor_tensor(dst[:, 0:ns, lo:hi], src[:, :, lo:hi], src[:, :, lo + v:hi + v], ALU.add))
                    src, dst, v = dst[:, 0:ns, :], PC if dst is PB else PB, 2 * v
                lo = PAD - window // 2
                mean = dst[:, 0:ns, PAD:PAD + LAT]
                link(pool.tensor_tensor(mean, src[:, :, lo:lo + LAT],
                                       CINV[:, t, :].unsqueeze(1).broadcast_to([P, ns, LAT]), ALU.mult))
                u = UP[:, t, 0:ns, PAD:PAD + LAT]
                pool.tensor_tensor(u, mean, u, ALU.subtract).then_inc(s.sig("pooled"), 1)

            layernorm(lns[0])
            for p in phases:
                if p.f == "mix":
                    pool.wait_ge(*p.s.at("aux_in", 48))
                    pool.wait_ge(*p.s.at("pads", 1))
                    pool.wait_ge(*p.s.at("up", 1))
                    window_means(p, 0)
                    pool.wait_ge(*p.s.at("u12", 1))
                    window_means(p, 1)
                    window_means(p, 2)
                    pool.wait_ge(*p.s.at("up", 2))
                    window_means(p, 3)
                    pool.wait_ge(*p.s.at("o", 4))
                else:
                    pool.wait_ge(block_done, p.n + FT)
                layernorm(p.ln)

        @block.tensor
        def _(pe):
            def three(out, wh, wl, xh, xl, start, stop):
                pe.matmul(out, wh, xh, start=start, stop=False)
                pe.matmul(out, wh, xl, start=False, stop=False)
                return pe.matmul(out, wl, xh, start=False, stop=stop)

            def columns(f):
                pe.wait_ge(rows_out, f + 1)
                if not (isinstance(f, int) and f == 0):
                    pe.wait_ge(mods_done, f)
                ins = pe.matmul(B_COLS[:, 0:4], ROWS[:, :], FOLD[:, :], start=True, stop=True)
                ins.then_inc(cols_ready, 1)

            def side(g, half):
                pe.wait_ge(side_lo, 2 * g + half + 2)
                if half == 0:
                    pe.wait_ge(rows_out, F0 + g)
                for x, part in enumerate((SWH, SWL)):
                    for j in range(KT // 2):
                        r = 4 * (half * KT // 2 + j)
                        ins = pe.matmul(B_ROWS[:, 0:2 * P], S4[:, r:r + P], part[:, j * 2 * P:(j + 1) * 2 * P],
                                        start=(half == 0 and x == 0 and j == 0),
                                        stop=(half == 1 and x == 1 and j == KT // 2 - 1))
                ins.then_inc(side_done, 1)

            def stats_begin(ln):
                acc, w = ln_acc[ln.scratch], ln.w
                pe.wait_ge(*ln.at("added", 8))
                pe.matmul(B_SC[0][:, 0:w], ONES[:, :], acc[0][:, 0:w], start=True, stop=False)
                pe.matmul(B_SC[1][:, 0:w], ONES[:, :], acc[1][:, 0:w], start=True, stop=False)

            def stats_end(ln):
                w = ln.w
                for t in (6, 7):
                    pe.wait_ge(*ln.at("z", t + 5))
                    ins = pe.matmul(B_SC[0][:, 0:w], ONES[:, :], H[:, t, 0:w], start=False, stop=t == 7)
                    if t == 7:
                        ins.then_inc(ln.sig("stats"), 1)
                    pe.wait_ge(*ln.at("sq", t + 1))
                    ins = pe.matmul(B_SC[1][:, 0:w], ONES[:, :], ln_sq[ln.scratch][t - 6][:, 0:w],
                                    start=False, stop=t == 7)
                ins.then_inc(ln.sig("stats"), 1)

            pe.wait_ge(sil_ready, 1)
            for b in range(START_BLOCKS):
                pe.wait_ge(start_full[b % START_SLOTS], 16 * (b // START_SLOTS) + 16)
                if b >= 2:
                    pe.wait_ge(rows_out, b - 1)
                for k in range(KT):
                    ins = pe.matmul(BANK[b % 2][0:2, 0:2 * P], CSIL[:, k, :],
                                    START[b % START_SLOTS][:, k * 2 * P:(k + 1) * 2 * P],
                                    start=k == 0, stop=k == KT - 1)
                ins.then_inc(rows_ready, 1)
                if b == 1:
                    pe.wait_ge(consts_in, 10 * 16)
                if b:
                    columns(b - 1)
            stats_begin(lns[0])
            columns(START_BLOCKS - 1)
            pe.wait_ge(s4_ready, 1)
            pe.wait_ge(s4_tail, 1)
            stats_end(lns[0])

            def by_piece(banks, slot, widths, pieces, high, low, between):
                def low_part(q):
                    pe.wait_ge(*low(q))
                    t, m = pieces[q]
                    ends = []
                    for h, w in enumerate(widths):
                        for k in range(t, t + m):
                            c = slice(k * 256 + h * P, k * 256 + (h + 1) * P)
                            ins = pe.matmul(banks[h][:, 0:w], WH[slot][:, c], XL[:, k, 0:w],
                                            start=False, stop=k == KT - 1)
                        ends.append(ins)
                    return ends

                for q, (t, m) in enumerate(pieces):
                    pe.wait_ge(*high(q))
                    for k in range(t, t + m):
                        for h, w in enumerate(widths):
                            c = slice(k * 256 + h * P, k * 256 + (h + 1) * P)
                            pe.matmul(banks[h][:, 0:w], WH[slot][:, c], XH[:, k, 0:w], start=k == 0, stop=False)
                            pe.matmul(banks[h][:, 0:w], WL[slot][:, c], XH[:, k, 0:w], start=False, stop=False)
                    if q:
                        low_part(q - 1)
                between()
                return low_part(len(pieces) - 1)

            def keep_warm(block, bank, count):
                pe.wait_ge(lo_done, block + 1)
                wh = WH[block % 2]
                for _ in range(count):
                    pe.matmul(bank[:, :], wh[:, 0:P], wh[:, 0:TOK], start=True, stop=True)

            def ffn(p):
                w = p.w
                keep_warm(p.n, PAIR[1][1], WARM_LN)
                for first, end, sided in p.loops:
                    def two_blocks(i):
                        for b in range(2):
                            slot = (p.n + b) % 2
                            pe.wait_ge(lo_done, p.n + b + 1 + 2 * i)
                            pe.wait_ge(pair_free[b], turn(p.G + b) + 1 + i)
                            if end == 1 and b == 0:
                                ins = by_piece(PAIR[b], slot, (w, w), PIECES,
                                               lambda q: p.lin.at("xh", q + 1), lambda q: p.lin.at("xl", q + 1),
                                               lambda: None)[1]
                            else:
                                for h in range(2):
                                    for k in range(KT):
                                        if sided and end > 1 and (h, k) == (1, 4):
                                            side(turn(p.a) + i, b)
                                        if sided and end == 1 and (h, k) in ((0, 4), (1, 6)):
                                            side(turn(p.a), h)
                                        c = slice(k * 256 + h * P, k * 256 + (h + 1) * P)
                                        ins = three(PAIR[b][h][:, 0:w], WH[slot][:, c], WL[slot][:, c],
                                                    XH[:, k, 0:w], XL[:, k, 0:w], k == 0, k == KT - 1)
                            ins.then_inc(block_done, 1)
                            if sided and b:
                                columns(turn(p.a) + F0 + i)

                    run_turns(pe, first, end, two_blocks)
                w = p.ln.w

                def four_tiles(i):
                    for b in range(6):
                        slot = (p.n + FT + b) % 2
                        lo, hi = KPARTS[b % 3]
                        pe.wait_ge(lo_done, p.n + FT + b + 1 + 6 * i)
                        if i == 0 and b < 3:
                            for j in range(2):
                                pe.wait_ge(pair_free[j], turn(p.G + hi - 2 + j) + 2)
                        if b % 3 == 0 and i + b > 0:
                            pe.wait_ge(*p.ln.at("z", 4 * i + 2 * (b // 3) + 2))
                        elif b == 0:
                            pe.wait_ge(pair_free[0], turn(p.G + FT - 2) + 2)
                        for h in range(2):
                            for k in range(lo, hi):
                                if h == 1 and k == lo + 4:
                                    if b < p.out_sides:
                                        side(turn(p.a_out + b) + turn(p.out_sides) * i, b % 2)
                                    if i == 1 and b == 5:
                                        stats_begin(p.ln)
                                c = slice((k - lo) * 256 + h * P, (k - lo) * 256 + (h + 1) * P)
                                ins = three(PAIR[b // 3][h][:, 0:w], WH[slot][:, c], WL[slot][:, c],
                                            AH[:, k, 0:w], AL[:, k, 0:w], k == 0, k == FT - 1)
                            if h == 0 and b % 3 == 2:
                                ins.then_inc(p.ln.sig("half"), 1)
                        ins.then_inc(block_done, 1)
                        if b < p.out_sides and b % 2:
                            columns(turn(p.a_out + b) + F0 + turn(p.out_sides) * i)

                four_tiles(0)
                four_tiles(1)
                stats_end(p.ln)

            def mixer(p):
                s = p.s
                wq, nt = p.nt * P, p.nt
                side_at = [p.a]

                def side_half(b, half):
                    if p.sides[b]:
                        side(turn(side_at[0]), half)

                def side_columns(b):
                    if p.sides[b]:
                        columns(turn(side_at[0]) + F0)
                        side_at[0] += 2

                def project(b, widths):
                    slot, row = (p.n + b) % 2, P * len(widths)
                    pe.wait_ge(lo_done, p.n + b + 1)
                    for h, k in [(h, k) for h in range(len(widths)) for k in range(KT)]:
                        w = widths[h]
                        if (h, k) == (0, 4):
                            side_half(b, 0)
                        if (h, k) == (1, 5):
                            side_half(b, 1)
                        if b == IN_BLOCKS - 1 and 4 <= k < 7:
                            if k == 4:
                                pe.wait_ge(*s.at("et_used", 16))
                            for d in range(2):
                                updates(k - 4, d)
                        c = slice(k * row + h * P, k * row + (h + 1) * P)
                        ins = three(PAIR[b % 2][h][:, 0:w], WH[slot][:, c], WL[slot][:, c],
                                    XH[:, k, 0:w], XL[:, k, 0:w], k == 0, k == KT - 1)
                    ins.then_inc(block_done, 1)
                    side_columns(b)

                def project_tokens(b):
                    slot = (p.n + b) % 2
                    pe.wait_ge(lo_done, p.n + b + 1)
                    for t in range(4):
                        x = slice(t * P, (t + 1) * P)
                        for k in range(KT):
                            if (t, k) == (1, 0):
                                side_half(b, 0)
                            if (t, k) == (3, 0):
                                side_half(b, 1)
                            c = slice(k * 256, (k + 1) * 256)
                            ins = three(PAIR[b % 2][t // 2][:, (t % 2) * 256:(t % 2) * 256 + 256],
                                        XH[:, k, x], XL[:, k, x], WH[slot][:, c], WL[slot][:, c],
                                        k == 0, k == KT - 1)
                    ins.then_inc(block_done, 1)
                    side_columns(b)

                def gates(t):
                    pe.wait_ge(*s.at("gd", 1))
                    pe.wait_ge(*s.at("pads", 1))
                    pe.wait_ge(*s.at("aux_in", 48))
                    if t >= 2:
                        pe.wait_ge(*s.at("et_used", t - 1))
                    pe.matmul(B_SC[t % 2][:, :], GD[:, t * P:(t + 1) * P], GU[:, :],
                              start=True, stop=True).then_inc(s.sig("gp"), 1)

                def turn_keys(t):
                    pe.wait_ge(*s.at("et_used", 3 + t))
                    for j in range(2):
                        for c in range(2):
                            x = (2 * t + j) * P
                            ins = pe.transpose(B_SC[t][:, j * 256 + c * P:j * 256 + (c + 1) * P],
                                               KTT[:, c, x:x + P], IDENT[:, :])
                    ins.then_inc(s.sig("knp"), 1)

                def cumulate(j):
                    c, d = j // 2, j % 2
                    if j < 2:
                        pe.wait_ge(*s.at("kn", j + 1))
                    else:
                        pe.wait_ge(*s.at("et", 4 + 2 * (j - 1)))
                    for t in range(4):
                        ins = pe.matmul(B_SC[d][:, t * P:(t + 1) * P], LA[:, t, d * 256 + c * P:d * 256 + (c + 1) * P],
                                        TRI[:, d, :], start=True, stop=True)
                    ins.then_inc(s.sig("bp"), 1)

                def to_chunk_end(t):
                    pe.wait_ge(*s.at("et", 10 + t + (t < 2) * t if t < 2 else 11 + t))
                    for d in range(2):
                        ins = pe.matmul(B_SC[t % 2][:, d * 256:(d + 1) * 256], TRI[:, 2 + d, :],
                                        LA[:, t, d * 256:(d + 1) * 256], start=True, stop=True)
                    ins.then_inc(s.sig("enp"), 1)

                def updates(i, d):
                    t = CHUNK_ORDER[d][i]
                    if i:
                        pe.wait_ge(*s.at("state", 2 * (i - 1) + d + 1))
                    for c in range(2):
                        for o in range(2):
                            x = d * 256 + c * P + o * 64
                            h = 2 * c + o
                            ins = pe.matmul(B_SC[d][o * 64:(o + 1) * 64, c * P:(c + 1) * P],
                                            KE[:, t, x:x + 64], VN[:, t, h * P:(h + 1) * P],
                                            start=True, stop=True)
                    ins.then_inc(s.sig("u"), 1)

                def pooled(t):
                    pe.wait_ge(*s.at("pooled", t + 1))
                    pe.wait_ge(*s.at("rt", 2 if t < 2 else 3))
                    pe.matmul(PAIR[(9 + t // 2) % 2][t % 2][:, 0:wq], PW[:, t, :],
                              UP[:, t, 0:wq // LAT, PAD:PAD + LAT], start=True, stop=True).then_inc(s.sig("pm"), 1)

                def scores(h):
                    c, r = h // 2, slice((h % 2) * 64, (h % 2 + 1) * 64)
                    for d in range(2):
                        if h:
                            pe.wait_ge(*s.at("cp", 2 * (h - 1) + d + 1))
                        for t in range(nt):
                            x = slice(t * P, (t + 1) * P)
                            ins = pe.matmul(B_SC[d][:, x], KF[d][r, c, x], QF[d][r, c, x], start=True, stop=True)
                        ins.then_inc(s.sig("sc"), 1)

                def outputs(h):
                    c, r = h // 2, slice((h % 2) * 64, (h % 2 + 1) * 64)
                    bank = PAIR[(11 + c) % 2][h % 2]
                    pe.wait_ge(*s.at("ym", 2 * c + 2))
                    pe.wait_ge(*s.at("at", h + 1))
                    for t in range(nt):
                        x = slice(t * P, (t + 1) * P)
                        pe.matmul(bank[:, x], VN[:, t, h * P:(h + 1) * P], AT[:, h, x],
                                  start=(t == 0), stop=False, skip_group_check=True)
                    for d in range(2):
                        for i in range(1, N_CH):
                            t = CHUNK_ORDER[d][i]
                            if t < nt:
                                x = slice(t * P, (t + 1) * P)
                                ins = pe.matmul(bank[:, x], SS[d][r, N_CH - 1 + i - 1, c, :], QF[d][r, c, x],
                                                start=False, stop=(d == 1 and i == N_CH - 1),
                                                skip_group_check=True)
                    ins.then_inc(s.sig("o"), 1)

                keep_warm(p.n, PAIR[1][1], WARM_LN)
                pe.wait_ge(lo_done, p.n + 1)
                ins = by_piece(PAIR[0], p.n % 2, (TOK, wq), PIECES,
                               lambda q: p.lin.at("xh", q + 1), lambda q: p.lin.at("xl", q + 1), lambda: None)[1]
                ins.then_inc(block_done, 1)
                project(1, (TOK, TOK))
                gates(0)
                gates(1)
                pe.wait_ge(*s.at("gd", 1))
                pe.wait_ge(*s.at("up", 1))
                project(2, (wq, wq))
                gates(2)
                gates(3)
                pe.wait_ge(*s.at("kv", 1))
                project_tokens(3)
                turn_keys(0)
                turn_keys(1)
                pe.wait_ge(*s.at("kv", 2))
                project_tokens(4)
                cumulate(0)
                cumulate(1)
                pe.wait_ge(*s.at("v_in", 1))
                project(5, (wq, wq))
                cumulate(2)
                cumulate(3)
                pe.wait_ge(*s.at("v_in", 2))
                project(6, (wq, wq))
                to_chunk_end(0)
                to_chunk_end(1)
                pe.wait_ge(*s.at("u12", 1))
                project(7, (wq, wq))
                to_chunk_end(2)
                to_chunk_end(3)
                pe.wait_ge(*s.at("up", 2))
                pe.wait_ge(*s.at("rt", 1))
                project(8, (wq,))
                for t in range(4):
                    pooled(t)
                pe.wait_ge(*s.at("state", 6))
                pe.wait_ge(*s.at("scaled", 6))

                def mean_squares(h):
                    pe.wait_ge(*s.at("osq", h + 1))
                    if h >= 2:
                        pe.wait_ge(*s.at("std", h - 1))
                    pe.matmul(B_MS[h % 2][:, 0:wq], ONES[:, :], SQH[:, h, 0:wq], start=True,
                              stop=True).then_inc(s.sig("ms"), 1)

                scores(0)
                for h in range(4):
                    if h < 3:
                        scores(h + 1)
                    outputs(h)
                    if h:
                        mean_squares(h - 1)
                mean_squares(3)
                keep_warm(p.n + IN_BLOCKS, B_SC[0], WARM_HEADS)
                w = p.ln.w
                for b in range(4):
                    slot = (p.n + IN_BLOCKS + b) % 2
                    pe.wait_ge(lo_done, p.n + IN_BLOCKS + b + 1)
                    pe.wait_ge(*p.ln.at("z", 2 * b + 2))
                    if b == 0:
                        half, ins = by_piece(PAIR[0], slot, (w, w), [(k, 1) for k in range(KT)],
                                             lambda q: s.at("xh", q + 1), lambda q: s.at("xl", q + 1),
                                             lambda: side(turn(side_at[0]), 0) if p.out_sides else None)
                        half.then_inc(p.ln.sig("half"), 1)
                    else:
                        for h in range(2):
                            for k in range(KT):
                                if p.out_sides and (h, k) == (1, 2):
                                    side(turn(side_at[0] + b), b % 2)
                                if (b, h, k) == (3, 1, 4):
                                    stats_begin(p.ln)
                                c = slice(k * 256 + h * P, k * 256 + (h + 1) * P)
                                ins = three(PAIR[b % 2][h][:, 0:w], WH[slot][:, c], WL[slot][:, c],
                                            XH[:, k, 0:w], XL[:, k, 0:w], k == 0, k == KT - 1)
                            if h == 0:
                                ins.then_inc(p.ln.sig("half"), 1)
                    ins.then_inc(block_done, 1)
                    if p.out_sides and b % 2:
                        columns(turn(side_at[0] + b) + F0)
                stats_end(p.ln)

            for p in phases:
                (mixer if p.f == "mix" else ffn)(p)


def kernel(**inputs):
    import numpy as np
    import concourse.bacc as bacc
    from concourse.bass_utils import run_bass_kernel_spmd as run

    v = {k: np.asarray(x) for k, x in inputs.items()}
    f32 = np.float32

    def feature_major(a):
        return np.ascontiguousarray(a.T.reshape(-1, P, a.shape[0]).transpose(1, 0, 2))

    def columns(a):
        return np.ascontiguousarray(a.reshape(-1, KT, P).transpose(2, 0, 1))

    def blocks(w, j, n):
        L, K, _ = w.shape
        return np.ascontiguousarray(w.reshape(L, K // P, P, j, n).transpose(0, 3, 2, 1, 4)
                                    .reshape(L, j, P, K // P * n))

    arrays = {}
    arrays["x"] = feature_major(np.concatenate([v["x"][0], v["ctx"][0]], axis=0))
    arrays["cond"] = feature_major(np.stack([v["c"][0], v["c_ctx"]]))
    w = blocks(v["w_ada"], N_MOD * KT // 2, 2 * P).reshape(FULLS, P, 2, D).transpose(0, 2, 1, 3)
    arrays["w_ada"] = np.ascontiguousarray(w.reshape(HALVES, P, D))
    arrays["b_ada"] = np.ascontiguousarray(v["b_ada"].reshape(2 * FULLS, P).T)
    one, zero = np.ones((1, D), f32), np.zeros((1, D), f32)
    arrays["ln_g"] = columns(np.concatenate([one, v["ln_g"].reshape(-1, D)]))
    arrays["ln_b"] = columns(np.concatenate([zero, v["ln_b"].reshape(-1, D)]))
    for f, name in (("a", "ffa"), ("b", "ffb")):
        w = v[name + "_w_in"].reshape(DEPTH, D, 2, FT, P).transpose(0, 1, 3, 2, 4)
        arrays["ff_in_" + f] = blocks(w.reshape(DEPTH, D, 2 * FF), FT, 256)
        arrays["ff_out_" + f] = blocks(v[name + "_w_out"], 4, 256)
    w = v["mix_w_in"]
    u, q, k, vv, r, gd = (w[..., a:b] for a, b in ((0, 512), (512, 768), (768, 1024), (1024, 1536),
                                                  (1536, 2048), (2048, 2080)))
    order = np.concatenate([gd, r[..., :96], u[..., :P], k, q, vv, u[..., P:], r[..., :3 * P]], axis=-1)
    full = blocks(order, IN_BLOCKS - 1, 256).transpose(0, 2, 1, 3).reshape(DEPTH, P, -1)
    arrays["mix_in"] = np.ascontiguousarray(np.concatenate([full, blocks(r[..., 3 * P:], 1, P)[:, 0]], axis=-1))
    arrays["mix_out"] = blocks(v["mix_w_out"], 4, 256)
    arrays["pool_w"] = np.ascontiguousarray(v["pool_w"].transpose(0, 2, 1, 3))
    gu = np.zeros((DEPTH, 33, TOK), f32)
    gu[:, 0:16, 0:256], gu[:, 16:32, 256:] = v["gate_up_f"], v["gate_up_b"]
    gu[:, 32, 0:256], gu[:, 32, 256:] = v["gate_bias_f"], v["gate_bias_b"]
    arrays["gate_up"] = gu
    cols = np.stack([v["pool_scale"].reshape(DEPTH, 4, P), v["gla_norm_g"].reshape(DEPTH, 4, P)], axis=1)
    arrays["cols"] = np.ascontiguousarray(cols.transpose(3, 0, 1, 2))

    omega = 1.0 / (10000.0 ** (np.arange(256, dtype=f32) / f32(256)))

    def enc(n):
        a = np.arange(n, dtype=f32)[:, None] * omega.astype(f32)
        return feature_major(np.concatenate([np.sin(a), np.cos(a)], axis=-1).astype(f32))

    arrays["pos_r"], arrays["pos_c"] = enc(4), enc(64)
    arrays["ident"] = np.eye(P, dtype=f32)
    fold = np.zeros((36, 4), f32)
    fold[0:4, 0:2] = fold[32:36, 2:4] = np.concatenate([np.eye(2, dtype=f32)] * 2)
    arrays["fold"] = fold
    arrays["ones"] = np.full((P, P), 1.0 / D, f32)
    j, i = np.arange(P)[:, None], np.arange(P)[None, :]
    run_f = (j <= i).astype(f32) - (j < MID).astype(f32)
    run_b = (j >= i).astype(f32) - (j >= MID).astype(f32)
    run_f[:, MID_COL[0]], run_b[:, MID_COL[1]] = j[:, 0] < MID, j[:, 0] >= MID
    tri = np.stack([run_f, run_b, (j > i).astype(f32), (j < i).astype(f32)], axis=1)
    arrays["tri"] = np.ascontiguousarray(tri / f32(16.0))
    t = np.arange(LAT)
    count = np.stack([np.minimum(t + w - 1 - w // 2, LAT - 1) - np.maximum(t - w // 2, 0) + 1 for w in WINDOWS])
    arrays["cinv"] = np.ascontiguousarray(np.broadcast_to(f32(1.0) / count.astype(f32), (P, 4, LAT)))

    nc = bacc.Bacc("TRN2", target_bir_lowering=False, num_devices=1)
    io = {n: nc.dram_tensor("in_" + n, a.shape, mybir.dt.from_np(a.dtype), kind="ExternalInput").ap()
          for n, a in arrays.items()}
    io["out"] = nc.dram_tensor("out", (P, KT, LAT), F32, kind="ExternalOutput").ap()
    build(nc, io)
    got = run(nc, [{"in_" + n: a for n, a in arrays.items()}], core_ids=[0])
    out = np.asarray(got.results[0]["out"])
    return np.ascontiguousarray(out.transpose(2, 1, 0).reshape(1, LAT, D))
```
